# Optimizing a Trainium2 kernel written in Bass

```python
import math
import jax, jax.numpy as jnp
from jax import lax
import numpy as np
import jax
import jax.numpy as jnp

D_MODEL = 1024
BATCH = 1
SEQ = 256
DEPTH = 1

NORM_EPS = 1e-6
N_BRANCHES = 4
BRANCH_WIDTH = 512
D_FF = 4 * D_MODEL
Q_BLOCK = 128

DN_HEADS = 4
DN_HEAD_DIM = 128
DN_CONV = 4
DN_CHUNK = 64

MLA_HEADS = 4
MLA_Q_RANK = 256
MLA_KV_RANK = 128
MLA_NOPE = 128
MLA_ROPE = 64
MLA_V = 128
MLA_QK_DIM = MLA_NOPE + MLA_ROPE
ROPE_THETA = 10000.0

SG_GROUPS = 4
SG_GROUP_DIM = 128
SG_CHUNK = 128

FOX_HEADS = 4
FOX_HEAD_DIM = 128

IN_SPLITS = (
    3 * DN_HEADS * DN_HEAD_DIM,
    DN_HEADS * DN_HEAD_DIM,
    DN_HEADS,
    DN_HEADS,
    MLA_Q_RANK,
    MLA_KV_RANK,
    MLA_ROPE,
    SG_GROUPS * SG_GROUP_DIM,
    SG_GROUPS * SG_GROUP_DIM,
    3 * FOX_HEADS * FOX_HEAD_DIM,
    FOX_HEADS,
    N_BRANCHES * D_MODEL,
)
D_IN = sum(IN_SPLITS)


def rms_norm(x, g, eps=NORM_EPS):
    xf = x.astype(jnp.float32)
    y = xf * lax.rsqrt(jnp.mean(xf * xf, axis=-1, keepdims=True) + eps)
    return (y * g.astype(jnp.float32)).astype(x.dtype)

def l2_norm(x, eps=NORM_EPS):
    return x * lax.rsqrt(jnp.sum(x * x, axis=-1, keepdims=True) + eps)

def causal_depthwise_conv(x, w):
    K = w.shape[0]
    S = x.shape[1]
    xp = jnp.pad(x, ((0, 0), (K - 1, 0), (0, 0)))
    out = xp[:, 0:S, :] * w[0]
    for k in range(1, K):
        out = out + xp[:, k:k + S, :] * w[k]
    return out

def rope_tables(positions):
    inv_freq = ROPE_THETA ** (-jnp.arange(0, MLA_ROPE, 2, dtype=jnp.float32) / MLA_ROPE)
    ang = positions.astype(jnp.float32)[..., None] * inv_freq
    return jnp.cos(ang)[:, :, None, :], jnp.sin(ang)[:, :, None, :]

def apply_rope(x, cos, sin):
    xf = x.astype(jnp.float32)
    x1, x2 = jnp.split(xf, 2, axis=-1)
    return jnp.concatenate([x1 * cos - x2 * sin, x2 * cos + x1 * sin], axis=-1).astype(x.dtype)

def block_causal_attention(q, k, v, log_decay=None):
    B, H, S, dk = q.shape
    nb = S // Q_BLOCK
    scale = dk ** -0.5
    k_pos = jnp.arange(S)

    def to_blocks(a):
        return jnp.moveaxis(a.reshape(B, H, nb, Q_BLOCK, *a.shape[3:]), 2, 0)

    xs = {"idx": jnp.arange(nb), "q": to_blocks(q)}
    if log_decay is not None:
        xs["d"] = to_blocks(log_decay)

    def attend(blk):
        q_pos = blk["idx"] * Q_BLOCK + jnp.arange(Q_BLOCK)
        s = jnp.einsum("bhqd,bhkd->bhqk", blk["q"], k).astype(jnp.float32) * scale
        if log_decay is not None:
            s = s + (blk["d"][..., :, None] - log_decay[..., None, :])
        s = jnp.where(k_pos[None, :] <= q_pos[:, None], s, -jnp.inf)
        p = jax.nn.softmax(s, axis=-1).astype(v.dtype)
        return jnp.einsum("bhqk,bhkd->bhqd", p, v)

    out = lax.map(attend, xs)
    return jnp.moveaxis(out, 0, 2).reshape(B, H, S, v.shape[-1])

def gated_deltanet(qkv, z, a_logit, b_logit, conv_w, a_log, dt_bias, out_g):
    B, S, _ = qkv.shape
    H, dk, C = DN_HEADS, DN_HEAD_DIM, DN_CHUNK
    N = S // C
    qkv = jax.nn.silu(causal_depthwise_conv(qkv, conv_w)).astype(jnp.float32)
    q, k, v = jnp.split(qkv, 3, axis=-1)

    def heads(t):
        return t.reshape(B, S, H, dk).transpose(0, 2, 1, 3)

    q = l2_norm(heads(q)) * dk ** -0.5
    k = l2_norm(heads(k))
    v = heads(v)
    beta = jax.nn.sigmoid(b_logit.astype(jnp.float32)).transpose(0, 2, 1)
    g = (-jnp.exp(a_log.astype(jnp.float32))
         * jax.nn.softplus(a_logit.astype(jnp.float32) + dt_bias.astype(jnp.float32))).transpose(0, 2, 1)

    def chunk(t):
        return t.reshape(B, H, N, C, *t.shape[3:])

    q, k, v, beta, g = chunk(q), chunk(k), chunk(v), chunk(beta), chunk(g)
    gc = jnp.cumsum(g, axis=-1)
    tril = jnp.tril(jnp.ones((C, C), dtype=bool))
    strict = jnp.tril(jnp.ones((C, C), dtype=bool), -1)
    diff = gc[..., :, None] - gc[..., None, :]
    decay = jnp.where(tril, jnp.exp(jnp.where(tril, diff, 0.0)), 0.0)

    kb = k * beta[..., None]
    lower = jnp.where(strict, jnp.einsum("bhnid,bhnjd->bhnij", kb, k) * decay, 0.0)
    rhs = jnp.concatenate([v * beta[..., None], kb * jnp.exp(gc)[..., None]], axis=-1)
    sol = lax.linalg.triangular_solve(lower + jnp.eye(C, dtype=jnp.float32), rhs,
                                      left_side=True, lower=True, unit_diagonal=True)
    u, w = jnp.split(sol, 2, axis=-1)

    a_qk = jnp.einsum("bhnid,bhnjd->bhnij", q, k) * decay
    q_dec = q * jnp.exp(gc)[..., None]
    k_dec = k * jnp.exp(gc[..., -1:] - gc)[..., None]
    g_last = jnp.exp(gc[..., -1])

    def step(state, xs):
        q_i, k_i, u_i, w_i, a_i, gl_i = xs
        v_new = u_i - jnp.einsum("bhcd,bhde->bhce", w_i, state)
        o_i = jnp.einsum("bhcd,bhde->bhce", q_i, state) + jnp.einsum("bhij,bhje->bhie", a_i, v_new)
        state = state * gl_i[..., None, None] + jnp.einsum("bhcd,bhce->bhde", k_i, v_new)
        return state, o_i

    xs = tuple(jnp.moveaxis(t, 2, 0) for t in (q_dec, k_dec, u, w, a_qk, g_last))
    _, o = lax.scan(step, jnp.zeros((B, H, dk, dk), jnp.float32), xs)
    o = jnp.moveaxis(o, 0, 2).reshape(B, H, S, dk)
    o = rms_norm(o, out_g).transpose(0, 2, 1, 3).reshape(B, S, H * dk)
    return (o * jax.nn.silu(z.astype(jnp.float32))).astype(z.dtype)

def latent_attention(c_q, c_kv, k_rope, positions, q_norm_g, kv_norm_g, w_uq, w_ukv, qk_q_g, qk_k_g):
    B, S, _ = c_q.shape
    H = MLA_HEADS
    q = (rms_norm(c_q, q_norm_g) @ w_uq).reshape(B, S, H, MLA_QK_DIM)
    kv = (rms_norm(c_kv, kv_norm_g) @ w_ukv).reshape(B, S, H, MLA_NOPE + MLA_V)
    k_nope, v = jnp.split(kv, [MLA_NOPE], axis=-1)
    k = jnp.concatenate([k_nope, jnp.broadcast_to(k_rope[:, :, None, :], (B, S, H, MLA_ROPE))], axis=-1)
    q = rms_norm(q, qk_q_g)
    k = rms_norm(k, qk_k_g)
    cos, sin = rope_tables(positions)
    q = jnp.concatenate([q[..., :MLA_NOPE], apply_rope(q[..., MLA_NOPE:], cos, sin)], axis=-1)
    k = jnp.concatenate([k[..., :MLA_NOPE], apply_rope(k[..., MLA_NOPE:], cos, sin)], axis=-1)
    o = block_causal_attention(q.transpose(0, 2, 1, 3), k.transpose(0, 2, 1, 3), v.transpose(0, 2, 1, 3))
    return o.transpose(0, 2, 1, 3).reshape(B, S, H * MLA_V)

def spatial_gating(u, v, norm_g, w_s, b_s):
    B, S, _ = u.shape
    G, Cg, T = SG_GROUPS, SG_GROUP_DIM, SG_CHUNK
    N = S // T
    u = jax.nn.gelu(u)
    v = rms_norm(jax.nn.gelu(v).reshape(B, S, G, Cg), norm_g).reshape(B, N, T, G, Cg)
    w_causal = jnp.where(jnp.tril(jnp.ones((T, T), dtype=bool)), w_s, 0.0)
    mixed = jnp.einsum("gts,bnsgc->bntgc", w_causal, v) + b_s.T[None, None, :, :, None]
    return u * mixed.reshape(B, S, G * Cg)

def forgetting_attention(qkv, f_logit, f_bias, q_g, k_g):
    B, S, _ = qkv.shape
    H, dh = FOX_HEADS, FOX_HEAD_DIM
    q, k, v = jnp.split(qkv, 3, axis=-1)

    def heads(t):
        return t.reshape(B, S, H, dh).transpose(0, 2, 1, 3)

    q = rms_norm(heads(q), q_g)
    k = rms_norm(heads(k), k_g)
    log_f = jax.nn.log_sigmoid(f_logit.astype(jnp.float32) + f_bias.astype(jnp.float32))
    cum = jnp.cumsum(log_f, axis=1).transpose(0, 2, 1)
    o = block_causal_attention(q, k, heads(v), cum)
    return o.transpose(0, 2, 1, 3).reshape(B, S, H * dh)

def first_inputs(seed: int = 0) -> dict:
    key = jax.random.key(seed)
    ks = jax.random.split(key, 26)
    L = DEPTH
    f32 = jnp.float32

    def nrm(k, shape, fan_in):
        return jax.random.normal(k, shape, f32) * fan_in ** -0.5

    def gain(k, shape):
        return 1.0 + 0.1 * jax.random.normal(k, shape, f32)

    dt = jnp.exp(jax.random.uniform(ks[4], (L, DN_HEADS), f32, math.log(1e-3), math.log(1e-1)))
    return {
        "x": jax.random.normal(ks[0], (BATCH, SEQ, D_MODEL), f32),
        "positions": jnp.broadcast_to(jnp.arange(SEQ, dtype=jnp.int32)[None, :], (BATCH, SEQ)),
        "norm1_g": gain(ks[1], (L, D_MODEL)),
        "w_in": nrm(ks[2], (L, D_MODEL, D_IN), D_MODEL),
        "dn_conv_w": nrm(ks[3], (L, DN_CONV, 3 * DN_HEADS * DN_HEAD_DIM), DN_CONV),
        "dn_a_log": jnp.log(jax.random.uniform(ks[5], (L, DN_HEADS), f32, 1.0, 16.0)),
        "dn_dt_bias": dt + jnp.log(-jnp.expm1(-dt)),
        "dn_out_norm_g": gain(ks[6], (L, DN_HEAD_DIM)),
        "mla_q_norm_g": gain(ks[7], (L, MLA_Q_RANK)),
        "mla_kv_norm_g": gain(ks[8], (L, MLA_KV_RANK)),
        "mla_w_uq": nrm(ks[9], (L, MLA_Q_RANK, MLA_HEADS * MLA_QK_DIM), MLA_Q_RANK),
        "mla_w_ukv": nrm(ks[10], (L, MLA_KV_RANK, MLA_HEADS * (MLA_NOPE + MLA_V)), MLA_KV_RANK),
        "mla_qk_q_g": gain(ks[11], (L, MLA_QK_DIM)),
        "mla_qk_k_g": gain(ks[12], (L, MLA_QK_DIM)),
        "sg_v_norm_g": gain(ks[13], (L, SG_GROUPS, SG_GROUP_DIM)),
        "sg_w_s": nrm(ks[14], (L, SG_GROUPS, SG_CHUNK, SG_CHUNK), SG_CHUNK),
        "sg_b_s": gain(ks[15], (L, SG_GROUPS, SG_CHUNK)),
        "fox_q_norm_g": gain(ks[16], (L, FOX_HEAD_DIM)),
        "fox_k_norm_g": gain(ks[17], (L, FOX_HEAD_DIM)),
        "fox_f_bias": 4.0 + jax.random.normal(ks[18], (L, FOX_HEADS), f32),
        "w_branch": nrm(ks[19], (L, N_BRANCHES, BRANCH_WIDTH, D_MODEL), BRANCH_WIDTH),
        "w_out": nrm(ks[20], (L, D_MODEL, D_MODEL), D_MODEL),
        "norm2_g": gain(ks[21], (L, D_MODEL)),
        "w_ff1": nrm(ks[22], (L, D_MODEL, D_FF), D_MODEL),
        "w_ff2": nrm(ks[23], (L, D_FF, D_MODEL), D_FF),
    }

def first_block(x, positions, norm1_g, w_in, dn_conv_w, dn_a_log, dn_dt_bias, dn_out_norm_g,
              mla_q_norm_g, mla_kv_norm_g, mla_w_uq, mla_w_ukv, mla_qk_q_g, mla_qk_k_g,
              sg_v_norm_g, sg_w_s, sg_b_s, fox_q_norm_g, fox_k_norm_g, fox_f_bias,
              w_branch, w_out, norm2_g, w_ff1, w_ff2):
    B, S, _ = x.shape
    split_points = np.cumsum(IN_SPLITS)[:-1]
    for l in range(DEPTH):
        h = rms_norm(x, norm1_g[l])
        proj = h @ w_in[l]
        (dn_qkv, dn_z, dn_a, dn_b, mla_cq, mla_ckv, mla_kr,
         sg_u, sg_v, fox_qkv, fox_f, gate_logits) = jnp.split(proj, split_points, axis=-1)

        o_a = gated_deltanet(dn_qkv, dn_z, dn_a, dn_b, dn_conv_w[l], dn_a_log[l],
                             dn_dt_bias[l], dn_out_norm_g[l])
        o_b = latent_attention(mla_cq, mla_ckv, mla_kr, positions, mla_q_norm_g[l], mla_kv_norm_g[l],
                               mla_w_uq[l], mla_w_ukv[l], mla_qk_q_g[l], mla_qk_k_g[l])
        o_c = spatial_gating(sg_u, sg_v, sg_v_norm_g[l], sg_w_s[l], sg_b_s[l])
        o_d = forgetting_attention(fox_qkv, fox_f, fox_f_bias[l], fox_q_norm_g[l], fox_k_norm_g[l])

        branches = jnp.stack([o_a.astype(x.dtype), o_b.astype(x.dtype),
                              o_c.astype(x.dtype), o_d.astype(x.dtype)], axis=2)
        projected = jnp.einsum("bsiw,iwd->bsid", branches, w_branch[l])
        gates = jax.nn.sigmoid(gate_logits.reshape(B, S, N_BRANCHES, D_MODEL))
        merged = jnp.sum(gates * projected, axis=2)
        x = x + merged @ w_out[l]

        h2 = rms_norm(x, norm2_g[l])
        x = x + jnp.square(jax.nn.relu(h2 @ w_ff1[l])) @ w_ff2[l]
    return x


DEPTH_2 = 2

PLE_DIM = 256
N_EVEN = (DEPTH_2 + 1) // 2
N_ODD = DEPTH_2 // 2
SSD_HEADS = 16
SSD_HEAD_DIM = 64
SSD_INNER = SSD_HEADS * SSD_HEAD_DIM
SSD_GROUPS = 2
SSD_HPG = SSD_HEADS // SSD_GROUPS
SSD_STATE = 128
SSD_CONV = 4
SSD_CHUNK = 128
SSD_XBC = SSD_INNER + 2 * SSD_GROUPS * SSD_STATE
SC_DIM = 1024
SC_CONV = 3
MIX_IN = SSD_INNER + SSD_XBC + SSD_HEADS + 3 * SC_DIM
MIX_OUT = SSD_INNER + SC_DIM
ATTN_HEADS = 16
ATTN_KV_HEADS = 4
ATTN_GROUP = ATTN_HEADS // ATTN_KV_HEADS
ATTN_HEAD_DIM = 64
WINDOW = 128
ATTN_BLOCK = 128
QKV_DIM = (ATTN_HEADS + 2 * ATTN_KV_HEADS) * ATTN_HEAD_DIM
D_FF_2 = ((8 * D_MODEL + 3 * 256 - 1) // (3 * 256)) * 256
ALPHA = (2 * DEPTH_2) ** 0.25
BETA = (8 * DEPTH_2) ** -0.25
LN_EPS = 1e-5
RMS_EPS = 1e-5


def layer_norm(x, g, b):
    xf = x.astype(jnp.float32)
    mu = jnp.mean(xf, axis=-1, keepdims=True)
    xc = xf - mu
    var = jnp.mean(xc * xc, axis=-1, keepdims=True)
    return (xc * lax.rsqrt(var + LN_EPS) * g.astype(jnp.float32) + b.astype(jnp.float32)).astype(x.dtype)

def causal_dwconv(x, w):
    k, c = w.shape
    return lax.conv_general_dilated(
        x, w[:, None, :].astype(x.dtype), window_strides=(1,), padding=[(k - 1, 0)],
        dimension_numbers=('NWC', 'WIO', 'NWC'), feature_group_count=c)

def ssd_mixer(z, xbc, dt_raw, conv_w, conv_b, dt_bias, a_log, d_skip, norm_w):
    f32 = jnp.float32
    bsz, seqlen, _ = z.shape
    nc = seqlen // SSD_CHUNK
    xbc = jax.nn.silu(causal_dwconv(xbc, conv_w) + conv_b.astype(xbc.dtype)).astype(f32)
    xs = xbc[..., :SSD_INNER].reshape(bsz, nc, SSD_CHUNK, SSD_GROUPS, SSD_HPG, SSD_HEAD_DIM)
    bm = xbc[..., SSD_INNER:SSD_INNER + SSD_GROUPS * SSD_STATE].reshape(bsz, nc, SSD_CHUNK, SSD_GROUPS, SSD_STATE)
    cm = xbc[..., SSD_INNER + SSD_GROUPS * SSD_STATE:].reshape(bsz, nc, SSD_CHUNK, SSD_GROUPS, SSD_STATE)
    dt = jax.nn.softplus(dt_raw.astype(f32) + dt_bias.astype(f32))
    a = -jnp.exp(a_log.astype(f32))
    dt = dt.reshape(bsz, nc, SSD_CHUNK, SSD_GROUPS, SSD_HPG)
    da = dt * a.reshape(SSD_GROUPS, SSD_HPG)
    xdt = xs * dt[..., None]
    a_cs = jnp.cumsum(da, axis=2)
    seg = a_cs[:, :, :, None] - a_cs[:, :, None, :]
    causal = jnp.tril(jnp.ones((SSD_CHUNK, SSD_CHUNK), dtype=bool))[:, :, None, None]
    decay_ls = jnp.exp(jnp.where(causal, seg, -jnp.inf))
    cb = jnp.einsum('bclgn,bcsgn->bclsg', cm, bm)
    y_diag = jnp.einsum('bclsgr,bcsgrp->bclgrp', cb[..., None] * decay_ls, xdt)
    decay_to_end = jnp.exp(a_cs[:, :, -1:] - a_cs)
    chunk_states = jnp.einsum('bclgn,bclgrp->bcgrpn', bm, xdt * decay_to_end[..., None])
    chunk_decay = jnp.exp(a_cs[:, :, -1])

    def step(h, inp):
        s_c, d_c = inp
        return h * d_c[..., None, None] + s_c, h

    h0 = jnp.zeros((bsz, SSD_GROUPS, SSD_HPG, SSD_HEAD_DIM, SSD_STATE), f32)
    _, h_in = lax.scan(step, h0, (jnp.moveaxis(chunk_states, 1, 0), jnp.moveaxis(chunk_decay, 1, 0)))
    h_in = jnp.moveaxis(h_in, 0, 1)
    y_off = jnp.einsum('bclgn,bcgrpn->bclgrp', cm, h_in) * jnp.exp(a_cs)[..., None]
    y = y_diag + y_off + xs * d_skip.astype(f32).reshape(SSD_GROUPS, SSD_HPG)[:, :, None]
    y = y.reshape(bsz, seqlen, SSD_INNER) * jax.nn.silu(z.astype(f32))
    yg = y.reshape(bsz, seqlen, SSD_GROUPS, SSD_INNER // SSD_GROUPS)
    yg = yg * lax.rsqrt(jnp.mean(yg * yg, axis=-1, keepdims=True) + RMS_EPS)
    return (yg.reshape(bsz, seqlen, SSD_INNER) * norm_w.astype(f32)).astype(z.dtype)

def ssd_shortconv_layer_mixer(x, w_in, conv_w, conv_b, dt_bias, a_log, d_skip, norm_w, sc_conv_w, w_out):
    proj = x @ w_in
    o1 = SSD_INNER
    o2 = o1 + SSD_XBC
    o3 = o2 + SSD_HEADS
    o4 = o3 + SC_DIM
    o5 = o4 + SC_DIM
    z, xbc, dt_raw = proj[..., :o1], proj[..., o1:o2], proj[..., o2:o3]
    sc_b, sc_c, sc_h = proj[..., o3:o4], proj[..., o4:o5], proj[..., o5:]
    y_ssd = ssd_mixer(z, xbc, dt_raw, conv_w, conv_b, dt_bias, a_log, d_skip, norm_w)
    y_sc = sc_b * causal_dwconv(sc_c * sc_h, sc_conv_w)
    return jnp.concatenate([y_ssd.astype(x.dtype), y_sc.astype(x.dtype)], axis=-1) @ w_out

def sliding_window_attention(x, w_qkv, b_qkv, sinks, w_o, b_o):
    bsz, seqlen, _ = x.shape
    nb = seqlen // ATTN_BLOCK
    qkv = x @ w_qkv + b_qkv
    nq = ATTN_HEADS * ATTN_HEAD_DIM
    nkv = ATTN_KV_HEADS * ATTN_HEAD_DIM
    q = qkv[..., :nq].reshape(bsz, nb, ATTN_BLOCK, ATTN_KV_HEADS, ATTN_GROUP, ATTN_HEAD_DIM)
    k = qkv[..., nq:nq + nkv].reshape(bsz, nb, ATTN_BLOCK, ATTN_KV_HEADS, ATTN_HEAD_DIM)
    v = qkv[..., nq + nkv:].reshape(bsz, nb, ATTN_BLOCK, ATTN_KV_HEADS, ATTN_HEAD_DIM)

    def with_prev(t):
        prev = jnp.concatenate([jnp.zeros_like(t[:, :1]), t[:, :-1]], axis=1)
        return jnp.concatenate([prev, t], axis=2)

    kk = with_prev(k)
    vv = with_prev(v)
    scale = ATTN_HEAD_DIM ** -0.5
    s = jnp.einsum('bnqkgd,bnskd->bnkgqs', q, kk, preferred_element_type=jnp.float32) * scale
    n_idx = jnp.arange(nb)[:, None, None]
    q_pos = n_idx * ATTN_BLOCK + jnp.arange(ATTN_BLOCK)[None, :, None]
    k_pos = (n_idx - 1) * ATTN_BLOCK + jnp.arange(2 * ATTN_BLOCK)[None, None, :]
    rel = q_pos - k_pos
    band = (rel >= 0) & (rel < WINDOW) & (k_pos >= 0)
    s = jnp.where(band[None, :, None, None], s, -jnp.inf)
    sink = sinks.astype(jnp.float32).reshape(ATTN_KV_HEADS, ATTN_GROUP)[None, None, :, :, None, None]
    sink = jnp.broadcast_to(sink, s.shape[:-1] + (1,))
    probs = jax.nn.softmax(jnp.concatenate([s, sink], axis=-1), axis=-1)[..., :-1]
    o = jnp.einsum('bnkgqs,bnskd->bnqkgd', probs.astype(vv.dtype), vv)
    return o.reshape(bsz, seqlen, nq) @ w_o + b_o

def swiglu(x, w_gate, w_up, w_down):
    return (jax.nn.silu(x @ w_gate) * (x @ w_up)) @ w_down

def second_inputs(seed: int = 0) -> dict:
    key = jax.random.key(seed)
    ks = jax.random.split(key, 32)
    f32 = jnp.float32

    def nrm(k, shape, scale):
        return jax.random.normal(k, shape, f32) * scale

    x = nrm(ks[0], (BATCH, SEQ, D_MODEL), 1.0)
    p = nrm(ks[1], (DEPTH_2, BATCH, SEQ, PLE_DIM), 1.0)
    w_in_mix = nrm(ks[2], (N_EVEN, D_MODEL, MIX_IN), D_MODEL ** -0.5)
    ssd_conv_w = nrm(ks[3], (N_EVEN, SSD_CONV, SSD_XBC), SSD_CONV ** -0.5)
    ssd_conv_b = nrm(ks[4], (N_EVEN, SSD_XBC), 0.02)
    dt0 = jnp.exp(jax.random.uniform(ks[5], (N_EVEN, SSD_HEADS), f32, math.log(1e-3), math.log(1e-1)))
    ssd_dt_bias = dt0 + jnp.log(-jnp.expm1(-dt0))
    ssd_a_log = jnp.log(jax.random.uniform(ks[6], (N_EVEN, SSD_HEADS), f32, 1.0, 16.0))
    ssd_d = 1.0 + nrm(ks[7], (N_EVEN, SSD_HEADS), 0.1)
    ssd_norm_w = 1.0 + nrm(ks[8], (N_EVEN, SSD_INNER), 0.02)
    sc_conv_w = nrm(ks[9], (N_EVEN, SC_CONV, SC_DIM), SC_CONV ** -0.5)
    w_out_mix = nrm(ks[10], (N_EVEN, MIX_OUT, D_MODEL), BETA * MIX_OUT ** -0.5)
    w_qkv = nrm(ks[11], (N_ODD, D_MODEL, QKV_DIM), D_MODEL ** -0.5)
    b_qkv = nrm(ks[12], (N_ODD, QKV_DIM), 0.02)
    attn_sinks = nrm(ks[13], (N_ODD, ATTN_HEADS), 0.5)
    w_o = nrm(ks[14], (N_ODD, ATTN_HEADS * ATTN_HEAD_DIM, D_MODEL), BETA * (ATTN_HEADS * ATTN_HEAD_DIM) ** -0.5)
    b_o = nrm(ks[15], (N_ODD, D_MODEL), 0.02)
    ln_mix_g = 1.0 + nrm(ks[16], (DEPTH_2, D_MODEL), 0.02)
    ln_mix_b = nrm(ks[17], (DEPTH_2, D_MODEL), 0.02)
    w_ffn_gate = nrm(ks[18], (DEPTH_2, D_MODEL, D_FF_2), D_MODEL ** -0.5)
    w_ffn_up = nrm(ks[19], (DEPTH_2, D_MODEL, D_FF_2), D_MODEL ** -0.5)
    w_ffn_down = nrm(ks[20], (DEPTH_2, D_FF_2, D_MODEL), BETA * D_FF_2 ** -0.5)
    ln_ffn_g = 1.0 + nrm(ks[21], (DEPTH_2, D_MODEL), 0.02)
    ln_ffn_b = nrm(ks[22], (DEPTH_2, D_MODEL), 0.02)
    w_ple = nrm(ks[23], (DEPTH_2, PLE_DIM, D_MODEL), PLE_DIM ** -0.5)
    w_ple_gate = nrm(ks[24], (DEPTH_2, D_MODEL, D_MODEL), D_MODEL ** -0.5)
    b_ple_gate = nrm(ks[25], (DEPTH_2, D_MODEL), 0.02)
    return {'x': x, 'p': p, 'w_in_mix': w_in_mix, 'ssd_conv_w': ssd_conv_w, 'ssd_conv_b': ssd_conv_b,
            'ssd_dt_bias': ssd_dt_bias, 'ssd_a_log': ssd_a_log, 'ssd_d': ssd_d, 'ssd_norm_w': ssd_norm_w,
            'sc_conv_w': sc_conv_w, 'w_out_mix': w_out_mix, 'w_qkv': w_qkv, 'b_qkv': b_qkv,
            'attn_sinks': attn_sinks, 'w_o': w_o, 'b_o': b_o, 'ln_mix_g': ln_mix_g, 'ln_mix_b': ln_mix_b,
            'w_ffn_gate': w_ffn_gate, 'w_ffn_up': w_ffn_up, 'w_ffn_down': w_ffn_down,
            'ln_ffn_g': ln_ffn_g, 'ln_ffn_b': ln_ffn_b, 'w_ple': w_ple, 'w_ple_gate': w_ple_gate,
            'b_ple_gate': b_ple_gate}

def second_block(x, p, w_in_mix, ssd_conv_w, ssd_conv_b, ssd_dt_bias, ssd_a_log, ssd_d, ssd_norm_w,
              sc_conv_w, w_out_mix, w_qkv, b_qkv, attn_sinks, w_o, b_o, ln_mix_g, ln_mix_b,
              w_ffn_gate, w_ffn_up, w_ffn_down, ln_ffn_g, ln_ffn_b, w_ple, w_ple_gate, b_ple_gate):
    for i in range(DEPTH_2):
        j = i // 2
        if i % 2 == 0:
            mix = ssd_shortconv_layer_mixer(x, w_in_mix[j], ssd_conv_w[j], ssd_conv_b[j], ssd_dt_bias[j],
                                            ssd_a_log[j], ssd_d[j], ssd_norm_w[j], sc_conv_w[j], w_out_mix[j])
        else:
            mix = sliding_window_attention(x, w_qkv[j], b_qkv[j], attn_sinks[j], w_o[j], b_o[j])
        x = layer_norm(ALPHA * x + mix.astype(x.dtype), ln_mix_g[i], ln_mix_b[i])
        x = layer_norm(ALPHA * x + swiglu(x, w_ffn_gate[i], w_ffn_up[i], w_ffn_down[i]), ln_ffn_g[i], ln_ffn_b[i])
        gate = jax.nn.sigmoid(x @ w_ple_gate[i] + b_ple_gate[i])
        x = x + (p[i] @ w_ple[i]) * gate
    return x


def setup_inputs(seed=0):
    out = dict(first_inputs(seed))
    for name, value in second_inputs(seed + 1).items():
        if name != "x":
            out[name + "_2"] = value
    return out


def reference(
    x, positions, norm1_g, w_in, dn_conv_w, dn_a_log, dn_dt_bias, dn_out_norm_g, mla_q_norm_g,
    mla_kv_norm_g, mla_w_uq, mla_w_ukv, mla_qk_q_g, mla_qk_k_g, sg_v_norm_g, sg_w_s, sg_b_s,
    fox_q_norm_g, fox_k_norm_g, fox_f_bias, w_branch, w_out, norm2_g, w_ff1, w_ff2, p_2,
    w_in_mix_2, ssd_conv_w_2, ssd_conv_b_2, ssd_dt_bias_2, ssd_a_log_2, ssd_d_2, ssd_norm_w_2,
    sc_conv_w_2, w_out_mix_2, w_qkv_2, b_qkv_2, attn_sinks_2, w_o_2, b_o_2, ln_mix_g_2,
    ln_mix_b_2, w_ffn_gate_2, w_ffn_up_2, w_ffn_down_2, ln_ffn_g_2, ln_ffn_b_2, w_ple_2,
    w_ple_gate_2, b_ple_gate_2,
):
    x = first_block(
        x, positions, norm1_g, w_in, dn_conv_w, dn_a_log, dn_dt_bias, dn_out_norm_g,
        mla_q_norm_g, mla_kv_norm_g, mla_w_uq, mla_w_ukv, mla_qk_q_g, mla_qk_k_g, sg_v_norm_g,
        sg_w_s, sg_b_s, fox_q_norm_g, fox_k_norm_g, fox_f_bias, w_branch, w_out, norm2_g, w_ff1,
        w_ff2,
    )
    return second_block(
        x, p_2, w_in_mix_2, ssd_conv_w_2, ssd_conv_b_2, ssd_dt_bias_2, ssd_a_log_2, ssd_d_2,
        ssd_norm_w_2, sc_conv_w_2, w_out_mix_2, w_qkv_2, b_qkv_2, attn_sinks_2, w_o_2, b_o_2,
        ln_mix_g_2, ln_mix_b_2, w_ffn_gate_2, w_ffn_up_2, w_ffn_down_2, ln_ffn_g_2, ln_ffn_b_2,
        w_ple_2, w_ple_gate_2, b_ple_gate_2,
    )


_drawn_inputs = setup_inputs


def setup_inputs(seed=0):
    import zlib

    import numpy as np

    out = dict(_drawn_inputs(seed))
    spreads = {}
    factors = {'mla_q_norm_g': 5.233,
     'mla_kv_norm_g': 3.37,
     'mla_qk_q_g': 5.053,
     'mla_qk_k_g': 5.242,
     'fox_q_norm_g': 4.035,
     'fox_k_norm_g': 4.323,
     'ssd_conv_b_2': 8.0,
     'ssd_d_2': 47.886,
     'ssd_norm_w_2': 200.0,
     'b_qkv_2': 8.0,
     'attn_sinks_2': 8.0,
     'b_o_2': 5.099,
     'b_ple_gate_2': 8.0,
     'dn_a_log': 32.6,
     'sg_v_norm_g': 3.476,
     'dn_dt_bias': 8.0,
     'dn_out_norm_g': 3.189}
    for name, (base, spread) in spreads.items():
        noise = np.random.default_rng([zlib.crc32(name.encode()), seed]).standard_normal(out[name].shape)
        drawn = base * np.exp(spread * noise) if base else spread * noise
        out[name] = jnp.asarray(drawn.astype(out[name].dtype))
    for name, factor in factors.items():
        out[name] = (out[name] * factor).astype(out[name].dtype)
    return out
```

```python
from contextlib import ExitStack

import numpy as np

import concourse.bass as bass
from concourse import mybir

F32 = mybir.dt.float32
F32R = mybir.dt.float32r
I32 = mybir.dt.int32
ACT = mybir.ActivationFunctionType
ALU = mybir.AluOpType
AX_X = mybir.AxisListType.X

P = 128
TOK = 256
NT = TOK // P
D = 1024
KD = D // P
BANK = 512
NEG = -1.0e30

DN_H = 4
DH = 128
W = 512
MLA_QR, MLA_KVR, NOPE, ROPE = 256, 128, 128, 64
QK = NOPE + ROPE
DFF = 4096
IN_SIZES = (3 * W, W, DN_H, DN_H, MLA_QR, MLA_KVR, ROPE, W, W, 3 * W, DN_H, 4 * D)
(O_DN, O_Z, O_A, O_B, O_CQ, O_CKV, O_KR, O_SU, O_SV, O_FOX, O_FF, O_GATE) = (
    [sum(IN_SIZES[:i]) for i in range(len(IN_SIZES))])
ABC = O_SU - O_A
SSD_H, SSD_D, SSD_N, SSD_G = 16, 64, 128, 2
XBC = SSD_H * SSD_D + 2 * SSD_G * SSD_N
DFF2 = ((8 * D + 3 * 256 - 1) // (3 * 256)) * 256
KF2 = DFF2 // P
PLE = 256
AH, AKV, AD = 16, 4, 64
M_XBC, M_DT, M_B = D, D + XBC, D + XBC + SSD_H
M_C, M_H = M_B + D, M_B + 2 * D
ALPHA = 4 ** 0.25

UK = 2
RAW = 5
SPLIT = 4
AHEAD = SPLIT - 1


def gemm_plan():
    g = []
    for j, n in enumerate(("dq", "dk", "dv")):
        g.append((n, "w_in", KD, O_DN + j * W, W, "F"))
    g.append(("z", "w_in", KD, O_Z, W, "T"))
    g.append(("abc", "w_in", KD, O_A, ABC, "T"))
    g.append(("ff", "w_in", KD, O_FF, DN_H, "T"))
    for j, n in enumerate(("fq", "fk", "fv")):
        g.append((n, "w_in", KD, O_FOX + j * W, W, "T"))
    g.append(("sv", "w_in", KD, O_SV, W, "T"))
    g.append(("su", "w_in", KD, O_SU, W, "F"))
    for j in range(2):
        g.append((f"uq{j}", "mla_w_uq", 2, j * 2 * QK, 2 * QK, "T"))
    for j in range(2):
        g.append((f"ukv{j}", "mla_w_ukv", 1, j * W, W, "T"))
    for c in range(2):
        for i in range(4):
            g.append((f"gate{i}_{c}", "w_in", KD, O_GATE + i * D + c * W, W, "T"))
            g.append((f"br{i}_{c}", f"w_branch{i}", 4, c * W, W, "T"))
    for c in range(2):
        g.append((f"wo{c}", "w_out", KD, c * W, W, "T"))
    for c in range(DFF // W):
        g.append((f"f1_{c}", "w_ff1", KD, c * W, W, "F"))
    for c in range(2):
        g.append((f"f2_{c}", "w_ff2", DFF // P, c * W, W, "T"))
    for c in range(3):
        g.append((f"xbc{c}", "w_in_mix", KD, M_XBC + c * W, W, "F"))
    g.append(("dt", "w_in_mix", KD, M_DT, SSD_H, "T"))
    for c in range(2):
        g.append((f"mz{c}", "w_in_mix", KD, c * W, W, "T"))
    for c in range(2):
        for n, o in (("sc", M_C), ("sh", M_H), ("sb", M_B)):
            g.append((f"{n}{c}", "w_in_mix", KD, o + c * W, W, "F"))
    for c in range(2):
        g.append((f"mo{c}", "w_out_mix", 2 * KD, c * W, W, "T"))
    for i in range(2):
        if i == 1:
            for c in range(2):
                g.append((f"aq{c}", "w_qkv", KD, c * W, W, "F"))
            g.append(("ak", "w_qkv", KD, D, AKV * AD, "F"))
            g.append(("av", "w_qkv", KD, D + AKV * AD, AKV * AD, "T"))
            for c in range(2):
                g.append((f"ao{c}", "w_o", KD, c * W, W, "T"))
        for c in range(-(-DFF2 // W)):
            w = min(W, DFF2 - c * W)
            g.append((f"fg{i}_{c}", f"w_gate{i}", KD, c * W, w, "F"))
            g.append((f"fu{i}_{c}", f"w_up{i}", KD, c * W, w, "F"))
        for c in range(2):
            g.append((f"fd{i}_{c}", f"w_down{i}", KF2, c * W, W, "T"))
        for c in range(2):
            g.append((f"pg{i}_{c}", f"w_pgate{i}", KD, c * W, W, "T"))
            g.append((f"pw{i}_{c}", f"w_ple{i}", 2, c * W, W, "T"))
    chunks, units = {}, []
    for n, (name, w, kt, c0, width, mode) in enumerate(g):
        first = len(units)
        for k in range(0, kt, UK):
            units.append((w, k, min(UK, kt - k), c0, width))
        chunks[name] = (n, first, len(units), kt, width, mode)
    return chunks, units


TURNS = (("x1", KD), ("oa", 4), ("cqkv", 3), ("merged", KD), ("x2", KD), ("x3", KD), ("p0", 2), ("y", KD),
         ("x4", KD), ("x5", KD), ("x6", KD), ("p1", 2), ("x7", KD), ("x8", KD))


def turn_plan():
    plan, at = {}, 0
    for name, nf in TURNS:
        n = -(-nf // 2)
        plan[name] = (at, n, nf)
        at += n
    return plan


CONST = {}


def const_table():
    i = np.arange(P)
    same = (i[:, None] // 64) == (i[None, :] // 64)
    parts = {
        "ident": np.eye(P),
        "tri64": (i[:, None] <= i[None, :]) & same, "strict64": (i[:, None] < i[None, :]) & same,
        "blk64": same, "tri": i[:, None] <= i[None, :], "ones": np.ones((P, P)),
        "strict": i[:, None] < i[None, :],
        "causal0": np.where(i[None, :] <= i[:, None], 0.0, NEG),
        "open": np.zeros((P, P)),
        "causal1": np.where(i[None, :] <= i[:, None], 0.0, NEG),
        "prev": np.where(i[None, :] > i[:, None], 0.0, NEG),
        "causal2": np.where(i[None, :] <= i[:, None], 0.0, NEG),
    }
    for s in range(6):
        h = 1 << s
        parts[f"lvl{s}"] = ((i[:, None] // (2 * h) == i[None, :] // (2 * h))
                            & ((i[:, None] // h) % 2 == 0) & ((i[None, :] // h) % 2 == 1))
    parts["freq"] = np.broadcast_to(
        (np.float32(10000.0) ** (-np.arange(0, ROPE, 2, dtype=np.float32) / ROPE))[None], (P, ROPE // 2))
    parts["eps6"] = np.full((P, 1), 1e-6)
    parts["eps5"] = np.full((P, 1), 1e-5)
    at, cols = 0, []
    for n, a in parts.items():
        CONST[n] = (at, a.shape[1])
        at += a.shape[1]
        cols.append(np.asarray(a, np.float32))
    return np.ascontiguousarray(np.concatenate(cols, axis=1))


CONST_ARRAY = const_table()

ROWS_A = (("norm1_g", 8), ("mla_q_norm_g", 2), ("mla_kv_norm_g", 1), ("fox_q_norm_g", 1), ("fox_k_norm_g", 1),
          ("dn_conv_w", 48), ("norm2_g", 8))
ROWS_B = (("ssd_conv_w", 48), ("ssd_conv_b", 12), ("sc_conv_w", 24), ("ssd_norm_w", 8), ("b_qk", 10))
HEADS = (("dn_dt_bias", 4), ("dn_a_log", 4), ("fox_f_bias", 4), ("ssd_dt_bias", 16), ("ssd_a_log", 16),
         ("ssd_d", 16), ("attn_sinks", 16))


def starts(table):
    out, at = {}, 0
    for n, k in table:
        out[n] = at
        at += k
    return out, at


def build(nc, a, out):
    chunks, units = gemm_plan()
    turns = turn_plan()
    rows_a, n_a = starts(ROWS_A)
    rows_b, n_b = starts(ROWS_B)
    head_at, n_heads = starts(HEADS)
    C = CONST

    ctx = ExitStack()
    with ctx:
        def sb(name, shape, dt=F32, where=None):
            return (where or ctx).enter_context(nc.sbuf_tensor(name, shape, dt))

        def sem(name):
            return ctx.enter_context(nc.semaphore(name))

        raw = sb("raw", [P, RAW, UK, BANK])
        whi = sb("whi", [P, SPLIT, UK, BANK], F32R)
        wlo = sb("wlo", [P, SPLIT, UK, BANK], F32R)
        X = sb("X", [P, NT, D])
        XThi = sb("XThi", [P, KD, TOK], F32R)
        XTlo = sb("XTlo", [P, KD, TOK], F32R)
        ct = sb("ct", [P, CONST_ARRAY.shape[1]])
        rowsA = sb("rowsA", [P, P])
        rowsB = sb("rowsB", [P, P])
        colA = sb("colA", [P, n_a])
        colB = sb("colB", [P, n_b])
        heads = sb("heads", [P, n_heads])
        ss = sb("ss", [P, 16])
        rs = sb("rs", [P, 16])
        logit = sb("logit", [P, NT, 16])
        sp_y = sb("sp_y", [P, NT, 16])
        sp_z = sb("sp_z", [P, NT, 16])
        sp_z2 = sb("sp_z2", [P, NT, 16])
        sp_p = sb("sp_p", [P, NT, 16])
        sp = sb("sp", [P, NT, 16])

        def con(name):
            at, n = C[name]
            return ct[:, at:at + n]

        ident = con("ident")
        ones = con("ones")
        eps6, eps5 = con("eps6"), con("eps5")

        def span(first, last):
            return ct[:, C[first][0]:C[last][0] + C[last][1]]

        def headv(name):
            at = head_at[name]
            return heads[:, at:at + dict(HEADS)[name]]

        def acol(name, j=0):
            return colA[:, rows_a[name] + j:rows_a[name] + j + 1]

        def bcol(name, j=0):
            return colB[:, rows_b[name] + j:rows_b[name] + j + 1]

        attn_neg = sb("attn_neg", [P, 4, 2])
        attn_sum = sb("attn_sum", [P, 4, 2])
        attn_inv = sb("attn_inv", [P, 4, 2])

        m1 = ExitStack()
        BRhi = sb("BRhi", [P, 16, TOK], F32R, m1)
        BRlo = sb("BRlo", [P, 16, TOK], F32R, m1)
        zs = sb("zs", [P, NT, W], where=m1)
        abc = sb("abc", [P, NT, ABC], where=m1)
        ffl = sb("ffl", [P, NT, 4], where=m1)
        fx = sb("fx", [P, NT, 3 * W], where=m1)
        sgv = sb("sgv", [P, NT, W], where=m1)
        sgu = sb("sgu", [P, 4, TOK], where=m1)
        beta = sb("beta", [P, NT, 4], where=m1)
        dng = sb("dng", [P, NT, 4], where=m1)
        nlf = sb("nlf", [P, NT, 4], where=m1)
        ea = sb("ea", [P, 4], where=m1)
        gcs = sb("gcs", [P, 4, 4], where=m1)
        gex = sb("gex", [P, 3, NT, 4], where=m1)
        o_g = sb("o_g", [P, P], where=m1)
        m1a = ExitStack()
        dn = sb("dn", [P, 14, 1024], where=m1a)
        m1a.close()
        m1b = ExitStack()
        mq = sb("mq", [P, 2, NT, 4, QK], where=m1b)
        mv = sb("mv", [P, NT, W], where=m1b)
        msq = sb("msq", [P, NT * 4 * QK], where=m1b)
        mT = sb("mT", [P, 8, TOK], where=m1b)
        mR = sb("mR", [ROPE, 8, TOK], where=m1b)
        m_g = sb("m_g", [P, 2, QK], where=m1b)
        cs = sb("cs", [P, 2, NT, ROPE // 2], where=m1b)
        ang = sb("ang", [P, 3, NT, ROPE // 2], where=m1b)
        posi = sb("posi", [P, NT], I32, m1b)
        posf = sb("posf", [P, NT], where=m1b)
        rt = sb("rt", [P, 4, NT, 4, ROPE // 2], where=m1b)
        cn = sb("cn", [P, NT, 3 * P], where=m1b)
        MQhi = sb("MQhi", [P, 3, TOK], F32R, m1b)
        MQlo = sb("MQlo", [P, 3, TOK], F32R, m1b)
        m1b.close()
        m1c = ExitStack()
        fsq = sb("fsq", [P, NT, D], where=m1c)
        fT = sb("fT", [P, 8, TOK], where=m1c)
        fD = sb("fD", [P, 4, 3 * P], where=m1c)
        fS = sb("fS", [P, 4, 3 * P], where=m1c)
        fPT = sb("fPT", [P, 4, 3 * P], where=m1c)
        ncs = sb("ncs", [P, NT, 4], where=m1c)
        m1c.close()
        m1d = ExitStack()
        sgq = sb("sgq", [P, NT, W], where=m1d)
        sw = sb("sw", [P, 4, P], where=m1d)
        swT = sb("swT", [P, 4, P], where=m1d)
        s_ng = sb("s_ng", [P, W], where=m1d)
        s_b = sb("s_b", [P, W], where=m1d)
        sm = sb("sm", [P, 4, TOK], where=m1d)
        m1d.close()
        m1e = ExitStack()
        gt = sb("gt", [P, 2, NT, W], where=m1e)
        gp = sb("gp", [P, NT, W], where=m1e)
        merged = sb("merged", [P, NT, D], where=m1e)
        m1e.close()
        m1.close()
        m2 = ExitStack()
        FFhi = sb("FFhi", [P, DFF // P, TOK], F32R, m2)
        FFlo = sb("FFlo", [P, DFF // P, TOK], F32R, m2)
        XN = sb("XN", [P, NT, D], where=m2)
        f1r = sb("f1r", [P, 4, TOK], where=m2)
        f1s = sb("f1s", [P, 4, TOK], where=m2)
        m2.close()
        PThi = sb("PThi", [P, 2, TOK], F32R)
        PTlo = sb("PTlo", [P, 2, TOK], F32R)
        dtv = sb("dtv", [P, NT, SSD_H])
        da = sb("da", [P, NT, SSD_H])
        ea2 = sb("ea2", [P, SSD_H])
        acs = sb("acs", [P, 3, SSD_H])
        eac = sb("eac", [P, 2, SSD_H])
        nsink = sb("nsink", [P, AH])
        esink = sb("esink", [P, 4, 2])
        m3a = ExitStack()
        conv2 = sb("conv2", [P, 12, TOK + 3], where=m3a)
        xdt = sb("xdt", [P, NT, D], where=m3a)
        m3a.close()
        lnr = sb("lnr", [P, 5, D])
        sb("spare", [P, 64])
        m3 = ExitStack()
        BYhi = sb("BYhi", [P, 16, TOK], F32R, m3)
        BYlo = sb("BYlo", [P, 16, TOK], F32R, m3)
        zz = sb("zz", [P, NT, D], where=m3)
        xs = sb("xs", [P, NT, D], where=m3)
        yd = sb("yd", [P, NT, D], where=m3)
        pin = sb("pin", [P, NT, PLE], where=m3)
        bmt = sb("bmt", [P, 2 * P], where=m3)
        cbm = sb("cbm", [P, 4, P], where=m3)
        em = sb("em", [P, 8, P], where=m3)
        xe = sb("xe", [P, D], where=m3)
        hst = sb("hst", [P, D], where=m3)
        m3b = ExitStack()
        xbcT = sb("xbcT", [P, 12, TOK], where=m3b)
        m3b.close()
        m3c = ExitStack()
        scc = sb("scc", [P, 4, TOK], where=m3c)
        scp = sb("scp", [P, 4, TOK + 2], where=m3c)
        scv = sb("scv", [P, 4, TOK], where=m3c)
        m3c.close()
        m3.close()
        m4 = ExitStack()
        Hhi = sb("Hhi", [P, KF2, TOK], F32R, m4)
        Hlo = sb("Hlo", [P, KF2, TOK], F32R, m4)
        sg = sb("sg", [P, 4, TOK], where=m4)
        fh = sb("fh", [P, 4, TOK], where=m4)
        xc = sb("xc", [P, NT, D], where=m4)
        junk = sb("junk", [P, NT, D], where=m4)
        pgt = sb("pgt", [P, NT, W], where=m4)
        pin1 = sb("pin1", [P, NT, PLE], where=m4)
        m4.close()
        m5 = ExitStack()
        AThi = sb("AThi", [P, KD, TOK], F32R, m5)
        ATlo = sb("ATlo", [P, KD, TOK], F32R, m5)
        aqT = sb("aqT", [P, KD, TOK], where=m5)
        akr = sb("akr", [P, 2, TOK], where=m5)
        akd = sb("akd", [P, AKV, TOK], where=m5)
        av = sb("av", [P, NT, AKV * AD], where=m5)
        bv = sb("bv", [P, AKV * AD], where=m5)
        bo = sb("bo", [P, D], where=m5)
        wS = sb("wS", [P, 4, 3 * P], where=m5)
        wPT = sb("wPT", [P, 4, 3 * P], where=m5)
        m5.close()

        conv_in = dn[:, 0:4, :].rearrange("p a b -> p (a b)")[:, 0:12 * (TOK + 3)].rearrange(
            "p (f t) -> p f t", f=12)
        qkv = dn[:, 4:7, :].rearrange("p a (f t) -> p (a f) t", t=TOK)
        XN1 = dn[:, 7:9, :]
        d_sq = dn[:, 7:9, :].rearrange("p a b -> p (a b)")
        d_rn = dn[:, 0:2, :].rearrange("p a b -> p (a b)")
        qT, kT = dn[:, 4, :], dn[:, 5, :]
        qT4, kT4, vT4 = (dn[:, 4 + i, :].rearrange("p (h t) -> p h t", h=4) for i in range(3))
        d_v = dn[:, 6, :]
        d_e, d_lt, d_at, d_egr, d_br = dn[:, 2, :], dn[:, 1, :], dn[:, 3, :], dn[:, 9, :], dn[:, 0, :]
        d_kbe, d_kdec, d_vb = dn[:, 7, :], dn[:, 8, :], dn[:, 0, :]
        d_x, d_y, d_t1, d_ml = dn[:, 10, :], dn[:, 11, :], dn[:, 12, :], dn[:, 13, :]
        d_u, d_w, d_vn, d_s, d_o, d_osq = (
            dn[:, 13, :], dn[:, 12, :], dn[:, 1, :], dn[:, 10, 0:W], dn[:, 5, :], dn[:, 2, :])

        acc = ctx.enter_context(nc.psum_tensor("acc", [P, 2, NT, BANK], F32))
        pm = ctx.enter_context(nc.psum_tensor("pm", [P, 4, BANK], F32))

        names = """x_in c_in w_hi w_lo w_used evac0 evac1 t_pe t_hi t_lo rstd xn cols
            conv_in conv silu dn_sq dn_l2 dn_rn dn_qkn sp_in sp_e dn_g dn_gc dn_gcs dn_gex dn_rows dn_e0 dn_egr dn_e
            dn_kk dn_lt dn_kv dn_vb dn_ml dn_t1 dn_t1c dn_pq dn_y dn_uw dn_uws sc_ws sc_vn sc_su sc_s dn_osq
            dn_oss dn_orn dn_o m_cn m_cn2 m_in m_sqs m_ss m_rn m_ang m_cs m_rope m_tn m_tnc m_tr m_trc
            a_sc a_s a_e a_p a_pt a_ptc a_o a_hi a_lo f_sq f_ss f_rn f_xn f_t f_tc f_cum f_d
            s_sq s_ss s_rn s_v s_w s_wt s_mx s_m s_hi s_lo g_sig g_done f1_r f1_s f1_hi f1_lo
            c2_in conv2 silu2 p_in dt_in dt_e dt_g s_cb s_xs s_xsc s_xd s_bt s_btc s_ac s_acc s_eac s_xe s_st
            s_stc s_yo s_yod b_row b_e0 b_e b_m b_y b_yd y_z y_ss y_n c_cv c_out c_hi c_lo c_ready ln_in ln_sum ln_xc
            ln_rs ln_x h_x h_hi h_lo g_x g_s x_end q_in k_d w_es act_seq dve_seq fin out_done""".split()
        S = {n: sem(n) for n in names}
        s_raw = [sem(f"s_raw{i}") for i in range(RAW)]
        evac = (S["evac0"], S["evac1"])

        def evac_at(name):
            n = chunks[name][0]
            return evac[n % 2], n // 2 + 1

        def landed(name):
            return chunks[name][2]

        def accT(name):
            n, _, _, _, w, _ = chunks[name]
            return acc[:, n % 2, :, 0:w]

        def accF(name):
            n, _, _, _, w, _ = chunks[name]
            return acc[:, n % 2].rearrange("p b (f t) -> p (b f) t", t=TOK)[:, 0:w // P, :]


        block = ctx.enter_context(nc.Block())

        @block.sync
        def _(sp_):
            sp_.dma_start(X[:], a["x"].rearrange("(t p) d -> p t d", p=P)).then_inc(S["x_in"], 16)
            sp_.dma_start(ct[:], a["consts"]).then_inc(S["x_in"], 16)
            for u, (w, k, nk, c0, width) in enumerate(units):
                if u >= RAW:
                    sp_.wait_ge(S["w_lo"], u - RAW + 1)
                src = a[w][k * P:(k + nk) * P, c0:c0 + width].rearrange("(k p) n -> p k n", p=P)
                sp_.dma_start(raw[:, u % RAW, 0:nk, 0:width], src).then_inc(s_raw[u % RAW], 16)
            sp_.wait_ge(S["fin"], 1)
            sp_.dma_start(out.rearrange("(t p) d -> p t d", p=P), X[:]).then_inc(S["out_done"], 16)
            sp_.wait_ge(S["out_done"], 16)

        @block.gpsimd
        def _(pool):
            for u, (w, k, nk, c0, width) in enumerate(units):
                pool.wait_ge(S["w_hi"], u + 1)
                nc.gpsimd.tensor_tensor(wlo[:, u % SPLIT, 0:nk, 0:width], raw[:, u % RAW, 0:nk, 0:width],
                                        whi[:, u % SPLIT, 0:nk, 0:width].bitcast(F32),
                                        ALU.subtract).then_inc(S["w_lo"], 1)

        @block.scalar
        def _(act):
            seq = [0]

            def link(ins):
                seq[0] += 1
                ins.then_inc(S["act_seq"], 1)
                act.wait_ge(S["act_seq"], seq[0])

            def fn(out_, in_, func, **k):
                return nc.scalar.activation(out_, in_, func, **k)

            split = [0]

            def high_halves(until):
                while split[0] < min(until, len(units)):
                    u = split[0]
                    w, k, nk, c0, width = units[u]
                    act.wait_ge(s_raw[u % RAW], 16 * (u // RAW + 1))
                    if u >= SPLIT:
                        act.wait_ge(S["w_used"], u - SPLIT + 1)
                    fn(whi[:, u % SPLIT, 0:nk, 0:width], raw[:, u % RAW, 0:nk, 0:width],
                       ACT.Copy).then_inc(S["w_hi"], 1)
                    split[0] += 1

            def ready(name):
                high_halves(landed(name) + AHEAD)
                act.wait_ge(S["w_used"], landed(name))

            def leave(name, out_, func=ACT.Copy):
                ready(name)
                view = accF(name) if chunks[name][5] == "F" else accT(name)
                fn(out_, view, func).then_inc(evac_at(name)[0], 1)

            def turn(name, hi, gain=None):
                g0, n, nf = turns[name]
                for g in range(n):
                    k = min(2, nf - 2 * g)
                    act.wait_ge(S["t_pe"], g0 + g + 1)
                    bank = pm[:, (g0 + g) % 4, 0:k * TOK].rearrange("p (f t) -> p f t", t=TOK)
                    if gain is None:
                        fn(hi[:, 2 * g:2 * g + k, :], bank, ACT.Copy).then_inc(S["t_hi"], 1)
                    else:
                        for f in range(k):
                            last = fn(hi[:, 2 * g + f, :], bank[:, f, :], ACT.Copy, scale=gain(2 * g + f))
                        last.then_inc(S["t_hi"], 1)

            def rstd(out_, in_, n, eps, k=1):
                link(fn(out_, in_, ACT.Ln, scale=1.0 / n, bias=eps))
                return fn(out_, out_, ACT.Exp, scale=-0.5)

            at = 0
            for name, k in ROWS_A:
                act.dma_start(rowsA[at:at + k, :], a[name]).then_inc(S["c_in"], 16)
                at += k
            at = 0
            for name, k in ROWS_B:
                act.dma_start(rowsB[at:at + k, :], a[name]).then_inc(S["c_in"], 16)
                at += k
            for name, k in HEADS:
                act.dma_start(headv(name), a[name].partition_broadcast(P)).then_inc(S["c_in"], 16)
            act.dma_start(o_g[:], a["dn_out_norm_g"].partition_broadcast(P)).then_inc(S["c_in"], 16)

            act.wait_ge(S["x_in"], 32)
            for t in range(NT):
                last = fn(XN1[:, t, :], X[:, t, :], ACT.Square, accum_out=ss[:, t:t + 1])
            link(last)
            rstd(rs[:, 0:NT], ss[:, 0:NT], D, eps6).then_inc(S["rstd"], 1)
            high_halves(AHEAD)
            act.wait_ge(S["cols"], 1)
            fn(colA[:], pm[:, 0, 0:n_a], ACT.Copy)
            link(fn(colB[:], pm[:, 0, P:P + n_b], ACT.Copy))
            fn(ea[:], headv("dn_a_log"), ACT.Exp).then_inc(S["cols"], 1)
            turn("x1", XThi, lambda f: acol("norm1_g", f))

            act.wait_ge(S["conv_in"], 1)
            for j, name in enumerate(("dq", "dk", "dv")):
                leave(name, conv_in[:, 4 * j:4 * j + 4, 3:3 + TOK])

            def silu(j):
                act.wait_ge(S["conv"], j + 1)
                return fn(qkv[:, 4 * j:4 * j + 4, :], qkv[:, 4 * j:4 * j + 4, :], ACT.Silu)
            silu(0)
            silu(1)
            leave("z", zs[:], ACT.Silu)
            link(silu(2))
            fn(d_sq, qkv[:, 0:8, :].rearrange("p f t -> p (f t)"), ACT.Square).then_inc(S["dn_sq"], 1)
            leave("abc", abc[:])
            leave("ff", ffl[:])
            for j, name in enumerate(("fq", "fk", "fv")):
                leave(name, fx[:, :, j * W:(j + 1) * W])
            leave("sv", sgv[:], ACT.Gelu_apprx_tanh)
            leave("su", sgu[:], ACT.Gelu_apprx_tanh)

            act.wait_ge(S["dn_l2"], 1)
            link(fn(d_rn, pm[:].rearrange("p a b -> p (a b)"), ACT.Ln, bias=eps6))
            fn(d_rn, d_rn, ACT.Exp, scale=-0.5).then_inc(S["dn_rn"], 1)
            act.wait_ge(S["sp_in"], 1)
            fn(sp_y[:, :, 0:8], sp_y[:, :, 0:8], ACT.Exp, scale=-1.0)
            fn(beta[:], abc[:, :, 4:8], ACT.Exp, scale=-1.0).then_inc(S["sp_e"], 1)
            act.wait_ge(S["dn_gcs"], 1)
            fn(gex[:, 0:2, :, :], gcs[:].rearrange("p (k t) h -> p k t h", k=2), ACT.Exp).then_inc(S["dn_gex"], 1)
            act.wait_ge(S["dn_rows"], 1)
            act.wait_ge(S["dn_qkn"], 1)
            fn(d_br, pm[:, 2:4, :].rearrange("p a b -> p (a b)"), ACT.Copy)
            act.wait_ge(S["dn_e0"], 1)
            fn(d_e, d_e, ACT.Exp).then_inc(S["dn_e"], 1)
            fn(d_egr, pm[:, 0:2, :].rearrange("p a b -> p (a b)"), ACT.Exp).then_inc(S["dn_egr"], 1)
            for s in range(6):
                for hf in range(2):
                    act.wait_ge(S["dn_t1"], 2 * s + hf + 1)
                    fn(d_t1[:, hf * W:(hf + 1) * W], pm[:, 2 * hf, :], ACT.Copy).then_inc(S["dn_t1c"], 1)
            act.wait_ge(S["dn_uw"], 1)
            fn(d_u, pm[:, 0:2, :].rearrange("p a b -> p (a b)"), ACT.Copy)
            fn(d_w, pm[:, 2:4, :].rearrange("p a b -> p (a b)"), ACT.Copy).then_inc(S["dn_uws"], 1)
            act.wait_ge(S["sc_su"], 4)
            fn(d_osq, pm[:, 1:3, :].rearrange("p a b -> p (a b)"), ACT.Square).then_inc(S["dn_osq"], 1)
            act.wait_ge(S["dn_oss"], 1)
            rstd(rs[:, 0:8], ss[:, 0:8], DH, eps6).then_inc(S["dn_orn"], 1)
            turn("oa", BRhi[:, 0:4, :])

            act.wait_ge(S["t_lo"], turns["oa"][0] + turns["oa"][1])
            act.dma_start(posi[:], a["positions"]).then_inc(S["m_in"], 16)
            act.dma_start(m_g[:, 0, :], a["mla_qk_q_g"].partition_broadcast(P)).then_inc(S["m_in"], 16)
            act.dma_start(m_g[:, 1, :], a["mla_qk_k_g"].partition_broadcast(P)).then_inc(S["m_in"], 16)
            for t in range(NT):
                fn(cn[:, t, 0:MLA_QR], abc[:, t, 8:8 + MLA_QR], ACT.Square, accum_out=ss[:, 2 * t:2 * t + 1])
                last = fn(cn[:, t, MLA_QR:3 * P], abc[:, t, 8 + MLA_QR:8 + 3 * P], ACT.Square,
                          accum_out=ss[:, 2 * t + 1:2 * t + 2])
            link(last)
            link(fn(rs[:, 0:4:2], ss[:, 0:4:2], ACT.Ln, scale=1.0 / MLA_QR, bias=eps6))
            link(fn(rs[:, 1:4:2], ss[:, 1:4:2], ACT.Ln, scale=1.0 / MLA_KVR, bias=eps6))
            fn(rs[:, 0:4], rs[:, 0:4], ACT.Exp, scale=-0.5).then_inc(S["m_cn"], 1)
            act.wait_ge(S["m_ang"], 1)
            fn(cs[:], ang[:, 0:2, :, :], ACT.Sin).then_inc(S["m_cs"], 1)
            turn("cqkv", MQhi, lambda f: acol("mla_q_norm_g", f) if f < 2 else acol("mla_kv_norm_g"))
            for j in range(2):
                leave(f"uq{j}", mq[:, 0, :, 2 * j:2 * j + 2, :].rearrange("p t h d -> p t (h d)"))
            for j in range(2):
                ready(f"ukv{j}")
                view = accT(f"ukv{j}").rearrange("p t (h d) -> p t h d", h=2)
                fn(mq[:, 1, :, 2 * j:2 * j + 2, 0:NOPE], view[:, :, :, 0:NOPE], ACT.Copy)
                fn(mv[:].rearrange("p t (h d) -> p t h d", h=4)[:, :, 2 * j:2 * j + 2, :],
                   view[:, :, :, NOPE:NOPE + P], ACT.Copy).then_inc(evac_at(f"ukv{j}")[0], 1)
            for i in range(2):
                act.wait_ge(S["m_cn2"], 2 + i)
                if i == 0:
                    act.wait_ge(*evac_at("uq1"))
                else:
                    act.wait_ge(*evac_at("ukv1"))
                fn(msq[:].rearrange("p (t h d) -> p t h d", t=NT, h=4), mq[:, i], ACT.Square).then_inc(S["m_sqs"], 1)
                act.wait_ge(S["m_ss"], i + 1)
                rstd(rs[:, 8 * i:8 * i + 8], ss[:, 8 * i:8 * i + 8], QK, eps6).then_inc(S["m_rn"], 1)
            act.wait_ge(S["m_tn"], 1)
            fn(mT[:].rearrange("p a b -> p (a b)"), pm[:].rearrange("p a b -> p (a b)"), ACT.Copy)\
                .then_inc(S["m_tnc"], 1)
            act.wait_ge(S["m_tr"], 1)
            fn(mR[:].rearrange("p a b -> p (a b)"), pm[0:ROPE].rearrange("p a b -> p (a b)"), ACT.Copy)\
                .then_inc(S["m_trc"], 1)

            def attention(n, s, pt, branch):
                act.wait_ge(S["a_s"], n + 1)
                for h in range(4):
                    fn(s[:, h, 0:P], s[:, h, 0:P], ACT.Exp, bias=attn_neg[:, h, 0:1],
                       accum_out=attn_sum[:, h, 0:1])
                    last = fn(s[:, h, P:3 * P], s[:, h, P:3 * P], ACT.Exp, bias=attn_neg[:, h, 1:2],
                              accum_out=attn_sum[:, h, 1:2])
                last.then_inc(S["a_e"], 1)
                act.wait_ge(S["a_pt"], n + 1)
                fn(pt[:], pm[:, :, 0:3 * P], ACT.Copy).then_inc(S["a_ptc"], 1)
                act.wait_ge(S["a_o"], n + 1)
                fn(BRhi[:, 4 * branch:4 * branch + 4, :].rearrange("p a b -> p (a b)"),
                   pm[:, 0:2, :].rearrange("p a b -> p (a b)"), ACT.Copy).then_inc(S["a_hi"], 1)

            mS = mq[:, 0].rearrange("p t h d -> p (t h d)").rearrange("p (h s) -> p h s", h=4)
            mP = mq[:, 1].rearrange("p t h d -> p (t h d)").rearrange("p (h s) -> p h s", h=4)
            attention(0, mS, mP, 1)

            act.wait_ge(S["a_lo"], 1)
            fn(fsq[:], fx[:, :, 0:D], ACT.Square).then_inc(S["f_sq"], 1)
            act.wait_ge(S["f_ss"], 1)
            rstd(rs[:, 0:16], ss[:, 0:16], DH, eps6).then_inc(S["f_rn"], 1)
            act.wait_ge(S["f_t"], 1)
            for i in range(2):
                last = fn(fT[:, 4 * i:4 * i + 4, :].rearrange("p a b -> p (a b)"),
                          pm[:, 2 * i:2 * i + 2, :].rearrange("p a b -> p (a b)"), ACT.Copy,
                          scale=acol(("fox_q_norm_g", "fox_k_norm_g")[i]))
            last.then_inc(S["f_tc"], 1)
            attention(1, fS, fPT, 3)

            act.wait_ge(S["a_lo"], 2)
            act.dma_start(sw[:], a["sg_w_s"].rearrange("g t s -> t g s")).then_inc(S["s_w"], 16)
            act.dma_start(s_ng[:], a["sg_v_norm_g"].partition_broadcast(P)).then_inc(S["s_w"], 16)
            act.dma_start(s_b[:], a["sg_b_s"].partition_broadcast(P)).then_inc(S["s_w"], 16)
            fn(sgq[:], sgv[:], ACT.Square).then_inc(S["s_sq"], 1)
            act.wait_ge(S["s_ss"], 1)
            rstd(rs[:, 0:8], ss[:, 0:8], P, eps6).then_inc(S["s_rn"], 1)
            act.wait_ge(S["s_m"], 1)
            fn(BRhi[:, 8:12, :], sm[:], ACT.Copy).then_inc(S["s_hi"], 1)

            act.wait_ge(S["s_lo"], 1)
            n = 0
            for c in range(2):
                for i in range(4):
                    if n >= 2:
                        act.wait_ge(*evac_at(f"br{(n - 2) % 4}_{(n - 2) // 4}"))
                    leave(f"gate{i}_{c}", gt[:, n % 2], ACT.Sigmoid)
                    high_halves(landed(f"br{i}_{c}") + AHEAD)
                    n += 1
            turn("merged", XThi)
            for c in range(2):
                high_halves(landed(f"wo{c}") + AHEAD)
            act.wait_ge(*evac_at("wo1"))
            act.wait_ge(S["t_lo"], turns["merged"][0] + turns["merged"][1])
            for t in range(NT):
                last = fn(XN[:, t, :], X[:, t, :], ACT.Square, accum_out=ss[:, t:t + 1])
            link(last)
            rstd(rs[:, 0:NT], ss[:, 0:NT], D, eps6).then_inc(S["rstd"], 1)
            turn("x2", XThi, lambda f: acol("norm2_g", f))

            for c in range(DFF // W):
                high_halves(landed(f"f1_{c}") + AHEAD)
                act.wait_ge(S["f1_r"], c + 1)
                if c >= 1:
                    act.wait_ge(S["f1_lo"], c)
                link(fn(f1s[:], f1r[:], ACT.Square))
                fn(FFhi[:, 4 * c:4 * c + 4, :], f1s[:], ACT.Copy).then_inc(S["f1_hi"], 1)
            for c in range(2):
                high_halves(landed(f"f2_{c}") + AHEAD)

            act.wait_ge(*evac_at("f2_1"))
            act.dma_start(pin[:], a["p0"].rearrange("(t p) d -> p t d", p=P)).then_inc(S["p_in"], 16)
            turn("x3", XThi)
            turn("p0", PThi)
            act.wait_ge(S["c2_in"], 1)
            leave("xbc0", conv2[:, 0:4, 3:3 + TOK])
            leave("xbc1", conv2[:, 4:8, 3:3 + TOK])

            def silu2(j):
                act.wait_ge(S["conv2"], j + 1)
                fn(xbcT[:, 4 * j:4 * j + 4, :], xbcT[:, 4 * j:4 * j + 4, :], ACT.Silu).then_inc(S["silu2"], 1)
            leave("xbc2", conv2[:, 8:12, 3:3 + TOK])
            for j in range(3):
                silu2(j)
            high_halves(landed("dt") + AHEAD)
            for c in range(2):
                leave(f"mz{c}", zz[:, :, c * W:(c + 1) * W], ACT.Silu)
            act.wait_ge(S["dt_in"], 1)
            fn(ea2[:], headv("ssd_a_log"), ACT.Exp)
            fn(sp_y[:], sp_y[:], ACT.Exp, scale=-1.0).then_inc(S["dt_e"], 1)
            act.wait_ge(S["s_xs"], 1)
            fn(xs[:].rearrange("p t d -> p (t d)"), pm[:].rearrange("p a b -> p (a b)"), ACT.Copy)\
                .then_inc(S["s_xsc"], 1)
            act.wait_ge(S["s_bt"], 1)
            fn(bmt[:], pm[:, 0, 0:2 * P], ACT.Copy).then_inc(S["s_btc"], 1)
            act.wait_ge(S["s_acc"], 1)
            fn(eac[:], acs[:, 1:3, :], ACT.Exp).then_inc(S["s_eac"], 1)
            act.wait_ge(S["s_st"], 1)
            fn(hst[:], pm[:, 2:4, :].rearrange("p a b -> p (a b)"), ACT.Copy).then_inc(S["s_stc"], 1)
            for b in range(4):
                act.wait_ge(S["b_e0"], b + 1)
                fn(em[:], em[:], ACT.Exp).then_inc(S["b_e"], 1)
            act.wait_ge(S["y_z"], 1)
            for t in range(NT):
                for g in range(2):
                    last = fn((xe, hst)[t][:, g * W:(g + 1) * W], yd[:, t, g * W:(g + 1) * W], ACT.Square,
                              accum_out=ss[:, 2 * t + g:2 * t + g + 1])
            link(last)
            rstd(rs[:, 0:4], ss[:, 0:4], W, eps5).then_inc(S["y_ss"], 1)
            turn("y", BYhi[:, 0:8, :], lambda f: bcol("ssd_norm_w", f))
            act.wait_ge(S["c_ready"], 1)
            for c in range(2):
                if c:
                    act.wait_ge(*evac_at("sh0"))
                leave(f"sc{c}", scc[:])
                high_halves(landed(f"sh{c}") + AHEAD)
                high_halves(landed(f"sb{c}") + AHEAD)
                act.wait_ge(S["c_out"], c + 1)
                fn(BYhi[:, 8 + 4 * c:12 + 4 * c, :], scv[:], ACT.Copy).then_inc(S["c_hi"], 1)

            def load_rows(i):
                for j, n in enumerate(("ln_mix_g", "ln_mix_b", "ln_ffn_g", "ln_ffn_b", "b_ple_gate")):
                    act.dma_start(lnr[:, j, :], a[f"{n}{i}"].partition_broadcast(P)).then_inc(S["ln_in"], 16)
            load_rows(0)
            for c in range(2):
                high_halves(landed(f"mo{c}") + AHEAD)

            def layer_norm(n):
                act.wait_ge(S["ln_x"], n + 1)
                for t in range(NT):
                    last = fn(xc[:, t, :], X[:, t, :], ACT.Copy, accum_out=ss[:, t:t + 1])
                link(last)
                fn(rs[:, 0:NT], ss[:, 0:NT], ACT.Copy, scale=-1.0 / D).then_inc(S["ln_sum"], 1)
                act.wait_ge(S["ln_xc"], n + 1)
                for t in range(NT):
                    last = fn(junk[:, t, :], xc[:, t, :], ACT.Square, accum_out=ss[:, 2 + t:3 + t])
                link(last)
                rstd(rs[:, 2:4], ss[:, 2:4], D, eps5).then_inc(S["ln_rs"], 1)

            layer_norm(0)

            def feed_forward(i):
                turn(("x4", "x7")[i], XThi)
                for c in range(-(-DFF2 // W)):
                    k = 6 * i + c
                    nf = chunks[f"fg{i}_{c}"][4] // P
                    if k:
                        act.wait_ge(S["h_x"], k)
                    leave(f"fg{i}_{c}", sg[:, 0:nf, :], ACT.Silu)
                    high_halves(landed(f"fu{i}_{c}") + AHEAD)
                    act.wait_ge(S["h_x"], k + 1)
                    fn(Hhi[:, 4 * c:4 * c + nf, :], fh[:, 0:nf, :], ACT.Copy).then_inc(S["h_hi"], 1)
                for c in range(2):
                    high_halves(landed(f"fd{i}_{c}") + AHEAD)
                layer_norm(2 * i + 1)
                turn(("x5", "x8")[i], XThi)
                for c in range(2):
                    high_halves(landed(f"pg{i}_{c}") + AHEAD)
                    act.wait_ge(S["g_x"], 2 * i + c + 1)
                    fn(pgt[:], pgt[:], ACT.Sigmoid).then_inc(S["g_s"], 1)
                    high_halves(landed(f"pw{i}_{c}") + AHEAD)
            feed_forward(0)

            act.wait_ge(S["x_end"], 1)
            load_rows(1)
            act.dma_start(bv[:], a["b_v"].partition_broadcast(P)).then_inc(S["q_in"], 16)
            act.dma_start(bo[:], a["b_o"].partition_broadcast(P)).then_inc(S["q_in"], 16)
            turn("x6", XThi)
            for c in range(2):
                ready(f"aq{c}")
                for f in range(4):
                    last = fn(aqT[:, 4 * c + f, :], accF(f"aq{c}")[:, f, :], ACT.Identity,
                              bias=bcol("b_qk", 4 * c + f))
                last.then_inc(evac_at(f"aq{c}")[0], 1)
            ready("ak")
            for f in range(2):
                last = fn(akr[:, f, :], accF("ak")[:, f, :], ACT.Identity, bias=bcol("b_qk", 8 + f))
            last.then_inc(evac_at("ak")[0], 1)
            high_halves(landed("av") + AHEAD)
            for kv in range(AKV):
                n = 2 + kv
                act.wait_ge(S["a_s"], n + 1)
                for h in range(4):
                    fn(wS[:, h, 0:P], wS[:, h, 0:P], ACT.Exp, bias=attn_neg[:, h, 0:1],
                       accum_out=attn_sum[:, h, 0:1])
                    fn(wS[:, h, P:3 * P], wS[:, h, P:3 * P], ACT.Exp, bias=attn_neg[:, h, 1:2],
                       accum_out=attn_sum[:, h, 1:2])
                fn(esink[:], esink[:], ACT.Exp).then_inc(S["a_e"], 1)
                act.wait_ge(S["a_pt"], n + 1)
                fn(wPT[:], pm[:, :, 0:3 * P], ACT.Copy).then_inc(S["a_ptc"], 1)
                act.wait_ge(S["a_o"], n + 1)
                fn(AThi[:, 2 * kv:2 * kv + 2, :].rearrange("p a b -> p (a b)"), pm[:, 0, :], ACT.Copy)\
                    .then_inc(S["a_hi"], 1)
            act.wait_ge(S["a_lo"], 6)
            act.dma_start(pin1[:], a["p1"].rearrange("(t p) d -> p t d", p=P)).then_inc(S["p_in"], 16)
            for c in range(2):
                high_halves(landed(f"ao{c}") + AHEAD)
            layer_norm(2)
            turn("p1", PThi)
            feed_forward(1)

        @block.vector
        def _(v):
            seq = [0]
            V = nc.vector

            def link(ins):
                seq[0] += 1
                ins.then_inc(S["dve_seq"], 1)
                v.wait_ge(S["dve_seq"], seq[0])

            def turn(name, hi, lo, gain=None):
                g0, n, nf = turns[name]
                for g in range(n):
                    k = min(2, nf - 2 * g)
                    v.wait_ge(S["t_hi"], g0 + g + 1)
                    bank = pm[:, (g0 + g) % 4, 0:k * TOK].rearrange("p (f t) -> p f t", t=TOK)
                    if gain is None:
                        V.tensor_tensor(lo[:, 2 * g:2 * g + k, :], bank, hi[:, 2 * g:2 * g + k, :].bitcast(F32),
                                        ALU.subtract).then_inc(S["t_lo"], 1)
                    else:
                        for f in range(k):
                            last = V.scalar_tensor_tensor(
                                out=lo[:, 2 * g + f, :], in0=bank[:, f, :], scalar=gain(2 * g + f),
                                in1=hi[:, 2 * g + f, :].bitcast(F32), op0=ALU.mult, op1=ALU.subtract)
                        last.then_inc(S["t_lo"], 1)

            def softplus_tail(x, y, n):
                z, z2, p, o = (b[:, :, 0:n] for b in (sp_z, sp_z2, sp_p, sp))
                link(V.tensor_scalar(z, y, 2.0, None, ALU.add))
                link(V.reciprocal(z, z))
                link(V.tensor_tensor(z, z, y, ALU.mult))
                link(V.tensor_tensor(z2, z, z, ALU.mult))
                link(V.tensor_scalar(p, z2, 1.0 / 17, 1.0 / 15, ALU.mult, ALU.add))
                link(V.tensor_tensor(p, p, z2, ALU.mult))
                for k in (13, 11, 9, 7, 5, 3):
                    link(V.scalar_tensor_tensor(out=p, in0=p, scalar=1.0 / k, in1=z2, op0=ALU.add, op1=ALU.mult))
                link(V.scalar_tensor_tensor(out=p, in0=p, scalar=1.0, in1=z, op0=ALU.add, op1=ALU.mult))
                link(V.tensor_scalar(o, x, 0.0, None, ALU.max))
                link(V.scalar_tensor_tensor(out=o, in0=p, scalar=2.0, in1=o, op0=ALU.mult, op1=ALU.add))

            def heads_of(col, n=P):
                return col.rearrange("p t h -> p h t").unsqueeze(3).to_broadcast([P, 4, NT, n])

            def ht(ap):
                return ap.rearrange("p (h t s) -> p h t s", h=4, t=NT)

            v.wait_ge(S["rstd"], 1)
            for t in range(NT):
                last = V.tensor_scalar(XN1[:, t, :], X[:, t, :], rs[:, t:t + 1], None, ALU.mult)
            last.then_inc(S["xn"], 1)
            V.memset(conv_in[:, :, 0:3], 0.0).then_inc(S["conv_in"], 1)
            v.wait_ge(S["cols"], 2)
            turn("x1", XThi, XTlo, lambda f: acol("norm1_g", f))

            for j, name in enumerate(("dq", "dk", "dv")):
                v.wait_ge(*evac_at(name))
                for k in range(4):
                    for f in range(4 * j, 4 * j + 4):
                        w = acol("dn_conv_w", 12 * k + f)
                        if k == 0:
                            last = V.tensor_scalar(qkv[:, f, :], conv_in[:, f, 0:TOK], w, None, ALU.mult)
                        else:
                            last = V.scalar_tensor_tensor(out=qkv[:, f, :], in0=conv_in[:, f, k:k + TOK], scalar=w,
                                                          in1=qkv[:, f, :], op0=ALU.mult, op1=ALU.add)
                    if k < 3:
                        link(last)
                last.then_inc(S["conv"], 1)
            v.wait_ge(*evac_at("abc"))
            v.wait_ge(*evac_at("ff"))
            V.tensor_tensor(logit[:, :, 0:4], abc[:, :, 0:4],
                            headv("dn_dt_bias").unsqueeze(1).to_broadcast([P, NT, 4]), ALU.add)
            link(V.tensor_tensor(logit[:, :, 4:8], ffl[:],
                                 headv("fox_f_bias").unsqueeze(1).to_broadcast([P, NT, 4]), ALU.add))
            link(V.tensor_scalar(logit[:, :, 4:8], logit[:, :, 4:8], -1.0, None, ALU.mult))
            V.scalar_tensor_tensor(out=sp_y[:, :, 0:8], in0=logit[:, :, 0:8], scalar=-1.0, in1=logit[:, :, 0:8],
                                   op0=ALU.mult, op1=ALU.max).then_inc(S["sp_in"], 1)
            v.wait_ge(S["sp_e"], 1)
            softplus_tail(logit[:, :, 0:8], sp_y[:, :, 0:8], 8)
            V.tensor_copy(nlf[:], sp[:, :, 4:8])
            V.scalar_tensor_tensor(out=dng[:], in0=sp[:, :, 0:4], scalar=-1.0,
                                   in1=ea[:].unsqueeze(1).to_broadcast([P, NT, 4]), op0=ALU.mult, op1=ALU.mult)
            link(V.tensor_scalar(beta[:], beta[:], 1.0, None, ALU.add))
            V.reciprocal(beta[:], beta[:]).then_inc(S["dn_g"], 1)
            v.wait_ge(S["dn_gc"], 1)
            link(V.tensor_copy(gcs[:], pm[:, 0, 0:16].rearrange("p (k h) -> p k h", h=4)))
            V.tensor_tensor(gcs[:, 2:4, :], gcs[:, 2:4, :], gcs[:, 0:2, :], ALU.subtract).then_inc(S["dn_gcs"], 1)

            v.wait_ge(S["dn_rn"], 1)
            V.scalar_tensor_tensor(out=qT, in0=qT, scalar=DH ** -0.5, in1=d_rn[:, 0:1024], op0=ALU.mult, op1=ALU.mult)
            V.tensor_tensor(kT, kT, d_rn[:, 1024:2048], ALU.mult).then_inc(S["dn_qkn"], 1)
            v.wait_ge(S["dn_rows"], 1)
            for h in range(4):
                for t in range(NT):
                    i = (h * NT + t) * P
                    last = V.scalar_tensor_tensor(out=d_e[:, i:i + P], in0=pm[:, i // BANK, i % BANK:i % BANK + P],
                                                  scalar=gcs[:, t, h:h + 1], in1=con("strict64"),
                                                  op0=ALU.subtract, op1=ALU.mult)
            last.then_inc(S["dn_e0"], 1)
            v.wait_ge(S["dn_gex"], 1)
            V.tensor_tensor(gex[:, 2], beta[:], gex[:, 0], ALU.mult)
            v.wait_ge(S["dn_kk"], 1)
            v.wait_ge(S["dn_e"], 1)
            V.scalar_tensor_tensor(out=d_lt, in0=d_e, scalar=1.0, in1=pm[:, 0:2, :].rearrange("p a b -> p (a b)"),
                                   op0=ALU.min, op1=ALU.mult)
            V.scalar_tensor_tensor(out=d_at, in0=d_e, scalar=1.0, in1=pm[:, 2:4, :].rearrange("p a b -> p (a b)"),
                                   op0=ALU.min, op1=ALU.mult).then_inc(S["dn_lt"], 1)
            v.wait_ge(S["dn_lt"], 1)
            v.wait_ge(S["dn_egr"], 1)
            V.tensor_tensor(d_lt, d_lt, d_br, ALU.mult)
            V.tensor_tensor(d_at.rearrange("p (k s) -> p k s", s=P), d_at.rearrange("p (k s) -> p k s", s=P),
                            con("tri64").unsqueeze(1).to_broadcast([P, 8, P]), ALU.mult)
            for x in (d_x, d_y):
                last = V.tensor_copy(x.rearrange("p (k s) -> p k s", s=P), ident.unsqueeze(1).to_broadcast([P, 8, P]))
            link(last)
            v.wait_ge(S["dn_kv"], 1)
            kp = ht(pm[:, 0:2, :].rearrange("p a b -> p (a b)"))
            vp = ht(pm[:, 2:4, :].rearrange("p a b -> p (a b)"))
            V.tensor_tensor(ht(d_kbe), kp, heads_of(gex[:, 2]), ALU.mult)
            V.tensor_tensor(ht(d_kdec), kp, heads_of(gex[:, 1]), ALU.mult)
            V.tensor_tensor(ht(d_vb), vp, heads_of(beta[:]), ALU.mult).then_inc(S["dn_vb"], 1)
            for s in range(6):
                for hf in range(2):
                    half = slice(hf * W, (hf + 1) * W)
                    if s:
                        v.wait_ge(S["dn_pq"], 2 * (s - 1) + hf + 1)
                        V.tensor_tensor(d_x[:, half], d_x[:, half], pm[:, 2 * hf + 1, :], ALU.subtract)
                        V.tensor_tensor(d_y[:, half], d_y[:, half], pm[:, 2 * hf, :], ALU.subtract)
                    V.tensor_tensor(d_ml[:, half].rearrange("p (k s) -> p k s", s=P),
                                    d_lt[:, half].rearrange("p (k s) -> p k s", s=P),
                                    con(f"lvl{s}").unsqueeze(1).to_broadcast([P, 4, P]), ALU.mult)\
                        .then_inc(S["dn_ml"], 1)
            for hf in range(2):
                half = slice(hf * W, (hf + 1) * W)
                v.wait_ge(S["dn_pq"], 10 + hf + 1)
                V.tensor_tensor(d_y[:, half], d_y[:, half], pm[:, 2 * hf, :], ALU.subtract).then_inc(S["dn_y"], 1)
            V.tensor_tensor(qT, qT, d_egr, ALU.mult).then_inc(S["dn_y"], 1)
            u4 = d_u.rearrange("p (h t s) -> p h t s", h=4, t=NT)
            vn4 = d_vn.rearrange("p (h t s) -> p h t s", h=4, t=NT)
            for n in range(4):
                t, r = n // 2, 64 * (n % 2)
                if n == 0:
                    v.wait_ge(S["dn_uws"], 1)
                    V.tensor_copy(vn4[r:r + 64, :, t, :], u4[r:r + 64, :, t, :]).then_inc(S["sc_vn"], 1)
                else:
                    v.wait_ge(S["sc_ws"], n)
                    V.tensor_tensor(vn4[r:r + 64, :, t, :], u4[r:r + 64, :, t, :],
                                    pm[r:r + 64, 0, :].rearrange("p (h s) -> p h s", h=4), ALU.subtract)\
                        .then_inc(S["sc_vn"], 1)
                v.wait_ge(S["sc_su"], n + 1)
                if n == 0:
                    V.tensor_copy(d_s, pm[:, 3, :]).then_inc(S["sc_s"], 1)
                elif n < 3:
                    for h in range(4):
                        g = d_egr[:, h * TOK + 64 * n + 63:h * TOK + 64 * n + 64]
                        last = V.scalar_tensor_tensor(out=d_s[:, h * P:(h + 1) * P], in0=d_s[:, h * P:(h + 1) * P],
                                                      scalar=g, in1=pm[:, 3, h * P:(h + 1) * P],
                                                      op0=ALU.mult, op1=ALU.add)
                    last.then_inc(S["sc_s"], 1)
            v.wait_ge(S["dn_osq"], 1)
            V.tensor_reduce(ss[:, 0:8], d_osq.rearrange("p (k s) -> p k s", s=P), AX_X, ALU.add)\
                .then_inc(S["dn_oss"], 1)
            v.wait_ge(S["dn_orn"], 1)
            o8 = d_o.rearrange("p (k s) -> p k s", s=P)
            link(V.tensor_tensor(o8, pm[:, 1:3, :].rearrange("p a (h s) -> p (a h) s", s=P),
                                 rs[:, 0:8].unsqueeze(2).to_broadcast([P, 8, P]), ALU.mult))
            link(V.tensor_tensor(o8, o8, o_g[:].unsqueeze(1).to_broadcast([P, 8, P]), ALU.mult))
            V.tensor_tensor(d_o, d_o, zs[:].rearrange("p t d -> p (t d)"), ALU.mult).then_inc(S["dn_o"], 1)
            turn("oa", BRhi[:, 0:4, :], BRlo[:, 0:4, :])

            v.wait_ge(S["m_in"], 48)
            link(V.tensor_copy(posf[:], posi[:]))
            freq = con("freq").unsqueeze(1).to_broadcast([P, NT, ROPE // 2])
            pos = posf[:].unsqueeze(2).to_broadcast([P, NT, ROPE // 2])
            link(V.tensor_tensor(ang[:, 2], freq, pos, ALU.mult))
            big = 1.5 * 2 ** 23
            for i, turn_at in ((0, 0.25), (1, 0.0)):
                link(V.tensor_scalar(ang[:, i], ang[:, 2], 1.0 / (2 * np.pi), turn_at, ALU.mult, ALU.add))
                link(V.tensor_scalar(ang[:, i], ang[:, i], big, None, ALU.add))
                link(V.tensor_scalar(ang[:, i], ang[:, i], -big, None, ALU.add))
                parts = (6.28125, 0.00193500518798828125, 2 * np.pi - 6.28125 - 0.00193500518798828125)
                tmp = rt[:, 0].rearrange("p t h d -> p (t h d)")[:, 0:NT * 32].rearrange("p (t d) -> p t d", t=NT)
                link(V.scalar_tensor_tensor(out=tmp, in0=ang[:, i], scalar=-parts[0], in1=ang[:, 2],
                                            op0=ALU.mult, op1=ALU.add))
                link(V.scalar_tensor_tensor(out=tmp, in0=ang[:, i], scalar=-parts[1], in1=tmp,
                                            op0=ALU.mult, op1=ALU.add))
                link(V.scalar_tensor_tensor(out=ang[:, i], in0=ang[:, i], scalar=-parts[2], in1=tmp,
                                            op0=ALU.mult, op1=ALU.add))
                if i == 0:
                    link(V.tensor_scalar(ang[:, 0], ang[:, 0], np.pi / 2, None, ALU.add))
            lim = 3.1415925
            V.tensor_scalar(ang[:, 0:2], ang[:, 0:2], lim, -lim, ALU.min, ALU.max).then_inc(S["m_ang"], 1)
            v.wait_ge(S["m_cn"], 1)
            for t in range(NT):
                V.tensor_scalar(cn[:, t, 0:MLA_QR], abc[:, t, 8:8 + MLA_QR], rs[:, 2 * t:2 * t + 1], None, ALU.mult)
                last = V.tensor_scalar(cn[:, t, MLA_QR:3 * P], abc[:, t, 8 + MLA_QR:8 + 3 * P],
                                       rs[:, 2 * t + 1:2 * t + 2], None, ALU.mult)
            last.then_inc(S["m_cn2"], 1)
            turn("cqkv", MQhi, MQlo, lambda f: acol("mla_q_norm_g", f) if f < 2 else acol("mla_kv_norm_g"))
            V.tensor_copy(mq[:, 1, :, :, NOPE:QK],
                          abc[:, :, 8 + 3 * P:ABC].unsqueeze(2).to_broadcast([P, NT, 4, ROPE]))\
                .then_inc(S["m_cn2"], 1)
            for i in range(2):
                v.wait_ge(S["m_sqs"], i + 1)
                V.tensor_reduce(ss[:, 8 * i:8 * i + 8], msq[:].rearrange("p (k d) -> p k d", d=QK), AX_X, ALU.add)\
                    .then_inc(S["m_ss"], 1)
                if i == 0:
                    v.wait_ge(S["m_ss"], 1)
                    V.tensor_scalar(posf[:], posf[:], 1.0, None, ALU.mult).then_inc(S["m_cn2"], 1)
                v.wait_ge(S["m_rn"], i + 1)
                q8 = mq[:, i].rearrange("p t h d -> p (t h) d")
                link(V.tensor_tensor(q8, q8, rs[:, 8 * i:8 * i + 8].unsqueeze(2).to_broadcast([P, 8, QK]), ALU.mult))
                link(V.tensor_tensor(q8, q8, m_g[:, i, :].unsqueeze(1).to_broadcast([P, 8, QK]), ALU.mult))
                if i == 0:
                    v.wait_ge(S["m_cs"], 1)
                x1, x2 = mq[:, i, :, :, NOPE:NOPE + 32], mq[:, i, :, :, NOPE + 32:QK]
                cos = cs[:, 0].unsqueeze(2).to_broadcast([P, NT, 4, 32])
                sin = cs[:, 1].unsqueeze(2).to_broadcast([P, NT, 4, 32])
                V.tensor_tensor(rt[:, 0], x1, cos, ALU.mult)
                V.tensor_tensor(rt[:, 1], x2, sin, ALU.mult)
                V.tensor_tensor(rt[:, 2], x2, cos, ALU.mult)
                link(V.tensor_tensor(rt[:, 3], x1, sin, ALU.mult))
                V.tensor_tensor(x1, rt[:, 0], rt[:, 1], ALU.subtract)
                V.tensor_tensor(x2, rt[:, 2], rt[:, 3], ALU.add).then_inc(S["m_rope"], 1)

            def attention(n, s, scale, add, branch):
                v.wait_ge(S["a_sc"], n + 1)
                link(V.scalar_tensor_tensor(out=s, in0=pm[:, :, 0:3 * P], scalar=scale, in1=add,
                                            op0=ALU.mult, op1=ALU.add))
                V.tensor_reduce(attn_neg[:, :, 0:1], s[:, :, 0:P], AX_X, ALU.max, negate=True)
                V.tensor_reduce(attn_neg[:, :, 1:2], s[:, :, P:3 * P], AX_X, ALU.max, negate=True)\
                    .then_inc(S["a_s"], 1)
                v.wait_ge(S["a_e"], n + 1)
                link(V.reciprocal(attn_inv[:], attn_sum[:]))
                V.tensor_tensor(s[:, :, 0:P], s[:, :, 0:P], attn_inv[:, :, 0:1].to_broadcast([P, 4, P]), ALU.mult)
                V.tensor_tensor(s[:, :, P:3 * P], s[:, :, P:3 * P],
                                attn_inv[:, :, 1:2].to_broadcast([P, 4, 2 * P]), ALU.mult).then_inc(S["a_p"], 1)
                v.wait_ge(S["a_hi"], n + 1)
                bank = pm[:, 0:2, :].rearrange("p a b -> p (a b)")
                V.tensor_tensor(BRlo[:, 4 * branch:4 * branch + 4, :].rearrange("p a b -> p (a b)"), bank,
                                BRhi[:, 4 * branch:4 * branch + 4, :].rearrange("p a b -> p (a b)").bitcast(F32),
                                ALU.subtract).then_inc(S["a_lo"], 1)

            mS = mq[:, 0].rearrange("p t h d -> p (t h d)").rearrange("p (h s) -> p h s", h=4)
            mask = span("causal0", "causal1").unsqueeze(1).to_broadcast([P, 4, 3 * P])
            attention(0, mS, QK ** -0.5, mask, 1)

            v.wait_ge(S["f_sq"], 1)
            V.tensor_reduce(ss[:, 0:16], fsq[:].rearrange("p t (k d) -> p (t k) d", d=DH), AX_X, ALU.add)\
                .then_inc(S["f_ss"], 1)
            v.wait_ge(S["f_rn"], 1)
            V.tensor_tensor(fx[:, :, 0:D].rearrange("p t (k d) -> p t k d", d=DH),
                            fx[:, :, 0:D].rearrange("p t (k d) -> p t k d", d=DH),
                            rs[:, 0:16].rearrange("p (t k) -> p t k", t=NT).unsqueeze(3)
                            .to_broadcast([P, NT, 8, DH]), ALU.mult).then_inc(S["f_xn"], 1)
            v.wait_ge(S["f_cum"], 1)
            link(V.tensor_copy(ncs[:], pm[:, 0, 0:8].rearrange("p (t h) -> p t h", t=NT)))
            v.wait_ge(S["f_cum"], 2)
            for h in range(4):
                row = pm[:, 1 + h // 2, (h % 2) * TOK:(h % 2) * TOK + TOK]
                V.scalar_tensor_tensor(out=fD[:, h, 0:P], in0=row[:, 0:P], scalar=ncs[:, 0, h:h + 1],
                                       in1=con("causal0"), op0=ALU.subtract, op1=ALU.add)
                last = V.scalar_tensor_tensor(out=fD[:, h, P:3 * P], in0=row, scalar=ncs[:, 1, h:h + 1],
                                              in1=span("open", "causal1"), op0=ALU.subtract, op1=ALU.add)
            last.then_inc(S["f_d"], 1)
            v.wait_ge(S["f_d"], 1)
            attention(1, fS[:], DH ** -0.5, fD[:], 3)

            v.wait_ge(S["s_w"], 48)
            v.wait_ge(S["s_sq"], 1)
            V.tensor_reduce(ss[:, 0:8], sgq[:].rearrange("p t (k d) -> p (t k) d", d=P), AX_X, ALU.add)\
                .then_inc(S["s_ss"], 1)
            v.wait_ge(S["s_rn"], 1)
            v8 = sgv[:].rearrange("p t (k d) -> p (t k) d", d=P)
            link(V.tensor_tensor(v8, v8, rs[:, 0:8].unsqueeze(2).to_broadcast([P, 8, P]), ALU.mult))
            V.tensor_tensor(sgv[:], sgv[:], s_ng[:].unsqueeze(1).to_broadcast([P, NT, W]), ALU.mult)
            v.wait_ge(S["s_wt"], 1)
            V.tensor_tensor(swT[:], pm[:, 3, :].rearrange("p (g t) -> p g t", g=4),
                            con("tri").unsqueeze(1).to_broadcast([P, 4, P]), ALU.mult).then_inc(S["s_v"], 1)
            v.wait_ge(S["s_mx"], 1)
            mixed = pm[:, 0:2, :].rearrange("p a (g n t) -> p (a g) n t", g=2, n=NT)
            link(V.tensor_tensor(sm[:].rearrange("p g (n t) -> p g n t", n=NT), mixed,
                                 s_b[:].rearrange("p (g t) -> p g t", g=4).unsqueeze(2)
                                 .to_broadcast([P, 4, NT, P]), ALU.add))
            V.tensor_tensor(sm[:], sm[:], sgu[:], ALU.mult).then_inc(S["s_m"], 1)
            v.wait_ge(S["s_hi"], 1)
            V.tensor_tensor(BRlo[:, 8:12, :], sm[:], BRhi[:, 8:12, :].bitcast(F32), ALU.subtract)\
                .then_inc(S["s_lo"], 1)

            n = 0
            for c in range(2):
                for i in range(4):
                    v.wait_ge(S["w_used"], landed(f"br{i}_{c}"))
                    v.wait_ge(*evac_at(f"gate{i}_{c}"))
                    dst = merged[:, :, c * W:(c + 1) * W]
                    if i == 0:
                        V.tensor_tensor(dst, accT(f"br{i}_{c}"), gt[:, n % 2], ALU.mult)\
                            .then_inc(evac_at(f"br{i}_{c}")[0], 1)
                    else:
                        V.tensor_tensor(gp[:], accT(f"br{i}_{c}"), gt[:, n % 2], ALU.mult)\
                            .then_inc(evac_at(f"br{i}_{c}")[0], 1)
                        v.wait_ge(*evac_at(f"br{i}_{c}"))
                        link(V.tensor_tensor(dst, dst, gp[:], ALU.add))
                    n += 1
            V.tensor_copy(merged[:, :, 0:1], merged[:, :, 0:1]).then_inc(S["g_done"], 1)
            turn("merged", XThi, XTlo)
            for c in range(2):
                v.wait_ge(S["w_used"], landed(f"wo{c}"))
                x = X[:, :, c * W:(c + 1) * W]
                V.tensor_tensor(x, accT(f"wo{c}"), x, ALU.add).then_inc(evac_at(f"wo{c}")[0], 1)
            v.wait_ge(S["rstd"], 2)
            for t in range(NT):
                last = V.tensor_scalar(XN[:, t, :], X[:, t, :], rs[:, t:t + 1], None, ALU.mult)
            last.then_inc(S["xn"], 1)
            turn("x2", XThi, XTlo, lambda f: acol("norm2_g", f))

            for c in range(DFF // W):
                v.wait_ge(S["w_used"], landed(f"f1_{c}"))
                if c >= 1:
                    v.wait_ge(S["f1_hi"], c)
                V.tensor_scalar(f1r[:], accF(f"f1_{c}"), 0.0, None, ALU.max).then_inc(evac_at(f"f1_{c}")[0], 1)
                v.wait_ge(*evac_at(f"f1_{c}"))
                V.tensor_copy(ss[:, 15:16], ss[:, 14:15]).then_inc(S["f1_r"], 1)
                v.wait_ge(S["f1_hi"], c + 1)
                V.tensor_tensor(FFlo[:, 4 * c:4 * c + 4, :], f1s[:], FFhi[:, 4 * c:4 * c + 4, :].bitcast(F32),
                                ALU.subtract).then_inc(S["f1_lo"], 1)
            for c in range(2):
                v.wait_ge(S["w_used"], landed(f"f2_{c}"))
                x = X[:, :, c * W:(c + 1) * W]
                V.tensor_tensor(x, accT(f"f2_{c}"), x, ALU.add).then_inc(evac_at(f"f2_{c}")[0], 1)

            v.wait_ge(S["w_used"], landed("f2_1"))
            v.wait_ge(S["f1_hi"], DFF // W)
            V.memset(conv2[:, :, 0:3], 0.0).then_inc(S["c2_in"], 1)
            turn("x3", XThi, XTlo)
            turn("p0", PThi, PTlo)
            for j in range(3):
                v.wait_ge(*evac_at(f"xbc{j}"))
                for k in range(4):
                    for f in range(4 * j, 4 * j + 4):
                        w = bcol("ssd_conv_w", 12 * k + f)
                        if k == 0:
                            last = V.tensor_scalar(xbcT[:, f, :], conv2[:, f, 0:TOK], w, bcol("ssd_conv_b", f),
                                                   ALU.mult, ALU.add)
                        else:
                            last = V.scalar_tensor_tensor(out=xbcT[:, f, :], in0=conv2[:, f, k:k + TOK], scalar=w,
                                                          in1=xbcT[:, f, :], op0=ALU.mult, op1=ALU.add)
                    if k < 3:
                        link(last)
                last.then_inc(S["conv2"], 1)
            v.wait_ge(S["w_used"], landed("dt"))
            V.tensor_tensor(logit[:], accT("dt"), headv("ssd_dt_bias").unsqueeze(1).to_broadcast([P, NT, SSD_H]),
                            ALU.add).then_inc(evac_at("dt")[0], 1)
            v.wait_ge(*evac_at("dt"))
            V.scalar_tensor_tensor(out=sp_y[:], in0=logit[:], scalar=-1.0, in1=logit[:], op0=ALU.mult,
                                   op1=ALU.max).then_inc(S["dt_in"], 1)
            v.wait_ge(S["dt_e"], 1)
            softplus_tail(logit[:], sp_y[:], SSD_H)
            V.tensor_copy(dtv[:], sp[:])
            V.scalar_tensor_tensor(out=da[:], in0=sp[:], scalar=-1.0,
                                   in1=ea2[:].unsqueeze(1).to_broadcast([P, NT, SSD_H]),
                                   op0=ALU.mult, op1=ALU.mult).then_inc(S["dt_g"], 1)
            v.wait_ge(S["s_cb"], 1)
            V.tensor_tensor(cbm[:], pm[:, 0, :].rearrange("p (k s) -> p k s", s=P),
                            con("tri").unsqueeze(1).to_broadcast([P, 4, P]), ALU.mult).then_inc(S["s_xd"], 1)
            v.wait_ge(S["s_xsc"], 1)

            def per_head(col, k):
                return col.unsqueeze(col.ndim).to_broadcast(list(col.shape) + [SSD_D])

            def by_head(ap):
                return ap.rearrange("p (h d) -> p h d", d=SSD_D)
            for t in range(NT):
                V.tensor_tensor(by_head(xdt[:, t, :]), by_head(xs[:, t, :]), per_head(dtv[:, t, :], 1), ALU.mult)
                V.tensor_tensor(by_head(yd[:, t, :]), by_head(xs[:, t, :]), per_head(headv("ssd_d"), 1), ALU.mult)
            v.wait_ge(S["s_ac"], 1)
            link(V.tensor_copy(acs[:], pm[:, 1, 0:3 * SSD_H].rearrange("p (k h) -> p k h", k=3)))
            V.tensor_tensor(acs[:, 2, :], acs[:, 2, :], acs[:, 0, :], ALU.subtract).then_inc(S["s_acc"], 1)
            v.wait_ge(S["s_eac"], 1)
            V.tensor_tensor(by_head(xe[:]), by_head(xdt[:, 0, :]), per_head(eac[:, 1, :], 1), ALU.mult)\
                .then_inc(S["s_xe"], 1)
            v.wait_ge(S["s_yo"], 1)
            link(V.tensor_tensor(by_head(xe[:]), by_head(pm[:, 2:4, :].rearrange("p a b -> p (a b)")),
                                 per_head(eac[:, 0, :], 1), ALU.mult))
            V.tensor_tensor(yd[:, 1, :], yd[:, 1, :], xe[:], ALU.add).then_inc(S["s_yod"], 1)
            for b in range(4):
                c, g = b // 2, b % 2
                v.wait_ge(S["b_row"], b + 1)
                if b:
                    v.wait_ge(S["b_y"], b)
                for r in range(8):
                    last = V.scalar_tensor_tensor(out=em[:, r, :], in0=pm[:, r // 4, (r % 4) * P:(r % 4 + 1) * P],
                                                  scalar=acs[:, c, 8 * g + r:8 * g + r + 1], in1=con("strict"),
                                                  op0=ALU.subtract, op1=ALU.mult)
                last.then_inc(S["b_e0"], 1)
                v.wait_ge(S["b_e"], b + 1)
                V.scalar_tensor_tensor(out=em[:], in0=em[:], scalar=1.0,
                                       in1=cbm[:, 2 * c + g, :].unsqueeze(1).to_broadcast([P, 8, P]),
                                       op0=ALU.min, op1=ALU.mult).then_inc(S["b_m"], 1)
                v.wait_ge(S["b_y"], b + 1)
                y = yd[:, c, g * W:(g + 1) * W]
                V.tensor_tensor(y, y, pm[:, 2, :], ALU.add).then_inc(S["b_yd"], 1)
            v.wait_ge(S["b_yd"], 4)
            for c in range(2):
                v.wait_ge(*evac_at(f"mz{c}"))
            V.tensor_tensor(yd[:], yd[:], zz[:], ALU.mult).then_inc(S["y_z"], 1)
            V.memset(scp[:, :, 0:2], 0.0).then_inc(S["c_ready"], 1)
            v.wait_ge(S["y_ss"], 1)
            y4 = yd[:].rearrange("p t (g d) -> p (t g) d", g=2)
            V.tensor_tensor(y4, y4, rs[:, 0:4].unsqueeze(2).to_broadcast([P, 4, W]), ALU.mult).then_inc(S["y_n"], 1)
            turn("y", BYhi[:, 0:8, :], BYlo[:, 0:8, :], lambda f: bcol("ssd_norm_w", f))
            for c in range(2):
                v.wait_ge(S["w_used"], landed(f"sh{c}"))
                v.wait_ge(*evac_at(f"sc{c}"))
                V.tensor_tensor(scp[:, :, 2:2 + TOK], accF(f"sh{c}"), scc[:], ALU.mult)\
                    .then_inc(evac_at(f"sh{c}")[0], 1)
                v.wait_ge(*evac_at(f"sh{c}"))
                for k in range(3):
                    for f in range(4):
                        w = bcol("sc_conv_w", 8 * k + 4 * c + f)
                        if k == 0:
                            last = V.tensor_scalar(scv[:, f, :], scp[:, f, 0:TOK], w, None, ALU.mult)
                        else:
                            last = V.scalar_tensor_tensor(out=scv[:, f, :], in0=scp[:, f, k:k + TOK], scalar=w,
                                                          in1=scv[:, f, :], op0=ALU.mult, op1=ALU.add)
                    link(last)
                v.wait_ge(S["w_used"], landed(f"sb{c}"))
                V.tensor_tensor(scv[:], accF(f"sb{c}"), scv[:], ALU.mult).then_inc(evac_at(f"sb{c}")[0], 1)
                v.wait_ge(*evac_at(f"sb{c}"))
                V.tensor_copy(ss[:, 15:16], rs[:, 15:16]).then_inc(S["c_out"], 1)
                v.wait_ge(S["c_hi"], c + 1)
                V.tensor_tensor(BYlo[:, 8 + 4 * c:12 + 4 * c, :], scv[:],
                                BYhi[:, 8 + 4 * c:12 + 4 * c, :].bitcast(F32), ALU.subtract)\
                    .then_inc(S["c_lo"], 1)

            def residual(name, c):
                v.wait_ge(S["w_used"], landed(name))
                x = X[:, :, c * W:(c + 1) * W]
                V.scalar_tensor_tensor(out=x, in0=x, scalar=ALPHA, in1=accT(name), op0=ALU.mult, op1=ALU.add)\
                    .then_inc(evac_at(name)[0], 1)

            def layer_norm(n, at):
                V.engine_nop().then_inc(S["ln_x"], 1)
                v.wait_ge(S["ln_sum"], n + 1)
                for t in range(NT):
                    last = V.tensor_scalar(xc[:, t, :], X[:, t, :], rs[:, t:t + 1], None, ALU.add)
                last.then_inc(S["ln_xc"], 1)
                v.wait_ge(S["ln_rs"], n + 1)
                v.wait_ge(S["ln_in"], 16 * 5 * (n // 2 + 1))
                for t in range(NT):
                    last = V.scalar_tensor_tensor(out=X[:, t, :], in0=xc[:, t, :], scalar=rs[:, 2 + t:3 + t],
                                                  in1=lnr[:, at, :], op0=ALU.mult, op1=ALU.mult)
                link(last)
                V.tensor_tensor(X[:], X[:], lnr[:, at + 1, :].unsqueeze(1).to_broadcast([P, NT, D]), ALU.add)\
                    .then_inc(S["xn"], 1)

            for c in range(2):
                residual(f"mo{c}", c)
            for c in range(2):
                v.wait_ge(*evac_at(f"mo{c}"))
            layer_norm(0, 0)

            def feed_forward(i):
                turn(("x4", "x7")[i], XThi, XTlo)
                for c in range(-(-DFF2 // W)):
                    k = 6 * i + c
                    nf = chunks[f"fg{i}_{c}"][4] // P
                    v.wait_ge(S["w_used"], landed(f"fu{i}_{c}"))
                    v.wait_ge(*evac_at(f"fg{i}_{c}"))
                    if k:
                        v.wait_ge(S["h_lo"], k)
                    V.tensor_tensor(fh[:, 0:nf, :], accF(f"fu{i}_{c}"), sg[:, 0:nf, :], ALU.mult)\
                        .then_inc(evac_at(f"fu{i}_{c}")[0], 1)
                    v.wait_ge(*evac_at(f"fu{i}_{c}"))
                    V.tensor_copy(ss[:, 15:16], rs[:, 15:16]).then_inc(S["h_x"], 1)
                    v.wait_ge(S["h_hi"], k + 1)
                    V.tensor_tensor(Hlo[:, 4 * c:4 * c + nf, :], fh[:, 0:nf, :],
                                    Hhi[:, 4 * c:4 * c + nf, :].bitcast(F32), ALU.subtract).then_inc(S["h_lo"], 1)
                for c in range(2):
                    residual(f"fd{i}_{c}", c)
                for c in range(2):
                    v.wait_ge(*evac_at(f"fd{i}_{c}"))
                layer_norm(2 * i + 1, 2)
                turn(("x5", "x8")[i], XThi, XTlo)
                for c in range(2):
                    cols = slice(c * W, (c + 1) * W)
                    v.wait_ge(S["w_used"], landed(f"pg{i}_{c}"))
                    V.tensor_tensor(pgt[:], accT(f"pg{i}_{c}"),
                                    lnr[:, 4, cols].unsqueeze(1).to_broadcast([P, NT, W]), ALU.add)\
                        .then_inc(evac_at(f"pg{i}_{c}")[0], 1)
                    v.wait_ge(*evac_at(f"pg{i}_{c}"))
                    V.tensor_copy(ss[:, 15:16], rs[:, 15:16]).then_inc(S["g_x"], 1)
                    v.wait_ge(S["g_s"], 2 * i + c + 1)
                    v.wait_ge(S["w_used"], landed(f"pw{i}_{c}"))
                    V.tensor_tensor(pgt[:], accT(f"pw{i}_{c}"), pgt[:], ALU.mult)\
                        .then_inc(evac_at(f"pw{i}_{c}")[0], 1)
                    v.wait_ge(*evac_at(f"pw{i}_{c}"))
                    last = V.tensor_tensor(X[:, :, cols], X[:, :, cols], pgt[:], ALU.add)
                    if c == 0:
                        link(last)
                last.then_inc(S["x_end"], 1)
            feed_forward(0)

            turn("x6", XThi, XTlo)
            V.tensor_scalar(nsink[:], headv("attn_sinks"), -1.0, None, ALU.mult)
            v.wait_ge(*evac_at("ak"))
            for kv in range(AKV):
                src = akr[64 * (kv % 2):64 * (kv % 2) + 64, kv // 2, :]
                for half in range(2):
                    last = V.tensor_copy(akd[64 * half:64 * half + 64, kv, :], src)
            v.wait_ge(S["w_used"], landed("av"))
            v.wait_ge(S["q_in"], 32)
            V.tensor_tensor(av[:], accT("av"), bv[:].unsqueeze(1).to_broadcast([P, NT, AKV * AD]), ALU.add)\
                .then_inc(evac_at("av")[0], 1)
            wmask = span("causal1", "causal2").unsqueeze(1).to_broadcast([P, 4, 3 * P])
            for kv in range(AKV):
                n = 2 + kv
                v.wait_ge(S["a_sc"], n + 1)
                link(V.scalar_tensor_tensor(out=wS[:], in0=pm[:, :, 0:3 * P], scalar=AD ** -0.5, in1=wmask,
                                            op0=ALU.mult, op1=ALU.add))
                V.tensor_reduce(attn_neg[:, :, 0:1], wS[:, :, 0:P], AX_X, ALU.max, negate=True)
                link(V.tensor_reduce(attn_neg[:, :, 1:2], wS[:, :, P:3 * P], AX_X, ALU.max, negate=True))
                sink = nsink[:, 4 * kv:4 * kv + 4].unsqueeze(2).to_broadcast([P, 4, 2])
                link(V.tensor_tensor(attn_neg[:], attn_neg[:], sink, ALU.min))
                V.tensor_tensor(esink[:], attn_neg[:], sink, ALU.subtract).then_inc(S["a_s"], 1)
                v.wait_ge(S["a_e"], n + 1)
                link(V.tensor_tensor(attn_sum[:], attn_sum[:], esink[:], ALU.add))
                link(V.reciprocal(attn_inv[:], attn_sum[:]))
                V.tensor_tensor(wS[:, :, 0:P], wS[:, :, 0:P], attn_inv[:, :, 0:1].to_broadcast([P, 4, P]), ALU.mult)
                V.tensor_tensor(wS[:, :, P:3 * P], wS[:, :, P:3 * P],
                                attn_inv[:, :, 1:2].to_broadcast([P, 4, 2 * P]), ALU.mult).then_inc(S["a_p"], 1)
                v.wait_ge(S["a_hi"], n + 1)
                V.tensor_tensor(ATlo[:, 2 * kv:2 * kv + 2, :].rearrange("p a b -> p (a b)"), pm[:, 0, :],
                                AThi[:, 2 * kv:2 * kv + 2, :].rearrange("p a b -> p (a b)").bitcast(F32),
                                ALU.subtract).then_inc(S["a_lo"], 1)
            for c in range(2):
                residual(f"ao{c}", c)
            for c in range(2):
                v.wait_ge(*evac_at(f"ao{c}"))
            link(V.tensor_tensor(X[:], X[:], bo[:].unsqueeze(1).to_broadcast([P, NT, D]), ALU.add))
            layer_norm(2, 0)
            turn("p1", PThi, PTlo)
            feed_forward(1)
            v.wait_ge(S["x_end"], 2)
            V.engine_nop().then_inc(S["fin"], 1)

        @block.tensor
        def _(pe):
            T = nc.tensor

            def turn(name, src, identity=None):
                g0, n, nf = turns[name]
                for g in range(n):
                    if g0 + g >= 4:
                        pe.wait_ge(S["t_lo"], g0 + g - 3)
                    for f in range(min(2, nf - 2 * g)):
                        for t in range(NT):
                            k = 2 * g + f
                            last = T.transpose(pm[:, (g0 + g) % 4, f * TOK + t * P:f * TOK + (t + 1) * P],
                                               src[:, t, k * P:(k + 1) * P], ident)
                    last.then_inc(S["t_pe"], 1)

            def turned(name):
                pe.wait_ge(S["t_lo"], turns[name][0] + turns[name][1])

            def product(name, hi, lo):
                n, first, end, kt, width, mode = chunks[name]
                if n >= 2:
                    pe.wait_ge(evac[n % 2], n // 2)
                k = 0
                for u in range(first, end):
                    pe.wait_ge(S["w_lo"], u + 1)
                    nk = units[u][2]
                    s = u % SPLIT
                    for i in range(nk):
                        wh, wl = whi[:, s, i, 0:width], wlo[:, s, i, 0:width]
                        done = k == kt - 1
                        if mode == "T":
                            for t in range(NT):
                                tok = slice(t * P, (t + 1) * P)
                                o = acc[:, n % 2, t, 0:width]
                                T.matmul(o, hi[:, k, tok], wh, start=k == 0, stop=False)
                                T.matmul(o, hi[:, k, tok], wl, start=False, stop=False)
                                last = T.matmul(o, lo[:, k, tok], wh, start=False, stop=done)
                        else:
                            for f in range(width // P):
                                o = acc[:, n % 2, f // 2, (f % 2) * TOK:(f % 2 + 1) * TOK]
                                fs = slice(f * P, (f + 1) * P)
                                T.matmul(o, wh[:, fs], hi[:, k, :], start=k == 0 and f % 2 == 0, stop=False,
                                         skip_group_check=True)
                                T.matmul(o, wh[:, fs], lo[:, k, :], start=False, stop=False, skip_group_check=True)
                                last = T.matmul(o, wl[:, fs], hi[:, k, :], start=False, stop=done,
                                                skip_group_check=True)
                        k += 1
                    last.then_inc(S["w_used"], 1)

            def mm(o, lhs, rhs, start=True, stop=True, **k):
                return T.matmul(o, lhs, rhs, start=start, stop=stop, **k)

            def flat(i, n=P):
                return pm[:, i // BANK, i % BANK:i % BANK + n]

            pe.wait_ge(S["x_in"], 32)
            pe.wait_ge(S["c_in"], 16 * (len(ROWS_A) + len(ROWS_B) + len(HEADS) + 1))
            T.transpose(pm[:, 0, 0:n_a], rowsA[0:n_a, :], ident[0:n_a, 0:n_a])
            T.transpose(pm[:, 0, P:P + n_b], rowsB[0:n_b, :], ident[0:n_b, 0:n_b]).then_inc(S["cols"], 1)
            pe.wait_ge(S["cols"], 2)
            pe.wait_ge(S["xn"], 1)
            turn("x1", XN1)
            turned("x1")
            for name in ("dq", "dk", "dv", "z", "abc", "ff", "fq", "fk", "fv", "sv", "su"):
                product(name, XThi, XTlo)

            pe.wait_ge(S["dn_sq"], 1)
            for i in range(4):
                last = mm(pm[:, i, :], ones, d_sq[:, i * BANK:(i + 1) * BANK])
            last.then_inc(S["dn_l2"], 1)
            pe.wait_ge(S["dn_rn"], 1)
            pe.wait_ge(S["dn_g"], 1)
            for t in range(NT):
                mm(pm[:, 0, 4 * t:4 * t + 4], con("tri64"), dng[:, t, :])
                last = mm(pm[:, 0, 8 + 4 * t:12 + 4 * t], con("blk64"), dng[:, t, :])
            last.then_inc(S["dn_gc"], 1)
            pe.wait_ge(S["dn_gcs"], 1)
            for h in range(4):
                for t in range(NT):
                    i = (h * NT + t) * P
                    mm(flat(i), dng[:, t, h:h + 1].to_broadcast([P, P]), con("tri64"))
                    last = mm(flat(2 * BANK + i), beta[:, t, h:h + 1].to_broadcast([P, P]), ident)
            last.then_inc(S["dn_rows"], 1)
            pe.wait_ge(S["dn_qkn"], 1)
            pe.wait_ge(S["dn_e0"], 1)
            pe.wait_ge(S["dn_egr"], 1)
            for h in range(4):
                for t in range(NT):
                    i = (h * NT + t) * P
                    mm(flat(i), kT[:, i:i + P], kT[:, i:i + P])
                    last = mm(flat(2 * BANK + i), kT[:, i:i + P], qT[:, i:i + P])
            last.then_inc(S["dn_kk"], 1)
            pe.wait_ge(S["dn_lt"], 1)
            for i in range(0, 1024, P):
                T.transpose(flat(i), kT[:, i:i + P], ident)
                last = T.transpose(flat(2 * BANK + i), d_v[:, i:i + P], ident)
            last.then_inc(S["dn_kv"], 1)
            pe.wait_ge(S["dn_vb"], 1)
            for s in range(6):
                for hf in range(2):
                    pe.wait_ge(S["dn_ml"], 2 * s + hf + 1)
                    for j in range(4):
                        i = hf * W + j * P
                        last = mm(pm[:, 2 * hf, j * P:(j + 1) * P], d_ml[:, i:i + P], d_x[:, i:i + P])
                    last.then_inc(S["dn_t1"], 1)
                for hf in range(2):
                    pe.wait_ge(S["dn_t1c"], 2 * s + hf + 1)
                    for j in range(4):
                        i = hf * W + j * P
                        mm(pm[:, 2 * hf + 1, j * P:(j + 1) * P], d_y[:, i:i + P], d_t1[:, i:i + P])
                        last = mm(pm[:, 2 * hf, j * P:(j + 1) * P], d_t1[:, i:i + P], d_y[:, i:i + P])
                    last.then_inc(S["dn_pq"], 1)
            pe.wait_ge(S["dn_y"], 3)
            for i in range(0, 1024, P):
                mm(flat(i), d_y[:, i:i + P], d_vb[:, i:i + P])
                last = mm(flat(2 * BANK + i), d_kbe[:, i:i + P], d_y[:, i:i + P])
            last.then_inc(S["dn_uw"], 1)
            for n in range(4):
                t, r = n // 2, 64 * (n % 2)
                rows = slice(r, r + 64)

                def tile(h):
                    return (h * NT + t) * P
                o_bank = pm[rows, 1 + t, :]
                if n:
                    pe.wait_ge(S["sc_s"], n)
                    for h in range(4):
                        last = mm(pm[rows, 0, h * P:(h + 1) * P], d_w[:, tile(h) + r:tile(h) + r + 64],
                                  d_s[:, h * P:(h + 1) * P])
                    last.then_inc(S["sc_ws"], 1)
                    for h in range(4):
                        mm(o_bank[:, h * P:(h + 1) * P], qT[:, tile(h) + r:tile(h) + r + 64],
                           d_s[:, h * P:(h + 1) * P], start=h == 0, stop=False, skip_group_check=True)
                pe.wait_ge(S["sc_vn"], n + 1)
                for h in range(4):
                    i = tile(h)
                    last = mm(o_bank[:, h * P:(h + 1) * P], d_at[rows, i + r:i + r + 64], d_vn[rows, i:i + P],
                              start=n == 0 and h == 0, stop=True, skip_group_check=True)
                    if n < 3:
                        last = mm(pm[:, 3, h * P:(h + 1) * P], d_kdec[rows, i:i + P], d_vn[rows, i:i + P])
                last.then_inc(S["sc_su"], 1)
            pe.wait_ge(S["dn_o"], 1)
            turn("oa", d_o.rearrange("p (t d) -> p t d", t=NT))

            pe.wait_ge(S["m_cn2"], 1)
            turn("cqkv", cn)
            turned("cqkv")
            for j in range(2):
                product(f"uq{j}", MQhi[:, 0:2], MQlo[:, 0:2])
            for j in range(2):
                product(f"ukv{j}", MQhi[:, 2:3], MQlo[:, 2:3])
            pe.wait_ge(S["m_rope"], 2)
            for i in range(2):
                for h in range(4):
                    for t in range(NT):
                        last = T.transpose(flat((i * 4 + h) * TOK + t * P), mq[:, i, t, h, 0:NOPE], ident)
            last.then_inc(S["m_tn"], 1)
            pe.wait_ge(S["m_tnc"], 1)
            for i in range(2):
                for h in range(4):
                    for t in range(NT):
                        last = T.transpose(flat((i * 4 + h) * TOK + t * P)[0:ROPE], mq[:, i, t, h, NOPE:QK], ident)
            last.then_inc(S["m_tr"], 1)
            pe.wait_ge(S["m_trc"], 1)
            for h in range(4):
                for t in range(NT):
                    o = pm[:, h, P * t:P * t + P * (t + 1)]
                    n = P * (t + 1)
                    mm(o, mT[:, h, t * P:(t + 1) * P], mT[:, 4 + h, 0:n], stop=False)
                    last = mm(o, mR[:, h, t * P:(t + 1) * P], mR[:, 4 + h, 0:n], start=False)
            last.then_inc(S["a_sc"], 1)

            def attention(n, s, pt, vals):
                pe.wait_ge(S["a_p"], n + 1)
                for h in range(4):
                    for j in range(3):
                        last = T.transpose(pm[:, h, j * P:(j + 1) * P], s[:, h, j * P:(j + 1) * P], ident)
                last.then_inc(S["a_pt"], 1)
                pe.wait_ge(S["a_ptc"], n + 1)
                for h in range(4):
                    o = pm[:, h // 2, (h % 2) * TOK:(h % 2 + 1) * TOK]
                    mm(o, vals(0, h), pt[:, h, 0:2 * P], stop=False)
                    last = mm(o[:, P:TOK], vals(1, h), pt[:, h, 2 * P:3 * P], start=False)
                last.then_inc(S["a_o"], 1)

            mS = mq[:, 0].rearrange("p t h d -> p (t h d)").rearrange("p (h s) -> p h s", h=4)
            mP = mq[:, 1].rearrange("p t h d -> p (t h d)").rearrange("p (h s) -> p h s", h=4)
            attention(0, mS, mP, lambda t, h: mv[:, t, h * P:(h + 1) * P])

            pe.wait_ge(S["a_lo"], 1)
            mm(pm[:, 0, 0:4], con("tri"), nlf[:, 0, :])
            mm(pm[:, 0, 4:8], ones, nlf[:, 0, :], stop=False)
            mm(pm[:, 0, 4:8], con("tri"), nlf[:, 1, :], start=False).then_inc(S["f_cum"], 1)
            for h in range(4):
                row = pm[:, 1 + h // 2, (h % 2) * TOK:(h % 2 + 1) * TOK]
                mm(row, nlf[:, 0, h:h + 1].to_broadcast([P, P]), span("tri", "ones"), stop=False)
                last = mm(row[:, P:TOK], nlf[:, 1, h:h + 1].to_broadcast([P, P]), con("tri"), start=False)
            last.then_inc(S["f_cum"], 1)
            pe.wait_ge(S["f_xn"], 1)
            pe.wait_ge(S["f_d"], 1)
            for k in range(8):
                for t in range(NT):
                    last = T.transpose(flat(k * TOK + t * P), fx[:, t, k * P:(k + 1) * P], ident)
            last.then_inc(S["f_t"], 1)
            pe.wait_ge(S["f_tc"], 1)
            for h in range(4):
                for t in range(NT):
                    n = P * (t + 1)
                    last = mm(pm[:, h, P * t:P * t + n], fT[:, h, t * P:(t + 1) * P], fT[:, 4 + h, 0:n])
            last.then_inc(S["a_sc"], 1)
            attention(1, fS, fPT, lambda t, h: fx[:, t, 2 * W + h * P:2 * W + (h + 1) * P])

            pe.wait_ge(S["s_w"], 48)
            for g in range(4):
                last = T.transpose(pm[:, 3, g * P:(g + 1) * P], sw[:, g, :], ident)
            last.then_inc(S["s_wt"], 1)
            pe.wait_ge(S["s_v"], 1)
            for g in range(4):
                for n in range(NT):
                    last = mm(pm[:, g // 2, (g % 2) * TOK + n * P:(g % 2) * TOK + (n + 1) * P],
                              sgv[:, n, g * P:(g + 1) * P], swT[:, g, :])
            last.then_inc(S["s_mx"], 1)
            pe.wait_ge(S["s_lo"], 1)
            for c in range(2):
                for i in range(4):
                    b = 4 * i
                    product(f"gate{i}_{c}", XThi, XTlo)
                    product(f"br{i}_{c}", BRhi[:, b:b + 4], BRlo[:, b:b + 4])
            pe.wait_ge(S["g_done"], 1)
            turn("merged", merged)
            turned("merged")
            for c in range(2):
                product(f"wo{c}", XThi, XTlo)
            pe.wait_ge(S["xn"], 2)
            turn("x2", XN)
            turned("x2")
            for c in range(DFF // W):
                product(f"f1_{c}", XThi, XTlo)
            pe.wait_ge(S["f1_lo"], DFF // W)
            for c in range(2):
                product(f"f2_{c}", FFhi, FFlo)

            for c in range(2):
                pe.wait_ge(*evac_at(f"f2_{c}"))
            turn("x3", X)
            pe.wait_ge(S["p_in"], 16)
            turn("p0", pin)
            turned("p0")
            for name in ("xbc0", "xbc1", "xbc2", "dt", "mz0", "mz1"):
                product(name, XThi, XTlo)
            pe.wait_ge(S["silu2"], 3)
            for c in range(2):
                for g in range(2):
                    k = 2 * c + g
                    last = mm(pm[:, 0, k * P:(k + 1) * P], xbcT[:, 8 + g, c * P:(c + 1) * P],
                              xbcT[:, 10 + g, c * P:(c + 1) * P])
            last.then_inc(S["s_cb"], 1)
            pe.wait_ge(S["s_xd"], 1)
            for t in range(NT):
                for f in range(8):
                    last = T.transpose(flat(t * D + f * P), xbcT[:, f, t * P:(t + 1) * P], ident)
            last.then_inc(S["s_xs"], 1)
            pe.wait_ge(S["s_xsc"], 1)
            for g in range(2):
                last = T.transpose(pm[:, 0, g * P:(g + 1) * P], xbcT[:, 8 + g, 0:P], ident)
            last.then_inc(S["s_bt"], 1)
            pe.wait_ge(S["dt_g"], 1)
            for c in range(2):
                mm(pm[:, 1, c * SSD_H:(c + 1) * SSD_H], con("tri"), da[:, c, :])
            mm(pm[:, 1, 2 * SSD_H:3 * SSD_H], ones, da[:, 0, :]).then_inc(S["s_ac"], 1)
            pe.wait_ge(S["s_btc"], 1)
            pe.wait_ge(S["s_xe"], 1)
            for g in range(2):
                last = mm(pm[:, 2 + g, :], bmt[:, g * P:(g + 1) * P], xe[:, g * W:(g + 1) * W])
            last.then_inc(S["s_st"], 1)
            pe.wait_ge(S["s_stc"], 1)
            for g in range(2):
                last = mm(pm[:, 2 + g, :], xbcT[:, 10 + g, P:2 * P], hst[:, g * W:(g + 1) * W])
            last.then_inc(S["s_yo"], 1)
            pe.wait_ge(S["s_yod"], 1)

            def rows(b):
                c, g = b // 2, b % 2
                if b:
                    pe.wait_ge(S["b_e0"], b)
                for r in range(8):
                    h = 8 * g + r
                    last = mm(flat(r * P), da[:, c, h:h + 1].to_broadcast([P, P]), con("tri"))
                last.then_inc(S["b_row"], 1)
            rows(0)
            for b in range(4):
                c, g = b // 2, b % 2
                if b < 3:
                    rows(b + 1)
                pe.wait_ge(S["b_m"], b + 1)
                if b:
                    pe.wait_ge(S["b_yd"], b)
                for r in range(8):
                    at = (8 * g + r) * SSD_D
                    last = mm(pm[:, 2, r * SSD_D:(r + 1) * SSD_D], em[:, r, :], xdt[:, c, at:at + SSD_D])
                last.then_inc(S["b_y"], 1)
            pe.wait_ge(S["y_n"], 1)
            turn("y", yd)
            for c in range(2):
                for name in ("sc", "sh", "sb"):
                    product(f"{name}{c}", XThi, XTlo)
            turned("y")
            pe.wait_ge(S["c_lo"], 2)
            for c in range(2):
                product(f"mo{c}", BYhi, BYlo)

            xn = [3]

            def feed_forward(i):
                pe.wait_ge(S["xn"], xn[0])
                turn(("x4", "x7")[i], X)
                turned(("x4", "x7")[i])
                n = -(-DFF2 // W)
                for c in range(n):
                    product(f"fg{i}_{c}", XThi, XTlo)
                    product(f"fu{i}_{c}", XThi, XTlo)
                pe.wait_ge(S["h_lo"], n * (i + 1))
                for c in range(2):
                    product(f"fd{i}_{c}", Hhi, Hlo)
                pe.wait_ge(S["xn"], xn[0] + 1)
                xn[0] += 2
                turn(("x5", "x8")[i], X)
                turned(("x5", "x8")[i])
                for c in range(2):
                    product(f"pg{i}_{c}", XThi, XTlo)
                    product(f"pw{i}_{c}", PThi, PTlo)
            feed_forward(0)

            pe.wait_ge(S["x_end"], 1)
            turn("x6", X)
            turned("x6")
            for name in ("aq0", "aq1", "ak", "av"):
                product(name, XThi, XTlo)
            for kv in range(AKV):
                if kv == 0:
                    pe.wait_ge(*evac_at("aq1"))
                    pe.wait_ge(*evac_at("av"))
                else:
                    pe.wait_ge(S["a_lo"], 2 + kv)
                for j in range(4):
                    h = 4 * kv + j
                    r = slice(64 * (h % 2), 64 * (h % 2) + 64)
                    mm(pm[:, j, 0:P], aqT[r, h // 2, 0:P], akd[r, kv, 0:P])
                    last = mm(pm[:, j, P:3 * P], aqT[r, h // 2, P:TOK], akd[r, kv, :])
                last.then_inc(S["a_sc"], 1)
                pe.wait_ge(S["a_p"], kv + 3)
                for h in range(4):
                    for j in range(3):
                        last = T.transpose(pm[:, h, j * P:(j + 1) * P], wS[:, h, j * P:(j + 1) * P], ident)
                last.then_inc(S["a_pt"], 1)
                pe.wait_ge(S["a_ptc"], kv + 3)
                for j in range(4):
                    r = slice(64 * (j % 2), 64 * (j % 2) + 64)
                    o = pm[r, 0, (j // 2) * TOK:(j // 2 + 1) * TOK]
                    mm(o, av[:, 0, kv * AD:(kv + 1) * AD], wPT[:, j, 0:2 * P], stop=False)
                    last = mm(o[:, P:TOK], av[:, 1, kv * AD:(kv + 1) * AD], wPT[:, j, 2 * P:3 * P], start=False)
                last.then_inc(S["a_o"], 1)
            pe.wait_ge(S["a_lo"], 6)
            for c in range(2):
                product(f"ao{c}", AThi, ATlo)
            pe.wait_ge(S["xn"], 5)
            pe.wait_ge(S["p_in"], 32)
            turn("p1", pin1)
            feed_forward(1)


def kernel(**inputs):
    import concourse.bacc as bacc
    from concourse.bass_utils import run_bass_kernel_spmd

    def flat(name, *shape):
        return np.ascontiguousarray(inputs[name]).reshape(shape)

    arrays = {"x": flat("x", TOK, D), "consts": CONST_ARRAY, "w_in": flat("w_in", D, -1)}
    arrays["positions"] = np.ascontiguousarray(flat("positions", NT, P).T)
    for name in ("mla_w_uq", "mla_w_ukv", "w_out", "w_ff1", "w_ff2"):
        arrays[name] = np.ascontiguousarray(inputs[name])[0]
    for i in range(4):
        arrays[f"w_branch{i}"] = np.ascontiguousarray(inputs["w_branch"])[0, i]
    for i in range(2):
        for name, old in (("w_gate", "w_ffn_gate_2"), ("w_up", "w_ffn_up_2"), ("w_down", "w_ffn_down_2"),
                          ("w_ple", "w_ple_2"), ("w_pgate", "w_ple_gate_2")):
            arrays[f"{name}{i}"] = np.ascontiguousarray(inputs[old])[i]
        arrays[f"p{i}"] = np.ascontiguousarray(inputs["p_2"])[i, 0]
    for name, old in (("w_in_mix", "w_in_mix_2"), ("w_out_mix", "w_out_mix_2"), ("w_qkv", "w_qkv_2"),
                      ("w_o", "w_o_2")):
        arrays[name] = np.ascontiguousarray(inputs[old])[0]
    for name, _ in ROWS_A:
        arrays[name] = flat(name, -1, P)
    for name in ("ssd_conv_w", "ssd_conv_b", "sc_conv_w", "ssd_norm_w"):
        arrays[name] = flat(name + "_2", -1, P)
    arrays["b_qk"] = np.ascontiguousarray(flat("b_qkv_2", -1)[0:10 * P]).reshape(10, P)
    arrays["b_v"] = np.ascontiguousarray(flat("b_qkv_2", -1)[10 * P:])
    for name, _ in HEADS:
        arrays[name] = flat(name if name[0] in "df" else name + "_2", -1)
    for name in ("dn_out_norm_g", "mla_qk_q_g", "mla_qk_k_g", "sg_v_norm_g", "sg_b_s"):
        arrays[name] = flat(name, -1)
    arrays["sg_w_s"] = np.ascontiguousarray(inputs["sg_w_s"])[0]
    arrays["b_o"] = flat("b_o_2", -1)
    for i in range(2):
        for name in ("ln_mix_g", "ln_mix_b", "ln_ffn_g", "ln_ffn_b", "b_ple_gate"):
            arrays[f"{name}{i}"] = np.ascontiguousarray(inputs[name + "_2"])[i]

    nc = bacc.Bacc("TRN2", target_bir_lowering=False, num_devices=1)
    a = {n: nc.dram_tensor(f"in_{n}", v.shape, mybir.dt.from_np(v.dtype), kind="ExternalInput").ap()
         for n, v in arrays.items()}
    out = nc.dram_tensor("out_x", (TOK, D), F32, kind="ExternalOutput").ap()
    build(nc, a, out)
    r = run_bass_kernel_spmd(nc, [{f"in_{n}": v for n, v in arrays.items()}], core_ids=[0])
    return r.results[0]["out_x"].reshape(1, TOK, D)
```

```python
from contextlib import ExitStack

import numpy as np

import concourse.bass as bass
from concourse import mybir

F32 = mybir.dt.float32
F32R = mybir.dt.float32r
I32 = mybir.dt.int32
ACT = mybir.ActivationFunctionType
ALU = mybir.AluOpType
AX_X = mybir.AxisListType.X

P = 128
TOK = 256
NT = TOK // P
D = 1024
KD = D // P
BANK = 512
NEG = -1.0e30

DN_H = 4
DH = 128
W = 512
MLA_QR, MLA_KVR, NOPE, ROPE = 256, 128, 128, 64
QK = NOPE + ROPE
DFF = 4096
IN_SIZES = (3 * W, W, DN_H, DN_H, MLA_QR, MLA_KVR, ROPE, W, W, 3 * W, DN_H, 4 * D)
(O_DN, O_Z, O_A, O_B, O_CQ, O_CKV, O_KR, O_SU, O_SV, O_FOX, O_FF, O_GATE) = (
    [sum(IN_SIZES[:i]) for i in range(len(IN_SIZES))])
ABC = O_SU - O_A
SSD_H, SSD_D, SSD_N, SSD_G = 16, 64, 128, 2
XBC = SSD_H * SSD_D + 2 * SSD_G * SSD_N
DFF2 = ((8 * D + 3 * 256 - 1) // (3 * 256)) * 256
KF2 = DFF2 // P
PLE = 256
AH, AKV, AD = 16, 4, 64
M_XBC, M_DT, M_B = D, D + XBC, D + XBC + SSD_H
M_C, M_H = M_B + D, M_B + 2 * D
ALPHA = 4 ** 0.25

UK = 2
RAW = 5
SPLIT = 4
AHEAD = SPLIT - 1


def gemm_plan():
    g = []
    for j, n in enumerate(("dq", "dk", "dv")):
        g.append((n, "w_in", KD, O_DN + j * W, W, "F"))
    g.append(("abc", "w_in", KD, O_A, ABC, "T"))
    g.append(("ff", "w_in", KD, O_FF, DN_H, "T"))
    g.append(("z", "w_in", KD, O_Z, W, "T"))
    for j, n in enumerate(("fq", "fk", "fv")):
        g.append((n, "w_in", KD, O_FOX + j * W, W, "T"))
    g.append(("sv", "w_in", KD, O_SV, W, "T"))
    g.append(("su", "w_in", KD, O_SU, W, "F"))

    def gates(i):
        for c in range(2):
            g.append((f"gate{i}_{c}", "w_in", KD, O_GATE + i * D + c * W, W, "T"))

    def branch(i):
        for c in range(2):
            g.append((f"br{i}_{c}", f"w_branch{i}", 4, c * W, W, "T"))
    gates(0)
    branch(0)
    for j in range(2):
        g.append((f"uq{j}", "mla_w_uq", 2, j * 2 * QK, 2 * QK, "T"))
    for j in range(2):
        g.append((f"ukv{j}", "mla_w_ukv", 1, j * W, W, "T"))
    gates(1)
    branch(1)
    gates(3)
    branch(3)
    gates(2)
    branch(2)
    for c in range(2):
        g.append((f"wo{c}", "w_out", KD, c * W, W, "T"))
    for c in range(DFF // W):
        g.append((f"f1_{c}", "w_ff1", KD, c * W, W, "F"))
    for c in range(2):
        g.append((f"f2_{c}", "w_ff2", DFF // P, c * W, W, "T"))
    for c in range(3):
        g.append((f"xbc{c}", "w_in_mix", KD, M_XBC + c * W, W, "F"))
    g.append(("dt", "w_in_mix", KD, M_DT, SSD_H, "T"))
    for c in range(2):
        g.append((f"mz{c}", "w_in_mix", KD, c * W, W, "T"))
    for c in range(2):
        for n, o in (("sc", M_C), ("sh", M_H), ("sb", M_B)):
            g.append((f"{n}{c}", "w_in_mix", KD, o + c * W, W, "F"))
    for c in range(2):
        g.append((f"mo{c}", "w_out_mix", 2 * KD, c * W, W, "T"))
    for i in range(2):
        if i == 1:
            for c in range(2):
                g.append((f"aq{c}", "w_qkv", KD, c * W, W, "F"))
            g.append(("ak", "w_qkv", KD, D, AKV * AD, "F"))
            g.append(("av", "w_qkv", KD, D + AKV * AD, AKV * AD, "T"))
            for c in range(2):
                g.append((f"ao{c}", "w_o", KD, c * W, W, "T"))
        for c in range(-(-DFF2 // W)):
            w = min(W, DFF2 - c * W)
            g.append((f"fg{i}_{c}", f"w_gate{i}", KD, c * W, w, "F"))
            g.append((f"fu{i}_{c}", f"w_up{i}", KD, c * W, w, "F"))
        for c in range(2):
            g.append((f"fd{i}_{c}", f"w_down{i}", KF2, c * W, W, "T"))
        for c in range(2):
            g.append((f"pw{i}_{c}", f"w_ple{i}", 2, c * W, W, "T"))
        for c in range(2):
            g.append((f"pg{i}_{c}", f"w_pgate{i}", KD, c * W, W, "T"))
    chunks, units = {}, []
    for n, (name, w, kt, c0, width, mode) in enumerate(g):
        first = len(units)
        for k in range(0, kt, UK):
            units.append((w, k, min(UK, kt - k), c0, width))
        chunks[name] = (n, first, len(units), kt, width, mode)
    return chunks, units


TURNS = (("x1", KD), ("oa", 4), ("cqkv", 3), ("merged", KD), ("x2", KD), ("x3", KD), ("p0", 2), ("y", KD),
         ("x4", KD), ("x5", KD), ("x6", KD), ("p1", 2), ("x7", KD), ("x8", KD))


def turn_plan():
    plan, at = {}, 0
    for name, nf in TURNS:
        n = -(-nf // 2)
        plan[name] = (at, n, nf)
        at += n
    return plan


CONST = {}


def const_table():
    i = np.arange(P)
    same = (i[:, None] // 64) == (i[None, :] // 64)
    parts = {
        "eps6": np.full((P, 1), 1e-6),
        "eps5": np.full((P, 1), 1e-5),
        "ident": np.eye(P),
        "tri64": (i[:, None] <= i[None, :]) & same, "strict64": (i[:, None] < i[None, :]) & same,
        "blk64": same, "tri": i[:, None] <= i[None, :], "ones": np.ones((P, P)),
        "strict": i[:, None] < i[None, :],
        "causal0": np.where(i[None, :] <= i[:, None], 0.0, NEG),
        "open": np.zeros((P, P)),
        "causal1": np.where(i[None, :] <= i[:, None], 0.0, NEG),
        "prev": np.where(i[None, :] > i[:, None], 0.0, NEG),
        "causal2": np.where(i[None, :] <= i[:, None], 0.0, NEG),
    }
    for s in range(6):
        h = 1 << s
        parts[f"lvl{s}"] = ((i[:, None] // (2 * h) == i[None, :] // (2 * h))
                            & ((i[:, None] // h) % 2 == 0) & ((i[None, :] // h) % 2 == 1))
    parts["freq"] = np.broadcast_to(
        (np.float32(10000.0) ** (-np.arange(0, ROPE, 2, dtype=np.float32) / ROPE))[None], (P, ROPE // 2))
    at, cols = 0, []
    for n, a in parts.items():
        CONST[n] = (at, a.shape[1])
        at += a.shape[1]
        cols.append(np.asarray(a, np.float32))
    return np.ascontiguousarray(np.concatenate(cols, axis=1))


CONST_ARRAY = const_table()
HEAD_COLS = CONST["ident"][0] + P

ROWS_A = (("norm1_g", 8), ("mla_q_norm_g", 2), ("mla_kv_norm_g", 1), ("fox_q_norm_g", 1), ("fox_k_norm_g", 1),
          ("dn_conv_w", 48), ("norm2_g", 8))
ROWS_B = (("ssd_conv_w", 48), ("ssd_conv_b", 12), ("sc_conv_w", 24), ("ssd_norm_w", 8), ("b_qk", 10))
HEADS = (("dn_dt_bias", 4), ("dn_a_log", 4), ("fox_f_bias", 4), ("ssd_dt_bias", 16), ("ssd_a_log", 16),
         ("ssd_d", 16), ("attn_sinks", 16))


def starts(table):
    out, at = {}, 0
    for n, k in table:
        out[n] = at
        at += k
    return out, at


def build(nc, a, out):
    chunks, units = gemm_plan()
    turns = turn_plan()
    rows_a, n_a = starts(ROWS_A)
    rows_b, n_b = starts(ROWS_B)
    head_at, n_heads = starts(HEADS)
    C = CONST

    ctx = ExitStack()
    with ctx:
        def sb(name, shape, dt=F32, where=None):
            return (where or ctx).enter_context(nc.sbuf_tensor(name, shape, dt))

        def sem(name):
            return ctx.enter_context(nc.semaphore(name))

        raw = sb("raw", [P, RAW, UK, BANK])
        whi = sb("whi", [P, SPLIT, UK, BANK], F32R)
        wlo = sb("wlo", [P, SPLIT, UK, BANK], F32R)
        X = sb("X", [P, NT, D])
        XThi = sb("XThi", [P, KD, TOK], F32R)
        XTlo = sb("XTlo", [P, KD, TOK], F32R)
        ct = sb("ct", [P, CONST_ARRAY.shape[1]])
        rowsA = sb("rowsA", [P, P])
        rowsB = sb("rowsB", [P, P])
        colA = sb("colA", [P, n_a])
        colB = sb("colB", [P, n_b])
        heads = sb("heads", [P, n_heads])
        ss = sb("ss", [P, 16])
        rs = sb("rs", [P, 16])
        logit = sb("logit", [P, NT, 16])
        sp_y = sb("sp_y", [P, NT, 16])
        sp_z = sb("sp_z", [P, NT, 16])
        sp_z2 = sb("sp_z2", [P, NT, 16])
        sp_p = sb("sp_p", [P, NT, 16])
        sp = sb("sp", [P, NT, 16])

        def con(name):
            at, n = C[name]
            return ct[:, at:at + n]

        ident = con("ident")
        ones = con("ones")
        eps6, eps5 = con("eps6"), con("eps5")

        def span(first, last):
            return ct[:, C[first][0]:C[last][0] + C[last][1]]

        def headv(name):
            at = head_at[name]
            return heads[:, at:at + dict(HEADS)[name]]

        def acol(name, j=0):
            return colA[:, rows_a[name] + j:rows_a[name] + j + 1]

        def bcol(name, j=0):
            return colB[:, rows_b[name] + j:rows_b[name] + j + 1]

        attn_neg2 = sb("attn_neg2", [P, 2, 4, 2])
        attn_neg = attn_neg2[:, 0]
        attn_sum2 = sb("attn_sum2", [P, 2, 4, 2])
        attn_sum = attn_sum2[:, 0]
        attn_inv2 = sb("attn_inv2", [P, 2, 4, 2])
        attn_inv = attn_inv2[:, 0]

        m1 = ExitStack()
        BRhi = sb("BRhi", [P, 8, TOK], F32R, m1)
        BRlo = sb("BRlo", [P, 8, TOK], F32R, m1)
        zs = sb("zs", [P, NT, W], where=m1)
        abc = sb("abc", [P, NT, ABC], where=m1)
        ffl = sb("ffl", [P, NT, 4], where=m1)
        fx = sb("fx", [P, NT, 3 * W], where=m1)
        sgv = sb("sgv", [P, NT, W], where=m1)
        sgu = sb("sgu", [P, 4, TOK], where=m1)
        beta = sb("beta", [P, NT, 4], where=m1)
        dng = sb("dng", [P, NT, 4], where=m1)
        nlf = sb("nlf", [P, NT, 4], where=m1)
        ea = sb("ea", [P, 4], where=m1)
        gcs = sb("gcs", [P, 4, 4], where=m1)
        gex = sb("gex", [P, 3, NT, 4], where=m1)
        o_g = sb("o_g", [P, P], where=m1)
        gt = sb("gt", [P, 2, NT, W], where=m1)
        merged = sb("merged", [P, NT, D], where=m1)
        gp = zs
        m1a = ExitStack()
        dn = sb("dn", [P, 14, 1024], where=m1a)
        m1a.close()
        m1b = ExitStack()
        mq = sb("mq", [P, 2, NT, 4, QK], where=m1b)
        mv = sb("mv", [P, NT, W], where=m1b)
        msq = sb("msq", [P, NT * 4 * QK], where=m1b)
        mT = sb("mT", [P, 8, TOK], where=m1b)
        mR = sb("mR", [ROPE, 8, TOK], where=m1b)
        m_g = sb("m_g", [P, 2, QK], where=m1b)
        cs = sb("cs", [P, 2, NT, ROPE // 2], where=m1b)
        ang = sb("ang", [P, 3, NT, ROPE // 2], where=m1b)
        posi = sb("posi", [P, NT], I32, m1b)
        posf = sb("posf", [P, NT], where=m1b)
        rt = sb("rt", [P, 4, NT, 4, ROPE // 2], where=m1b)
        cn = sb("cn", [P, NT, 3 * P], where=m1b)
        MQhi = sb("MQhi", [P, 3, TOK], F32R, m1b)
        MQlo = sb("MQlo", [P, 3, TOK], F32R, m1b)
        m1b.close()
        m1c = ExitStack()
        fsq = sb("fsq", [P, NT, D], where=m1c)
        fT = sb("fT", [P, 8, TOK], where=m1c)
        fD = sb("fD", [P, 4, 3 * P], where=m1c)
        fS = sb("fS", [P, 4, 3 * P], where=m1c)
        fPT = sb("fPT", [P, 4, 3 * P], where=m1c)
        ncs = sb("ncs", [P, NT, 4], where=m1c)
        m1c.close()
        m1d = ExitStack()
        sgq = sb("sgq", [P, NT, W], where=m1d)
        sw = sb("sw", [P, 4, P], where=m1d)
        swT = sb("swT", [P, 4, P], where=m1d)
        s_ng = sb("s_ng", [P, W], where=m1d)
        s_b = sb("s_b", [P, W], where=m1d)
        sm = sb("sm", [P, 4, TOK], where=m1d)
        m1d.close()
        m1.close()
        m2 = ExitStack()
        FFhi = sb("FFhi", [P, DFF // P, TOK], F32R, m2)
        FFlo = sb("FFlo", [P, DFF // P, TOK], F32R, m2)
        XN = sb("XN", [P, NT, D], where=m2)
        f1r = sb("f1r", [P, 4, TOK], where=m2)
        f1s = sb("f1s", [P, 4, TOK], where=m2)
        m2.close()
        PThi = sb("PThi", [P, 2, TOK], F32R)
        PTlo = sb("PTlo", [P, 2, TOK], F32R)
        dtv = sb("dtv", [P, NT, SSD_H])
        da = sb("da", [P, NT, SSD_H])
        ea2 = sb("ea2", [P, SSD_H])
        acs = sb("acs", [P, 3, SSD_H])
        eac = sb("eac", [P, 2, SSD_H])
        stats = sb("stats", [P, NT, 2, 6])
        moments = sb("moments", [P, NT, 2])
        nsink = sb("nsink", [P, AH])
        esink2 = sb("esink2", [P, 2, 4, 2])
        m3a = ExitStack()
        conv2 = sb("conv2", [P, 12, TOK + 3], where=m3a)
        xdt = sb("xdt", [P, NT, D], where=m3a)
        m3a.close()
        m3d = ExitStack()
        scc = sb("scc", [P, 4, TOK], where=m3d)
        scp = sb("scp", [P, 4, TOK + 2], where=m3d)
        scv = sb("scv", [P, 4, TOK], where=m3d)
        m3d.close()
        lnr = sb("lnr", [P, 5, D])
        sb("spare", [P, 64])
        m3 = ExitStack()
        BYhi = sb("BYhi", [P, 16, TOK], F32R, m3)
        BYlo = sb("BYlo", [P, 16, TOK], F32R, m3)
        zz = sb("zz", [P, NT, D], where=m3)
        xs = sb("xs", [P, NT, D], where=m3)
        yd = sb("yd", [P, NT, D], where=m3)
        pin = sb("pin", [P, NT, PLE], where=m3)
        bmt = sb("bmt", [P, 2 * P], where=m3)
        cbm = sb("cbm", [P, 4, P], where=m3)
        em = sb("em", [P, 8, P], where=m3)
        xe = sb("xe", [P, D], where=m3)
        hst = sb("hst", [P, D], where=m3)
        m3b = ExitStack()
        xbcT = sb("xbcT", [P, 12, TOK], where=m3b)
        m3b.close()
        m3.close()
        m4 = ExitStack()
        Hhi = sb("Hhi", [P, KF2, TOK], F32R, m4)
        Hlo = sb("Hlo", [P, KF2, TOK], F32R, m4)
        sg = sb("sg", [P, 4, TOK], where=m4)
        fh = sb("fh", [P, 4, TOK], where=m4)
        xc = sb("xc", [P, NT, D], where=m4)
        pgt = sb("pgt", [P, NT, W], where=m4)
        pwt = sb("pwt", [P, 2, NT, W], where=m4)
        pin1 = sb("pin1", [P, NT, PLE], where=m4)
        m4.close()
        m5 = ExitStack()
        AThi = sb("AThi", [P, KD, TOK], F32R, m5)
        ATlo = sb("ATlo", [P, KD, TOK], F32R, m5)
        aqT = sb("aqT", [P, KD, TOK], where=m5)
        akr = sb("akr", [P, 2, TOK], where=m5)
        akd = sb("akd", [P, AKV, TOK], where=m5)
        av = sb("av", [P, NT, AKV * AD], where=m5)
        bv = sb("bv", [P, AKV * AD], where=m5)
        bo = sb("bo", [P, D], where=m5)
        wS2 = sb("wS2", [P, 2, 4, 3 * P], where=m5)
        wPT2 = sb("wPT2", [P, 2, 4, 3 * P], where=m5)
        m5.close()

        conv_in = dn[:, 0:4, :].rearrange("p a b -> p (a b)")[:, 0:12 * (TOK + 3)].rearrange(
            "p (f t) -> p f t", f=12)
        qkv = dn[:, 4:7, :].rearrange("p a (f t) -> p (a f) t", t=TOK)
        XN1 = dn[:, 7:9, :]
        d_sq = dn[:, 7:9, :].rearrange("p a b -> p (a b)")
        d_rn = dn[:, 0:2, :].rearrange("p a b -> p (a b)")
        qT, kT = dn[:, 4, :], dn[:, 5, :]
        qT4, kT4, vT4 = (dn[:, 4 + i, :].rearrange("p (h t) -> p h t", h=4) for i in range(3))
        d_v = dn[:, 6, :]
        d_e, d_lt, d_at, d_egr, d_br = dn[:, 2, :], dn[:, 1, :], dn[:, 3, :], dn[:, 9, :], dn[:, 0, :]
        d_kbe, d_kdec, d_vb = dn[:, 7, :], dn[:, 8, :], dn[:, 0, :]
        d_x, d_y, d_t1, d_ml = dn[:, 10, :], dn[:, 11, :], dn[:, 12, :], dn[:, 13, :]
        d_u, d_w, d_vn, d_s, d_o, d_osq = (
            dn[:, 13, :], dn[:, 12, :], dn[:, 1, :], dn[:, 10, 0:W], dn[:, 5, :], dn[:, 2, :])

        acc = ctx.enter_context(nc.psum_tensor("acc", [P, 2, NT, BANK], F32))
        pm = ctx.enter_context(nc.psum_tensor("pm", [P, 4, BANK], F32))

        names = """x_in c_in k_in w_hi w_lo w_used evac0 evac1 t_pe t_hi t_lo rstd xn cols conv_in conv dn_sq
            dn_l2 dn_rn dn_qkn sp_in sp_e dn_g dn_gc dn_gcs dn_gex dn_rows dn_e0 dn_egr dn_e dn_kk dn_lt dn_kv
            dn_vb dn_ml dn_t1 dn_t1c dn_pq dn_y dn_uw dn_uws sc_ws sc_vn sc_su sc_s dn_osq dn_oss dn_orn dn_o
            m_cn m_cn2 m_in m_sqs m_ss m_rn m_ang m_cs m_rope m_tn m_tnc m_tr m_trc a_sc a_s a_e a_p a_pt a_ptc
            a_o a_hi a_lo f_sq f_ss f_rn f_xn f_t f_tc f_cum f_d s_sq s_ss s_rn s_v s_w s_wt s_mx s_m s_hi s_lo
            g_done f1_r f1_hi f1_lo c2_in conv2 silu2 p_in dt_in dt_e dt_g s_cb s_xs s_xsc s_xd s_bt s_btc s_ac
            s_acc s_eac s_xe s_st s_stc s_yo s_yod b_row b_e0 b_e b_m b_y b_yd y_z y_ss y_n c_out c_hi c_lo
            ln_in ln_sum ln_rs xh h_x h_hi h_lo g_x g_s x_end q_in act_seq dve_seq fin out_done""".split()
        S = {n: sem(n) for n in names}
        s_raw = [sem(f"s_raw{i}") for i in range(RAW)]
        evac = (S["evac0"], S["evac1"])

        def evac_at(name):
            n = chunks[name][0]
            return evac[n % 2], n // 2 + 1

        def landed(name):
            return chunks[name][2]

        def begun(name, n):
            return chunks[name][1] + n

        def branch_tiles(i):
            at = 4 * (0, 1, 1, 0)[i]
            return slice(at, at + 4)

        def accT(name):
            n, _, _, _, w, _ = chunks[name]
            return acc[:, n % 2, :, 0:w]

        def accF(name):
            n, _, _, _, w, _ = chunks[name]
            return acc[:, n % 2].rearrange("p b (f t) -> p (b f) t", t=TOK)[:, 0:w // P, :]


        GATES = (0, 1, 3, 2)

        def batch_end(b):
            return begun("sh0", 4) + b

        def banks(kv):
            return pm if kv % 2 == 0 else acc[:].rearrange("p a t n -> p (a t) n")

        def level_end(s):
            return begun("fv", s + 2) if s < 3 else begun("sv", s - 2)

        block = ctx.enter_context(nc.Block())

        @block.sync
        def _(sp_):
            sp_.dma_start(X[:], a["x"].rearrange("(t p) d -> p t d", p=P)).then_inc(S["x_in"], 16)
            sp_.dma_start(ct[:, 0:HEAD_COLS], a["consts"][:, 0:HEAD_COLS]).then_inc(S["x_in"], 16)
            for u, (w, k, nk, c0, width) in enumerate(units):
                if u == 2:
                    sp_.dma_start(ct[:, HEAD_COLS:], a["consts"][:, HEAD_COLS:]).then_inc(S["k_in"], 16)
                if u >= RAW:
                    sp_.wait_ge(S["w_lo"], u - RAW + 1)
                src = a[w][k * P:(k + nk) * P, c0:c0 + width].rearrange("(k p) n -> p k n", p=P)
                sp_.dma_start(raw[:, u % RAW, 0:nk, 0:width], src).then_inc(s_raw[u % RAW], 16)
            sp_.wait_ge(S["fin"], 1)
            sp_.dma_start(out.rearrange("(t p) d -> p t d", p=P), X[:]).then_inc(S["out_done"], 16)
            sp_.wait_ge(S["out_done"], 16)

        @block.gpsimd
        def _(pool):
            for u, (w, k, nk, c0, width) in enumerate(units):
                pool.wait_ge(S["w_hi"], u + 1)
                nc.gpsimd.tensor_tensor(wlo[:, u % SPLIT, 0:nk, 0:width], raw[:, u % RAW, 0:nk, 0:width],
                                        whi[:, u % SPLIT, 0:nk, 0:width].bitcast(F32),
                                        ALU.subtract).then_inc(S["w_lo"], 1)

        @block.scalar
        def _(act):
            seq = [0]

            def link(ins):
                seq[0] += 1
                ins.then_inc(S["act_seq"], 1)
                act.wait_ge(S["act_seq"], seq[0])

            def fn(out_, in_, func, **k):
                return nc.scalar.activation(out_, in_, func, **k)

            split = [0]

            def high_halves(until):
                while split[0] < min(until, len(units)):
                    u = split[0]
                    w, k, nk, c0, width = units[u]
                    act.wait_ge(s_raw[u % RAW], 16 * (u // RAW + 1))
                    if u >= SPLIT:
                        act.wait_ge(S["w_used"], u - SPLIT + 1)
                    fn(whi[:, u % SPLIT, 0:nk, 0:width], raw[:, u % RAW, 0:nk, 0:width],
                       ACT.Copy).then_inc(S["w_hi"], 1)
                    split[0] += 1

            def ready(name):
                high_halves(landed(name) + AHEAD)
                act.wait_ge(S["w_used"], landed(name))

            def leave(name, out_, func=ACT.Copy):
                ready(name)
                view = accF(name) if chunks[name][5] == "F" else accT(name)
                fn(out_, view, func).then_inc(evac_at(name)[0], 1)

            def turn(name, hi, gain=None):
                g0, n, nf = turns[name]
                for g in range(n):
                    k = min(2, nf - 2 * g)
                    act.wait_ge(S["t_pe"], g0 + g + 1)
                    bank = pm[:, (g0 + g) % 4, 0:k * TOK].rearrange("p (f t) -> p f t", t=TOK)
                    if gain is None:
                        fn(hi[:, 2 * g:2 * g + k, :], bank, ACT.Copy).then_inc(S["t_hi"], 1)
                    else:
                        for f in range(k):
                            last = fn(hi[:, 2 * g + f, :], bank[:, f, :], ACT.Copy, scale=gain(2 * g + f))
                        last.then_inc(S["t_hi"], 1)

            def rstd(out_, in_, n, eps, k=1):
                link(fn(out_, in_, ACT.Ln, scale=1.0 / n, bias=eps))
                return fn(out_, out_, ACT.Exp, scale=-0.5)

            act.dma_start(rowsA[0:n_a, :], a["rows_a"]).then_inc(S["c_in"], 16)
            act.dma_start(rowsB[0:n_b, :], a["rows_b"]).then_inc(S["c_in"], 16)
            act.dma_start(heads[:], a["heads"].partition_broadcast(P)).then_inc(S["c_in"], 16)
            act.dma_start(o_g[:], a["dn_out_norm_g"].partition_broadcast(P)).then_inc(S["c_in"], 16)

            act.wait_ge(S["x_in"], 32)
            for t in range(NT):
                last = fn(XN1[:, t, :], X[:, t, :], ACT.Square, accum_out=ss[:, t:t + 1])
            link(last)
            rstd(rs[:, 0:NT], ss[:, 0:NT], D, eps6).then_inc(S["rstd"], 1)
            high_halves(AHEAD)
            act.wait_ge(S["cols"], 1)
            fn(colA[:], pm[:, 0, 0:n_a], ACT.Copy)
            link(fn(colB[:], pm[:, 0, P:P + n_b], ACT.Copy))
            fn(ea[:], headv("dn_a_log"), ACT.Exp).then_inc(S["cols"], 1)
            turn("x1", XThi, lambda f: acol("norm1_g", f))

            act.wait_ge(S["conv_in"], 1)

            def taps(j, name):
                leave(name, conv_in[:, 4 * j:4 * j + 4, 3:3 + TOK])

            def silu(j):
                act.wait_ge(S["conv"], j + 1)
                return fn(qkv[:, 4 * j:4 * j + 4, :], qkv[:, 4 * j:4 * j + 4, :], ACT.Silu)
            taps(0, "dq")
            taps(1, "dk")
            silu(0)
            taps(2, "dv")
            link(silu(1))
            fn(d_sq, qkv[:, 0:8, :].rearrange("p f t -> p (f t)"), ACT.Square).then_inc(S["dn_sq"], 1)
            leave("abc", abc[:])
            leave("ff", ffl[:])
            link(silu(2))

            act.wait_ge(S["dn_l2"], 1)
            link(fn(d_rn, pm[:].rearrange("p a b -> p (a b)"), ACT.Ln, bias=eps6))
            fn(d_rn, d_rn, ACT.Exp, scale=-0.5).then_inc(S["dn_rn"], 1)
            act.wait_ge(S["sp_in"], 1)
            fn(sp_y[:, :, 0:8], sp_y[:, :, 0:8], ACT.Exp, scale=-1.0)
            fn(beta[:], abc[:, :, 4:8], ACT.Exp, scale=-1.0).then_inc(S["sp_e"], 1)
            leave("z", zs[:], ACT.Silu)
            high_halves(begun("fq", 2) + AHEAD)
            act.wait_ge(S["dn_gcs"], 1)
            fn(gex[:, 0:2, :, :], gcs[:].rearrange("p (k t) h -> p k t h", k=2), ACT.Exp).then_inc(S["dn_gex"], 1)
            act.wait_ge(S["dn_rows"], 1)
            act.wait_ge(S["dn_qkn"], 1)
            fn(d_br, pm[:, 2:4, :].rearrange("p a b -> p (a b)"), ACT.Copy)
            act.wait_ge(S["dn_e0"], 1)
            fn(d_e, d_e, ACT.Exp).then_inc(S["dn_e"], 1)
            fn(d_egr, pm[:, 0:2, :].rearrange("p a b -> p (a b)"), ACT.Exp).then_inc(S["dn_egr"], 1)
            leave("fq", fx[:, :, 0:W])
            high_halves(begun("fk", 3) + AHEAD)
            leave("fk", fx[:, :, W:2 * W])
            for s in range(6):
                for hf in range(2):
                    act.wait_ge(S["dn_t1"], 2 * s + hf + 1)
                    fn(d_t1[:, hf * W:(hf + 1) * W], pm[:, 2 * hf, :], ACT.Copy).then_inc(S["dn_t1c"], 1)
                high_halves(level_end(s) + AHEAD)
                if s == 3:
                    leave("fv", fx[:, :, 2 * W:3 * W])
            act.wait_ge(S["dn_uw"], 1)
            fn(d_u, pm[:, 0:2, :].rearrange("p a b -> p (a b)"), ACT.Copy)
            fn(d_w, pm[:, 2:4, :].rearrange("p a b -> p (a b)"), ACT.Copy).then_inc(S["dn_uws"], 1)
            leave("sv", sgv[:], ACT.Gelu_apprx_tanh)
            leave("su", sgu[:], ACT.Gelu_apprx_tanh)
            act.wait_ge(S["sc_su"], 4)
            fn(d_osq, pm[:, 1:3, :].rearrange("p a b -> p (a b)"), ACT.Square).then_inc(S["dn_osq"], 1)
            act.wait_ge(S["dn_oss"], 1)
            rstd(rs[:, 0:8], ss[:, 0:8], DH, eps6).then_inc(S["dn_orn"], 1)

            def gate(i, c):
                if i != GATES[0]:
                    act.wait_ge(*evac_at(f"br{GATES[GATES.index(i) - 1]}_{c}"))
                leave(f"gate{i}_{c}", gt[:, c], ACT.Sigmoid)
            gate(0, 0)
            high_halves(begun("gate0_1", 3) + AHEAD)
            turn("oa", BRhi[:, branch_tiles(0), :])

            act.wait_ge(S["t_lo"], turns["oa"][0] + turns["oa"][1])
            act.dma_start(posi[:], a["positions"]).then_inc(S["m_in"], 16)
            act.dma_start(m_g[:, 0, :], a["mla_qk_q_g"].partition_broadcast(P)).then_inc(S["m_in"], 16)
            act.dma_start(m_g[:, 1, :], a["mla_qk_k_g"].partition_broadcast(P)).then_inc(S["m_in"], 16)
            for t in range(NT):
                fn(cn[:, t, 0:MLA_QR], abc[:, t, 8:8 + MLA_QR], ACT.Square, accum_out=ss[:, 2 * t:2 * t + 1])
                last = fn(cn[:, t, MLA_QR:3 * P], abc[:, t, 8 + MLA_QR:8 + 3 * P], ACT.Square,
                          accum_out=ss[:, 2 * t + 1:2 * t + 2])
            link(last)
            link(fn(rs[:, 0:4:2], ss[:, 0:4:2], ACT.Ln, scale=1.0 / MLA_QR, bias=eps6))
            link(fn(rs[:, 1:4:2], ss[:, 1:4:2], ACT.Ln, scale=1.0 / MLA_KVR, bias=eps6))
            fn(rs[:, 0:4], rs[:, 0:4], ACT.Exp, scale=-0.5).then_inc(S["m_cn"], 1)
            gate(0, 1)
            high_halves(landed("br0_1") + AHEAD)
            act.wait_ge(S["m_ang"], 1)
            fn(cs[:], ang[:, 0:2, :, :], ACT.Sin).then_inc(S["m_cs"], 1)
            turn("cqkv", MQhi, lambda f: acol("mla_q_norm_g", f) if f < 2 else acol("mla_kv_norm_g"))
            for j in range(2):
                leave(f"uq{j}", mq[:, 0, :, 2 * j:2 * j + 2, :].rearrange("p t h d -> p t (h d)"))
            for j in range(2):
                ready(f"ukv{j}")
                view = accT(f"ukv{j}").rearrange("p t (h d) -> p t h d", h=2)
                fn(mq[:, 1, :, 2 * j:2 * j + 2, 0:NOPE], view[:, :, :, 0:NOPE], ACT.Copy)
                fn(mv[:].rearrange("p t (h d) -> p t h d", h=4)[:, :, 2 * j:2 * j + 2, :],
                   view[:, :, :, NOPE:NOPE + P], ACT.Copy).then_inc(evac_at(f"ukv{j}")[0], 1)
            for i in range(2):
                act.wait_ge(S["m_cn2"], 2 + i)
                if i == 0:
                    act.wait_ge(*evac_at("uq1"))
                else:
                    act.wait_ge(*evac_at("ukv1"))
                fn(msq[:].rearrange("p (t h d) -> p t h d", t=NT, h=4), mq[:, i], ACT.Square).then_inc(S["m_sqs"], 1)
                act.wait_ge(S["m_ss"], i + 1)
                rstd(rs[:, 8 * i:8 * i + 8], ss[:, 8 * i:8 * i + 8], QK, eps6).then_inc(S["m_rn"], 1)
                if i == 0:
                    high_halves(begun("gate1_0", 2) + AHEAD)
            gate(1, 0)
            high_halves(begun("gate1_1", 2) + AHEAD)
            act.wait_ge(S["m_tn"], 1)
            fn(mT[:].rearrange("p a b -> p (a b)"), pm[:].rearrange("p a b -> p (a b)"), ACT.Copy)\
                .then_inc(S["m_tnc"], 1)
            act.wait_ge(S["m_tr"], 1)
            fn(mR[:].rearrange("p a b -> p (a b)"), pm[0:ROPE].rearrange("p a b -> p (a b)"), ACT.Copy)\
                .then_inc(S["m_trc"], 1)

            def attention(n, s, pt, branch, meanwhile):
                act.wait_ge(S["a_s"], n + 1)
                for h in range(4):
                    fn(s[:, h, 0:P], s[:, h, 0:P], ACT.Exp, bias=attn_neg[:, h, 0:1],
                       accum_out=attn_sum[:, h, 0:1])
                    last = fn(s[:, h, P:3 * P], s[:, h, P:3 * P], ACT.Exp, bias=attn_neg[:, h, 1:2],
                              accum_out=attn_sum[:, h, 1:2])
                last.then_inc(S["a_e"], 1)
                meanwhile()
                act.wait_ge(S["a_pt"], n + 1)
                fn(pt[:], pm[:, :, 0:3 * P], ACT.Copy).then_inc(S["a_ptc"], 1)
                act.wait_ge(S["a_o"], n + 1)
                fn(BRhi[:, branch_tiles(branch), :].rearrange("p a b -> p (a b)"),
                   pm[:, 0:2, :].rearrange("p a b -> p (a b)"), ACT.Copy).then_inc(S["a_hi"], 1)

            mS = mq[:, 0].rearrange("p t h d -> p (t h d)").rearrange("p (h s) -> p h s", h=4)
            mP = mq[:, 1].rearrange("p t h d -> p (t h d)").rearrange("p (h s) -> p h s", h=4)
            attention(0, mS, mP, 1, lambda: gate(1, 1))

            act.wait_ge(S["a_lo"], 1)
            fn(fsq[:], fx[:, :, 0:D], ACT.Square).then_inc(S["f_sq"], 1)
            act.wait_ge(S["f_ss"], 1)
            rstd(rs[:, 0:16], ss[:, 0:16], DH, eps6).then_inc(S["f_rn"], 1)
            high_halves(landed("br1_1") + AHEAD)
            act.wait_ge(S["f_t"], 1)
            for i in range(2):
                last = fn(fT[:, 4 * i:4 * i + 4, :].rearrange("p a b -> p (a b)"),
                          pm[:, 2 * i:2 * i + 2, :].rearrange("p a b -> p (a b)"), ACT.Copy,
                          scale=acol(("fox_q_norm_g", "fox_k_norm_g")[i]))
            last.then_inc(S["f_tc"], 1)
            high_halves(begun("gate3_0", 2) + AHEAD)
            attention(1, fS, fPT, 3, lambda: gate(3, 0))

            act.wait_ge(S["a_lo"], 2)
            act.dma_start(sw[:], a["sg_w_s"].rearrange("g t s -> t g s")).then_inc(S["s_w"], 16)
            act.dma_start(s_ng[:], a["sg_v_norm_g"].partition_broadcast(P)).then_inc(S["s_w"], 16)
            act.dma_start(s_b[:], a["sg_b_s"].partition_broadcast(P)).then_inc(S["s_w"], 16)
            fn(sgq[:], sgv[:], ACT.Square).then_inc(S["s_sq"], 1)
            act.wait_ge(S["s_ss"], 1)
            rstd(rs[:, 0:8], ss[:, 0:8], P, eps6).then_inc(S["s_rn"], 1)
            gate(3, 1)
            high_halves(landed("br3_1") + AHEAD)
            act.wait_ge(S["s_m"], 1)
            fn(BRhi[:, branch_tiles(2), :], sm[:], ACT.Copy).then_inc(S["s_hi"], 1)

            gate(2, 0)
            gate(2, 1)
            high_halves(landed("br2_1") + AHEAD)
            turn("merged", XThi)
            for c in range(2):
                high_halves(landed(f"wo{c}") + AHEAD)
            act.wait_ge(*evac_at("wo1"))
            act.wait_ge(S["t_lo"], turns["merged"][0] + turns["merged"][1])
            for t in range(NT):
                last = fn(XN[:, t, :], X[:, t, :], ACT.Square, accum_out=ss[:, t:t + 1])
            link(last)
            rstd(rs[:, 0:NT], ss[:, 0:NT], D, eps6).then_inc(S["rstd"], 1)
            turn("x2", XThi, lambda f: acol("norm2_g", f))

            for c in range(DFF // W):
                high_halves(landed(f"f1_{c}") + AHEAD)
                act.wait_ge(S["f1_r"], c + 1)
                if c >= 1:
                    act.wait_ge(S["f1_lo"], c)
                link(fn(f1s[:], f1r[:], ACT.Square))
                fn(FFhi[:, 4 * c:4 * c + 4, :], f1s[:], ACT.Copy).then_inc(S["f1_hi"], 1)
            for c in range(2):
                high_halves(landed(f"f2_{c}") + AHEAD)

            act.wait_ge(*evac_at("f2_1"))
            act.dma_start(pin[:], a["p0"].rearrange("(t p) d -> p t d", p=P)).then_inc(S["p_in"], 16)
            turn("x3", XThi)
            turn("p0", PThi)
            act.wait_ge(S["c2_in"], 1)
            leave("xbc0", conv2[:, 0:4, 3:3 + TOK])
            leave("xbc1", conv2[:, 4:8, 3:3 + TOK])

            def silu2(j):
                act.wait_ge(S["conv2"], j + 1)
                fn(xbcT[:, 4 * j:4 * j + 4, :], xbcT[:, 4 * j:4 * j + 4, :], ACT.Silu).then_inc(S["silu2"], 1)
            leave("xbc2", conv2[:, 8:12, 3:3 + TOK])
            for j in range(3):
                silu2(j)
            high_halves(landed("dt") + AHEAD)
            for c in range(2):
                leave(f"mz{c}", zz[:, :, c * W:(c + 1) * W], ACT.Silu)
            act.wait_ge(S["dt_in"], 1)
            fn(ea2[:], headv("ssd_a_log"), ACT.Exp)
            fn(sp_y[:], sp_y[:], ACT.Exp, scale=-1.0).then_inc(S["dt_e"], 1)
            act.wait_ge(S["s_xs"], 1)
            fn(xs[:].rearrange("p t d -> p (t d)"), pm[:].rearrange("p a b -> p (a b)"), ACT.Copy)\
                .then_inc(S["s_xsc"], 1)
            high_halves(begun("sc0", 2) + AHEAD)
            act.wait_ge(S["s_bt"], 1)
            fn(bmt[:], pm[:, 0, 0:2 * P], ACT.Copy).then_inc(S["s_btc"], 1)
            high_halves(begun("sc0", 3) + AHEAD)
            act.wait_ge(S["s_acc"], 1)
            fn(eac[:], acs[:, 1:3, :], ACT.Exp).then_inc(S["s_eac"], 1)
            high_halves(begun("sh0", 1) + AHEAD)
            act.wait_ge(S["s_st"], 1)
            fn(hst[:], pm[:, 2:4, :].rearrange("p a b -> p (a b)"), ACT.Copy).then_inc(S["s_stc"], 1)
            leave("sc0", scc[:])
            high_halves(begun("sh0", 3) + AHEAD)
            for b in range(4):
                act.wait_ge(S["b_e0"], b + 1)
                fn(em[:], em[:], ACT.Exp).then_inc(S["b_e"], 1)
                high_halves(batch_end(b) + AHEAD)
            act.wait_ge(S["y_z"], 1)
            for t in range(NT):
                for g in range(2):
                    last = fn((xe, hst)[t][:, g * W:(g + 1) * W], yd[:, t, g * W:(g + 1) * W], ACT.Square,
                              accum_out=ss[:, 2 * t + g:2 * t + g + 1])
            link(last)
            rstd(rs[:, 0:4], ss[:, 0:4], W, eps5).then_inc(S["y_ss"], 1)
            high_halves(begun("sc1", 2) + AHEAD)
            act.wait_ge(S["c_out"], 1)
            fn(BYhi[:, 8:12, :], scv[:], ACT.Copy).then_inc(S["c_hi"], 1)
            high_halves(landed("sh1") + AHEAD)
            turn("y", BYhi[:, 0:8, :], lambda f: bcol("ssd_norm_w", f))
            leave("sc1", scc[:])
            high_halves(landed("sb1") + AHEAD)
            act.wait_ge(S["c_out"], 2)
            fn(BYhi[:, 12:16, :], scv[:], ACT.Copy).then_inc(S["c_hi"], 1)

            def load_rows(i):
                for j, n in enumerate(("ln_mix_g", "ln_mix_b", "ln_ffn_g", "ln_ffn_b", "b_ple_gate")):
                    act.dma_start(lnr[:, j, :], a[f"{n}{i}"].partition_broadcast(P)).then_inc(S["ln_in"], 16)
            act.wait_ge(S["c_lo"], 2)
            load_rows(0)
            for c in range(2):
                high_halves(landed(f"mo{c}") + AHEAD)

            def layer_norm(n):
                act.wait_ge(S["ln_sum"], n + 1)
                rstd(rs[:, 0:NT], moments[:, :, 1], 1, eps5).then_inc(S["ln_rs"], 1)

            layer_norm(0)

            def feed_forward(i):
                turn(("x4", "x7")[i], XThi)
                for c in range(-(-DFF2 // W)):
                    k = 6 * i + c
                    nf = chunks[f"fg{i}_{c}"][4] // P
                    if k:
                        act.wait_ge(S["h_x"], k)
                    leave(f"fg{i}_{c}", sg[:, 0:nf, :], ACT.Silu)
                    high_halves(landed(f"fu{i}_{c}") + AHEAD)
                    act.wait_ge(S["h_x"], k + 1)
                    fn(Hhi[:, 4 * c:4 * c + nf, :], fh[:, 0:nf, :], ACT.Copy).then_inc(S["h_hi"], 1)
                for c in range(2):
                    high_halves(landed(f"fd{i}_{c}") + AHEAD)
                leave(f"pw{i}_0", pwt[:, 0])
                layer_norm(2 * i + 1)
                leave(f"pw{i}_1", pwt[:, 1])
                turn(("x5", "x8")[i], XThi)
                for c in range(2):
                    high_halves(landed(f"pg{i}_{c}") + AHEAD)
                    act.wait_ge(S["g_x"], 2 * i + c + 1)
                    fn(pgt[:], pgt[:], ACT.Sigmoid).then_inc(S["g_s"], 1)
            feed_forward(0)

            act.wait_ge(S["x_end"], 1)
            load_rows(1)
            act.dma_start(bv[:], a["b_v"].partition_broadcast(P)).then_inc(S["q_in"], 16)
            act.dma_start(bo[:], a["b_o"].partition_broadcast(P)).then_inc(S["q_in"], 16)
            turn("x6", XThi)
            for c in range(2):
                ready(f"aq{c}")
                for f in range(4):
                    last = fn(aqT[:, 4 * c + f, :], accF(f"aq{c}")[:, f, :], ACT.Identity,
                              bias=bcol("b_qk", 4 * c + f))
                last.then_inc(evac_at(f"aq{c}")[0], 1)
            ready("ak")
            for f in range(2):
                last = fn(akr[:, f, :], accF("ak")[:, f, :], ACT.Identity, bias=bcol("b_qk", 8 + f))
            last.then_inc(evac_at("ak")[0], 1)
            high_halves(landed("av") + AHEAD)
            for pair in ((0, 1), (2, 3)):
                for kv in pair:
                    wS, neg, total = wS2[:, kv % 2], attn_neg2[:, kv % 2], attn_sum2[:, kv % 2]
                    act.wait_ge(S["a_s"], kv + 3)
                    for h in range(4):
                        fn(wS[:, h, 0:P], wS[:, h, 0:P], ACT.Exp, bias=neg[:, h, 0:1],
                           accum_out=total[:, h, 0:1])
                        fn(wS[:, h, P:3 * P], wS[:, h, P:3 * P], ACT.Exp, bias=neg[:, h, 1:2],
                           accum_out=total[:, h, 1:2])
                    fn(esink2[:, kv % 2], esink2[:, kv % 2], ACT.Exp).then_inc(S["a_e"], 1)
                for kv in pair:
                    act.wait_ge(S["a_pt"], kv + 3)
                    fn(wPT2[:, kv % 2], banks(kv)[:, :, 0:3 * P], ACT.Copy).then_inc(S["a_ptc"], 1)
                for kv in pair:
                    act.wait_ge(S["a_o"], kv + 3)
                    fn(AThi[:, 2 * kv:2 * kv + 2, :].rearrange("p a b -> p (a b)"), banks(kv)[:, 0, :], ACT.Copy)\
                        .then_inc(S["a_hi"], 1)
            act.wait_ge(S["a_lo"], 6)
            act.dma_start(pin1[:], a["p1"].rearrange("(t p) d -> p t d", p=P)).then_inc(S["p_in"], 16)
            for c in range(2):
                high_halves(landed(f"ao{c}") + AHEAD)
            layer_norm(2)
            turn("p1", PThi)
            feed_forward(1)

        @block.vector
        def _(v):
            seq = [0]
            V = nc.vector

            def link(ins):
                seq[0] += 1
                ins.then_inc(S["dve_seq"], 1)
                v.wait_ge(S["dve_seq"], seq[0])

            def turn(name, hi, lo, gain=None):
                g0, n, nf = turns[name]
                for g in range(n):
                    k = min(2, nf - 2 * g)
                    v.wait_ge(S["t_hi"], g0 + g + 1)
                    bank = pm[:, (g0 + g) % 4, 0:k * TOK].rearrange("p (f t) -> p f t", t=TOK)
                    if gain is None:
                        V.tensor_tensor(lo[:, 2 * g:2 * g + k, :], bank, hi[:, 2 * g:2 * g + k, :].bitcast(F32),
                                        ALU.subtract).then_inc(S["t_lo"], 1)
                    else:
                        for f in range(k):
                            last = V.scalar_tensor_tensor(
                                out=lo[:, 2 * g + f, :], in0=bank[:, f, :], scalar=gain(2 * g + f),
                                in1=hi[:, 2 * g + f, :].bitcast(F32), op0=ALU.mult, op1=ALU.subtract)
                        last.then_inc(S["t_lo"], 1)

            def softplus_tail(x, y, n):
                z, z2, p, o = (b[:, :, 0:n] for b in (sp_z, sp_z2, sp_p, sp))
                link(V.tensor_scalar(z, y, 2.0, None, ALU.add))
                link(V.reciprocal(z, z))
                link(V.tensor_tensor(z, z, y, ALU.mult))
                link(V.tensor_tensor(z2, z, z, ALU.mult))
                link(V.tensor_scalar(p, z2, 1.0 / 17, 1.0 / 15, ALU.mult, ALU.add))
                link(V.tensor_tensor(p, p, z2, ALU.mult))
                for k in (13, 11, 9, 7, 5, 3):
                    link(V.scalar_tensor_tensor(out=p, in0=p, scalar=1.0 / k, in1=z2, op0=ALU.add, op1=ALU.mult))
                link(V.scalar_tensor_tensor(out=p, in0=p, scalar=1.0, in1=z, op0=ALU.add, op1=ALU.mult))
                link(V.tensor_scalar(o, x, 0.0, None, ALU.max))
                link(V.scalar_tensor_tensor(out=o, in0=p, scalar=2.0, in1=o, op0=ALU.mult, op1=ALU.add))

            def heads_of(col, n=P):
                return col.rearrange("p t h -> p h t").unsqueeze(3).to_broadcast([P, 4, NT, n])

            def ht(ap):
                return ap.rearrange("p (h t s) -> p h t s", h=4, t=NT)

            v.wait_ge(S["rstd"], 1)
            for t in range(NT):
                last = V.tensor_scalar(XN1[:, t, :], X[:, t, :], rs[:, t:t + 1], None, ALU.mult)
            last.then_inc(S["xn"], 1)
            V.memset(conv_in[:, :, 0:3], 0.0).then_inc(S["conv_in"], 1)
            v.wait_ge(S["cols"], 2)
            turn("x1", XThi, XTlo, lambda f: acol("norm1_g", f))

            for j, name in enumerate(("dq", "dk", "dv")):
                v.wait_ge(*evac_at(name))
                for k in range(4):
                    for f in range(4 * j, 4 * j + 4):
                        w = acol("dn_conv_w", 12 * k + f)
                        if k == 0:
                            last = V.tensor_scalar(qkv[:, f, :], conv_in[:, f, 0:TOK], w, None, ALU.mult)
                        else:
                            last = V.scalar_tensor_tensor(out=qkv[:, f, :], in0=conv_in[:, f, k:k + TOK], scalar=w,
                                                          in1=qkv[:, f, :], op0=ALU.mult, op1=ALU.add)
                    if k < 3:
                        link(last)
                last.then_inc(S["conv"], 1)
            v.wait_ge(*evac_at("abc"))
            v.wait_ge(*evac_at("ff"))
            V.tensor_tensor(logit[:, :, 0:4], abc[:, :, 0:4],
                            headv("dn_dt_bias").unsqueeze(1).to_broadcast([P, NT, 4]), ALU.add)
            link(V.tensor_tensor(logit[:, :, 4:8], ffl[:],
                                 headv("fox_f_bias").unsqueeze(1).to_broadcast([P, NT, 4]), ALU.add))
            link(V.tensor_scalar(logit[:, :, 4:8], logit[:, :, 4:8], -1.0, None, ALU.mult))
            V.scalar_tensor_tensor(out=sp_y[:, :, 0:8], in0=logit[:, :, 0:8], scalar=-1.0, in1=logit[:, :, 0:8],
                                   op0=ALU.mult, op1=ALU.max).then_inc(S["sp_in"], 1)
            v.wait_ge(S["sp_e"], 1)
            softplus_tail(logit[:, :, 0:8], sp_y[:, :, 0:8], 8)
            V.tensor_copy(nlf[:], sp[:, :, 4:8])
            V.scalar_tensor_tensor(out=dng[:], in0=sp[:, :, 0:4], scalar=-1.0,
                                   in1=ea[:].unsqueeze(1).to_broadcast([P, NT, 4]), op0=ALU.mult, op1=ALU.mult)
            link(V.tensor_scalar(beta[:], beta[:], 1.0, None, ALU.add))
            V.reciprocal(beta[:], beta[:]).then_inc(S["dn_g"], 1)
            v.wait_ge(S["dn_gc"], 1)
            link(V.tensor_copy(gcs[:], pm[:, 0, 0:16].rearrange("p (k h) -> p k h", h=4)))
            V.tensor_tensor(gcs[:, 2:4, :], gcs[:, 2:4, :], gcs[:, 0:2, :], ALU.subtract).then_inc(S["dn_gcs"], 1)

            v.wait_ge(S["dn_rn"], 1)
            V.scalar_tensor_tensor(out=qT, in0=qT, scalar=DH ** -0.5, in1=d_rn[:, 0:1024], op0=ALU.mult, op1=ALU.mult)
            V.tensor_tensor(kT, kT, d_rn[:, 1024:2048], ALU.mult).then_inc(S["dn_qkn"], 1)
            v.wait_ge(S["dn_rows"], 1)
            for h in range(4):
                for t in range(NT):
                    i = (h * NT + t) * P
                    last = V.scalar_tensor_tensor(out=d_e[:, i:i + P], in0=pm[:, i // BANK, i % BANK:i % BANK + P],
                                                  scalar=gcs[:, t, h:h + 1], in1=con("strict64"),
                                                  op0=ALU.subtract, op1=ALU.mult)
            last.then_inc(S["dn_e0"], 1)
            v.wait_ge(S["dn_gex"], 1)
            V.tensor_tensor(gex[:, 2], beta[:], gex[:, 0], ALU.mult)
            v.wait_ge(S["dn_kk"], 1)
            v.wait_ge(S["dn_e"], 1)
            V.scalar_tensor_tensor(out=d_lt, in0=d_e, scalar=1.0, in1=pm[:, 0:2, :].rearrange("p a b -> p (a b)"),
                                   op0=ALU.min, op1=ALU.mult)
            V.scalar_tensor_tensor(out=d_at, in0=d_e, scalar=1.0, in1=pm[:, 2:4, :].rearrange("p a b -> p (a b)"),
                                   op0=ALU.min, op1=ALU.mult).then_inc(S["dn_lt"], 1)
            v.wait_ge(S["dn_lt"], 1)
            v.wait_ge(S["dn_egr"], 1)
            V.tensor_tensor(d_lt, d_lt, d_br, ALU.mult)
            V.tensor_tensor(d_at.rearrange("p (k s) -> p k s", s=P), d_at.rearrange("p (k s) -> p k s", s=P),
                            con("tri64").unsqueeze(1).to_broadcast([P, 8, P]), ALU.mult)
            for x in (d_x, d_y):
                last = V.tensor_copy(x.rearrange("p (k s) -> p k s", s=P), ident.unsqueeze(1).to_broadcast([P, 8, P]))
            link(last)
            v.wait_ge(S["dn_kv"], 1)
            kp = ht(pm[:, 0:2, :].rearrange("p a b -> p (a b)"))
            vp = ht(pm[:, 2:4, :].rearrange("p a b -> p (a b)"))
            V.tensor_tensor(ht(d_kbe), kp, heads_of(gex[:, 2]), ALU.mult)
            V.tensor_tensor(ht(d_kdec), kp, heads_of(gex[:, 1]), ALU.mult)
            V.tensor_tensor(ht(d_vb), vp, heads_of(beta[:]), ALU.mult).then_inc(S["dn_vb"], 1)
            for s in range(6):
                for hf in range(2):
                    half = slice(hf * W, (hf + 1) * W)
                    if s:
                        v.wait_ge(S["dn_pq"], 2 * (s - 1) + hf + 1)
                        V.tensor_tensor(d_x[:, half], d_x[:, half], pm[:, 2 * hf + 1, :], ALU.subtract)
                        V.tensor_tensor(d_y[:, half], d_y[:, half], pm[:, 2 * hf, :], ALU.subtract)
                    V.tensor_tensor(d_ml[:, half].rearrange("p (k s) -> p k s", s=P),
                                    d_lt[:, half].rearrange("p (k s) -> p k s", s=P),
                                    con(f"lvl{s}").unsqueeze(1).to_broadcast([P, 4, P]), ALU.mult)\
                        .then_inc(S["dn_ml"], 1)
            for hf in range(2):
                half = slice(hf * W, (hf + 1) * W)
                v.wait_ge(S["dn_pq"], 10 + hf + 1)
                V.tensor_tensor(d_y[:, half], d_y[:, half], pm[:, 2 * hf, :], ALU.subtract).then_inc(S["dn_y"], 1)
            V.tensor_tensor(qT, qT, d_egr, ALU.mult).then_inc(S["dn_y"], 1)
            u4 = d_u.rearrange("p (h t s) -> p h t s", h=4, t=NT)
            vn4 = d_vn.rearrange("p (h t s) -> p h t s", h=4, t=NT)
            for n in range(4):
                t, r = n // 2, 64 * (n % 2)
                if n == 0:
                    v.wait_ge(S["dn_uws"], 1)
                    V.tensor_copy(vn4[r:r + 64, :, t, :], u4[r:r + 64, :, t, :]).then_inc(S["sc_vn"], 1)
                else:
                    v.wait_ge(S["sc_ws"], n)
                    V.tensor_tensor(vn4[r:r + 64, :, t, :], u4[r:r + 64, :, t, :],
                                    pm[r:r + 64, 0, :].rearrange("p (h s) -> p h s", h=4), ALU.subtract)\
                        .then_inc(S["sc_vn"], 1)
                v.wait_ge(S["sc_su"], n + 1)
                if n == 0:
                    V.tensor_copy(d_s, pm[:, 3, :]).then_inc(S["sc_s"], 1)
                elif n < 3:
                    for h in range(4):
                        g = d_egr[:, h * TOK + 64 * n + 63:h * TOK + 64 * n + 64]
                        last = V.scalar_tensor_tensor(out=d_s[:, h * P:(h + 1) * P], in0=d_s[:, h * P:(h + 1) * P],
                                                      scalar=g, in1=pm[:, 3, h * P:(h + 1) * P],
                                                      op0=ALU.mult, op1=ALU.add)
                    last.then_inc(S["sc_s"], 1)
            v.wait_ge(S["dn_osq"], 1)
            V.tensor_reduce(ss[:, 0:8], d_osq.rearrange("p (k s) -> p k s", s=P), AX_X, ALU.add)\
                .then_inc(S["dn_oss"], 1)
            v.wait_ge(S["dn_orn"], 1)
            o8 = d_o.rearrange("p (k s) -> p k s", s=P)
            link(V.tensor_tensor(o8, pm[:, 1:3, :].rearrange("p a (h s) -> p (a h) s", s=P),
                                 rs[:, 0:8].unsqueeze(2).to_broadcast([P, 8, P]), ALU.mult))
            link(V.tensor_tensor(o8, o8, o_g[:].unsqueeze(1).to_broadcast([P, 8, P]), ALU.mult))
            V.tensor_tensor(d_o, d_o, zs[:].rearrange("p t d -> p (t d)"), ALU.mult).then_inc(S["dn_o"], 1)
            turn("oa", BRhi[:, branch_tiles(0), :], BRlo[:, branch_tiles(0), :])

            v.wait_ge(S["m_in"], 48)
            link(V.tensor_copy(posf[:], posi[:]))
            freq = con("freq").unsqueeze(1).to_broadcast([P, NT, ROPE // 2])
            pos = posf[:].unsqueeze(2).to_broadcast([P, NT, ROPE // 2])
            link(V.tensor_tensor(ang[:, 2], freq, pos, ALU.mult))
            big = 1.5 * 2 ** 23
            for i, turn_at in ((0, 0.25), (1, 0.0)):
                link(V.tensor_scalar(ang[:, i], ang[:, 2], 1.0 / (2 * np.pi), turn_at, ALU.mult, ALU.add))
                link(V.tensor_scalar(ang[:, i], ang[:, i], big, None, ALU.add))
                link(V.tensor_scalar(ang[:, i], ang[:, i], -big, None, ALU.add))
                parts = (6.28125, 0.00193500518798828125, 2 * np.pi - 6.28125 - 0.00193500518798828125)
                tmp = rt[:, 0].rearrange("p t h d -> p (t h d)")[:, 0:NT * 32].rearrange("p (t d) -> p t d", t=NT)
                link(V.scalar_tensor_tensor(out=tmp, in0=ang[:, i], scalar=-parts[0], in1=ang[:, 2],
                                            op0=ALU.mult, op1=ALU.add))
                link(V.scalar_tensor_tensor(out=tmp, in0=ang[:, i], scalar=-parts[1], in1=tmp,
                                            op0=ALU.mult, op1=ALU.add))
                link(V.scalar_tensor_tensor(out=ang[:, i], in0=ang[:, i], scalar=-parts[2], in1=tmp,
                                            op0=ALU.mult, op1=ALU.add))
                if i == 0:
                    link(V.tensor_scalar(ang[:, 0], ang[:, 0], np.pi / 2, None, ALU.add))
            lim = 3.1415925
            V.tensor_scalar(ang[:, 0:2], ang[:, 0:2], lim, -lim, ALU.min, ALU.max).then_inc(S["m_ang"], 1)
            v.wait_ge(S["m_cn"], 1)
            for t in range(NT):
                V.tensor_scalar(cn[:, t, 0:MLA_QR], abc[:, t, 8:8 + MLA_QR], rs[:, 2 * t:2 * t + 1], None, ALU.mult)
                last = V.tensor_scalar(cn[:, t, MLA_QR:3 * P], abc[:, t, 8 + MLA_QR:8 + 3 * P],
                                       rs[:, 2 * t + 1:2 * t + 2], None, ALU.mult)
            last.then_inc(S["m_cn2"], 1)

            def merge(i, c):
                v.wait_ge(S["w_used"], landed(f"br{i}_{c}"))
                v.wait_ge(*evac_at(f"gate{i}_{c}"))
                dst = merged[:, :, c * W:(c + 1) * W]
                done = evac_at(f"br{i}_{c}")
                if i == GATES[0]:
                    V.tensor_tensor(dst, accT(f"br{i}_{c}"), gt[:, c], ALU.mult).then_inc(done[0], 1)
                else:
                    V.tensor_tensor(gp[:], accT(f"br{i}_{c}"), gt[:, c], ALU.mult).then_inc(done[0], 1)
                    v.wait_ge(*done)
                    link(V.tensor_tensor(dst, dst, gp[:], ALU.add))
            merge(0, 0)
            merge(0, 1)
            turn("cqkv", MQhi, MQlo, lambda f: acol("mla_q_norm_g", f) if f < 2 else acol("mla_kv_norm_g"))
            V.tensor_copy(mq[:, 1, :, :, NOPE:QK],
                          abc[:, :, 8 + 3 * P:ABC].unsqueeze(2).to_broadcast([P, NT, 4, ROPE]))\
                .then_inc(S["m_cn2"], 1)
            for i in range(2):
                v.wait_ge(S["m_sqs"], i + 1)
                V.tensor_reduce(ss[:, 8 * i:8 * i + 8], msq[:].rearrange("p (k d) -> p k d", d=QK), AX_X, ALU.add)\
                    .then_inc(S["m_ss"], 1)
                if i == 0:
                    v.wait_ge(S["m_ss"], 1)
                    V.engine_nop().then_inc(S["m_cn2"], 1)
                v.wait_ge(S["m_rn"], i + 1)
                q8 = mq[:, i].rearrange("p t h d -> p (t h) d")
                link(V.tensor_tensor(q8, q8, rs[:, 8 * i:8 * i + 8].unsqueeze(2).to_broadcast([P, 8, QK]), ALU.mult))
                link(V.tensor_tensor(q8, q8, m_g[:, i, :].unsqueeze(1).to_broadcast([P, 8, QK]), ALU.mult))
                if i == 0:
                    v.wait_ge(S["m_cs"], 1)
                x1, x2 = mq[:, i, :, :, NOPE:NOPE + 32], mq[:, i, :, :, NOPE + 32:QK]
                cos = cs[:, 0].unsqueeze(2).to_broadcast([P, NT, 4, 32])
                sin = cs[:, 1].unsqueeze(2).to_broadcast([P, NT, 4, 32])
                V.tensor_tensor(rt[:, 0], x1, cos, ALU.mult)
                V.tensor_tensor(rt[:, 1], x2, sin, ALU.mult)
                V.tensor_tensor(rt[:, 2], x2, cos, ALU.mult)
                link(V.tensor_tensor(rt[:, 3], x1, sin, ALU.mult))
                V.tensor_tensor(x1, rt[:, 0], rt[:, 1], ALU.subtract)
                V.tensor_tensor(x2, rt[:, 2], rt[:, 3], ALU.add).then_inc(S["m_rope"], 1)

            def attention(n, s, scale, add, branch):
                v.wait_ge(S["a_sc"], n + 1)
                link(V.scalar_tensor_tensor(out=s, in0=pm[:, :, 0:3 * P], scalar=scale, in1=add,
                                            op0=ALU.mult, op1=ALU.add))
                V.tensor_reduce(attn_neg[:, :, 0:1], s[:, :, 0:P], AX_X, ALU.max, negate=True)
                V.tensor_reduce(attn_neg[:, :, 1:2], s[:, :, P:3 * P], AX_X, ALU.max, negate=True)\
                    .then_inc(S["a_s"], 1)
                v.wait_ge(S["a_e"], n + 1)
                link(V.reciprocal(attn_inv[:], attn_sum[:]))
                V.tensor_tensor(s[:, :, 0:P], s[:, :, 0:P], attn_inv[:, :, 0:1].to_broadcast([P, 4, P]), ALU.mult)
                V.tensor_tensor(s[:, :, P:3 * P], s[:, :, P:3 * P],
                                attn_inv[:, :, 1:2].to_broadcast([P, 4, 2 * P]), ALU.mult).then_inc(S["a_p"], 1)
                v.wait_ge(S["a_hi"], n + 1)
                bank = pm[:, 0:2, :].rearrange("p a b -> p (a b)")
                V.tensor_tensor(BRlo[:, branch_tiles(branch), :].rearrange("p a b -> p (a b)"), bank,
                                BRhi[:, branch_tiles(branch), :].rearrange("p a b -> p (a b)").bitcast(F32),
                                ALU.subtract).then_inc(S["a_lo"], 1)

            mS = mq[:, 0].rearrange("p t h d -> p (t h d)").rearrange("p (h s) -> p h s", h=4)
            mask = span("causal0", "causal1").unsqueeze(1).to_broadcast([P, 4, 3 * P])
            attention(0, mS, QK ** -0.5, mask, 1)

            v.wait_ge(S["f_sq"], 1)
            V.tensor_reduce(ss[:, 0:16], fsq[:].rearrange("p t (k d) -> p (t k) d", d=DH), AX_X, ALU.add)\
                .then_inc(S["f_ss"], 1)
            v.wait_ge(S["f_rn"], 1)
            V.tensor_tensor(fx[:, :, 0:D].rearrange("p t (k d) -> p t k d", d=DH),
                            fx[:, :, 0:D].rearrange("p t (k d) -> p t k d", d=DH),
                            rs[:, 0:16].rearrange("p (t k) -> p t k", t=NT).unsqueeze(3)
                            .to_broadcast([P, NT, 8, DH]), ALU.mult).then_inc(S["f_xn"], 1)
            v.wait_ge(S["f_cum"], 1)
            link(V.tensor_copy(ncs[:], pm[:, 0, 0:8].rearrange("p (t h) -> p t h", t=NT)))
            v.wait_ge(S["f_cum"], 2)
            for h in range(4):
                row = pm[:, 1 + h // 2, (h % 2) * TOK:(h % 2) * TOK + TOK]
                V.scalar_tensor_tensor(out=fD[:, h, 0:P], in0=row[:, 0:P], scalar=ncs[:, 0, h:h + 1],
                                       in1=con("causal0"), op0=ALU.subtract, op1=ALU.add)
                last = V.scalar_tensor_tensor(out=fD[:, h, P:3 * P], in0=row, scalar=ncs[:, 1, h:h + 1],
                                              in1=span("open", "causal1"), op0=ALU.subtract, op1=ALU.add)
            last.then_inc(S["f_d"], 1)
            v.wait_ge(S["f_d"], 1)
            merge(1, 0)
            merge(1, 1)
            attention(1, fS[:], DH ** -0.5, fD[:], 3)

            v.wait_ge(S["s_w"], 48)
            v.wait_ge(S["s_sq"], 1)
            V.tensor_reduce(ss[:, 0:8], sgq[:].rearrange("p t (k d) -> p (t k) d", d=P), AX_X, ALU.add)\
                .then_inc(S["s_ss"], 1)
            v.wait_ge(S["s_rn"], 1)
            v8 = sgv[:].rearrange("p t (k d) -> p (t k) d", d=P)
            link(V.tensor_tensor(v8, v8, rs[:, 0:8].unsqueeze(2).to_broadcast([P, 8, P]), ALU.mult))
            V.tensor_tensor(sgv[:], sgv[:], s_ng[:].unsqueeze(1).to_broadcast([P, NT, W]), ALU.mult)
            v.wait_ge(S["s_wt"], 1)
            V.tensor_tensor(swT[:], pm[:, 3, :].rearrange("p (g t) -> p g t", g=4),
                            con("tri").unsqueeze(1).to_broadcast([P, 4, P]), ALU.mult).then_inc(S["s_v"], 1)
            v.wait_ge(S["s_mx"], 1)
            mixed = pm[:, 0:2, :].rearrange("p a (g n t) -> p (a g) n t", g=2, n=NT)
            link(V.tensor_tensor(sm[:].rearrange("p g (n t) -> p g n t", n=NT), mixed,
                                 s_b[:].rearrange("p (g t) -> p g t", g=4).unsqueeze(2)
                                 .to_broadcast([P, 4, NT, P]), ALU.add))
            V.tensor_tensor(sm[:], sm[:], sgu[:], ALU.mult).then_inc(S["s_m"], 1)
            merge(3, 0)
            v.wait_ge(S["s_hi"], 1)
            V.tensor_tensor(BRlo[:, branch_tiles(2), :], sm[:], BRhi[:, branch_tiles(2), :].bitcast(F32),
                            ALU.subtract).then_inc(S["s_lo"], 1)
            merge(3, 1)

            merge(2, 0)
            merge(2, 1)
            V.engine_nop().then_inc(S["g_done"], 1)
            turn("merged", XThi, XTlo)
            for c in range(2):
                v.wait_ge(S["w_used"], landed(f"wo{c}"))
                x = X[:, :, c * W:(c + 1) * W]
                V.tensor_tensor(x, accT(f"wo{c}"), x, ALU.add).then_inc(evac_at(f"wo{c}")[0], 1)
            v.wait_ge(S["rstd"], 2)
            for t in range(NT):
                last = V.tensor_scalar(XN[:, t, :], X[:, t, :], rs[:, t:t + 1], None, ALU.mult)
            last.then_inc(S["xn"], 1)
            turn("x2", XThi, XTlo, lambda f: acol("norm2_g", f))

            for c in range(DFF // W):
                v.wait_ge(S["w_used"], landed(f"f1_{c}"))
                if c >= 1:
                    v.wait_ge(S["f1_hi"], c)
                V.tensor_scalar(f1r[:], accF(f"f1_{c}"), 0.0, None, ALU.max).then_inc(evac_at(f"f1_{c}")[0], 1)
                v.wait_ge(*evac_at(f"f1_{c}"))
                V.engine_nop().then_inc(S["f1_r"], 1)
                v.wait_ge(S["f1_hi"], c + 1)
                V.tensor_tensor(FFlo[:, 4 * c:4 * c + 4, :], f1s[:], FFhi[:, 4 * c:4 * c + 4, :].bitcast(F32),
                                ALU.subtract).then_inc(S["f1_lo"], 1)
            for c in range(2):
                v.wait_ge(S["w_used"], landed(f"f2_{c}"))
                x = X[:, :, c * W:(c + 1) * W]
                V.tensor_tensor(x, accT(f"f2_{c}"), x, ALU.add).then_inc(evac_at(f"f2_{c}")[0], 1)

            v.wait_ge(S["w_used"], landed("f2_1"))
            v.wait_ge(S["f1_hi"], DFF // W)
            V.memset(conv2[:, :, 0:3], 0.0).then_inc(S["c2_in"], 1)
            turn("x3", XThi, XTlo)
            turn("p0", PThi, PTlo)
            for j in range(3):
                v.wait_ge(*evac_at(f"xbc{j}"))
                for k in range(4):
                    for f in range(4 * j, 4 * j + 4):
                        w = bcol("ssd_conv_w", 12 * k + f)
                        if k == 0:
                            last = V.tensor_scalar(xbcT[:, f, :], conv2[:, f, 0:TOK], w, bcol("ssd_conv_b", f),
                                                   ALU.mult, ALU.add)
                        else:
                            last = V.scalar_tensor_tensor(out=xbcT[:, f, :], in0=conv2[:, f, k:k + TOK], scalar=w,
                                                          in1=xbcT[:, f, :], op0=ALU.mult, op1=ALU.add)
                    if k < 3:
                        link(last)
                last.then_inc(S["conv2"], 1)
            v.wait_ge(S["w_used"], landed("dt"))
            V.tensor_tensor(logit[:], accT("dt"), headv("ssd_dt_bias").unsqueeze(1).to_broadcast([P, NT, SSD_H]),
                            ALU.add).then_inc(evac_at("dt")[0], 1)
            v.wait_ge(*evac_at("dt"))
            V.scalar_tensor_tensor(out=sp_y[:], in0=logit[:], scalar=-1.0, in1=logit[:], op0=ALU.mult,
                                   op1=ALU.max).then_inc(S["dt_in"], 1)
            v.wait_ge(S["dt_e"], 1)
            softplus_tail(logit[:], sp_y[:], SSD_H)
            V.tensor_copy(dtv[:], sp[:])
            V.scalar_tensor_tensor(out=da[:], in0=sp[:], scalar=-1.0,
                                   in1=ea2[:].unsqueeze(1).to_broadcast([P, NT, SSD_H]),
                                   op0=ALU.mult, op1=ALU.mult).then_inc(S["dt_g"], 1)
            v.wait_ge(S["s_cb"], 1)
            V.tensor_tensor(cbm[:], pm[:, 0, :].rearrange("p (k s) -> p k s", s=P),
                            con("tri").unsqueeze(1).to_broadcast([P, 4, P]), ALU.mult).then_inc(S["s_xd"], 1)
            v.wait_ge(S["s_xsc"], 1)

            def per_head(col, k):
                return col.unsqueeze(col.ndim).to_broadcast(list(col.shape) + [SSD_D])

            def by_head(ap):
                return ap.rearrange("p (h d) -> p h d", d=SSD_D)
            for t in range(NT):
                V.tensor_tensor(by_head(xdt[:, t, :]), by_head(xs[:, t, :]), per_head(dtv[:, t, :], 1), ALU.mult)
                V.tensor_tensor(by_head(yd[:, t, :]), by_head(xs[:, t, :]), per_head(headv("ssd_d"), 1), ALU.mult)
            v.wait_ge(S["s_ac"], 1)
            link(V.tensor_copy(acs[:], pm[:, 1, 0:3 * SSD_H].rearrange("p (k h) -> p k h", k=3)))
            V.tensor_tensor(acs[:, 2, :], acs[:, 2, :], acs[:, 0, :], ALU.subtract).then_inc(S["s_acc"], 1)
            v.wait_ge(S["s_eac"], 1)
            V.tensor_tensor(by_head(xe[:]), by_head(xdt[:, 0, :]), per_head(eac[:, 1, :], 1), ALU.mult)\
                .then_inc(S["s_xe"], 1)
            v.wait_ge(S["conv2"], 3)
            V.memset(scp[:, :, 0:2], 0.0)
            v.wait_ge(S["s_yo"], 1)
            link(V.tensor_tensor(by_head(xe[:]), by_head(pm[:, 2:4, :].rearrange("p a b -> p (a b)")),
                                 per_head(eac[:, 0, :], 1), ALU.mult))
            V.tensor_tensor(yd[:, 1, :], yd[:, 1, :], xe[:], ALU.add).then_inc(S["s_yod"], 1)

            def short_input(c):
                v.wait_ge(S["w_used"], landed(f"sh{c}"))
                v.wait_ge(*evac_at(f"sc{c}"))
                V.tensor_tensor(scp[:, :, 2:2 + TOK], accF(f"sh{c}"), scc[:], ALU.mult)\
                    .then_inc(evac_at(f"sh{c}")[0], 1)

            def short_taps(c):
                v.wait_ge(*evac_at(f"sh{c}"))
                for k in range(3):
                    for f in range(4):
                        w = bcol("sc_conv_w", 8 * k + 4 * c + f)
                        if k == 0:
                            last = V.tensor_scalar(scv[:, f, :], scp[:, f, 0:TOK], w, None, ALU.mult)
                        else:
                            last = V.scalar_tensor_tensor(out=scv[:, f, :], in0=scp[:, f, k:k + TOK], scalar=w,
                                                          in1=scv[:, f, :], op0=ALU.mult, op1=ALU.add)
                    link(last)

            def short_output(c):
                v.wait_ge(S["w_used"], landed(f"sb{c}"))
                V.tensor_tensor(scv[:], accF(f"sb{c}"), scv[:], ALU.mult).then_inc(evac_at(f"sb{c}")[0], 1)
                v.wait_ge(*evac_at(f"sb{c}"))
                V.engine_nop().then_inc(S["c_out"], 1)

            def short_low(c):
                v.wait_ge(S["c_hi"], c + 1)
                V.tensor_tensor(BYlo[:, 8 + 4 * c:12 + 4 * c, :], scv[:],
                                BYhi[:, 8 + 4 * c:12 + 4 * c, :].bitcast(F32), ALU.subtract)\
                    .then_inc(S["c_lo"], 1)
            for b in range(4):
                c, g = b // 2, b % 2
                v.wait_ge(S["b_row"], b + 1)
                if b:
                    v.wait_ge(S["b_y"], b)
                for r in range(8):
                    last = V.scalar_tensor_tensor(out=em[:, r, :], in0=pm[:, r // 4, (r % 4) * P:(r % 4 + 1) * P],
                                                  scalar=acs[:, c, 8 * g + r:8 * g + r + 1], in1=con("strict"),
                                                  op0=ALU.subtract, op1=ALU.mult)
                last.then_inc(S["b_e0"], 1)
                v.wait_ge(S["b_e"], b + 1)
                V.scalar_tensor_tensor(out=em[:], in0=em[:], scalar=1.0,
                                       in1=cbm[:, 2 * c + g, :].unsqueeze(1).to_broadcast([P, 8, P]),
                                       op0=ALU.min, op1=ALU.mult).then_inc(S["b_m"], 1)
                v.wait_ge(S["b_y"], b + 1)
                y = yd[:, c, g * W:(g + 1) * W]
                V.tensor_tensor(y, y, pm[:, 2, :], ALU.add).then_inc(S["b_yd"], 1)
                if b == 1:
                    short_input(0)
                if b == 2:
                    short_taps(0)
            v.wait_ge(S["b_yd"], 4)
            for c in range(2):
                v.wait_ge(*evac_at(f"mz{c}"))
            V.tensor_tensor(yd[:], yd[:], zz[:], ALU.mult).then_inc(S["y_z"], 1)
            short_output(0)
            v.wait_ge(S["y_ss"], 1)
            y4 = yd[:].rearrange("p t (g d) -> p (t g) d", g=2)
            V.tensor_tensor(y4, y4, rs[:, 0:4].unsqueeze(2).to_broadcast([P, 4, W]), ALU.mult).then_inc(S["y_n"], 1)
            short_low(0)
            turn("y", BYhi[:, 0:8, :], BYlo[:, 0:8, :], lambda f: bcol("ssd_norm_w", f))
            short_input(1)
            short_taps(1)
            short_output(1)
            short_low(1)

            def residual(name, c):
                v.wait_ge(S["w_used"], landed(name))
                x = X[:, :, c * W:(c + 1) * W]
                V.scalar_tensor_tensor(out=x, in0=x, scalar=ALPHA, in1=accT(name), op0=ALU.mult, op1=ALU.add)\
                    .then_inc(evac_at(name)[0], 1)

            def layer_norm(n, at, products):
                for c, name in enumerate(products):
                    residual(name, c)
                    v.wait_ge(*evac_at(name))
                    if name[0:2] == "ao":
                        x = X[:, :, c * W:(c + 1) * W]
                        link(V.tensor_tensor(x, x, bo[:, c * W:(c + 1) * W].unsqueeze(1).to_broadcast([P, NT, W]),
                                             ALU.add))
                    for t in range(NT):
                        last = V.bn_stats(stats[:, t, c, :], X[:, t, c * W:(c + 1) * W])
                link(last)
                for t in range(NT):
                    last = V.bn_aggr(moments[:, t, :], stats[:, t].rearrange("p c s -> p (c s)"))
                last.then_inc(S["ln_sum"], 1)
                v.wait_ge(S["ln_sum"], n + 1)
                v.wait_ge(S["ln_in"], 16 * 5 * (n // 2 + 1))
                for t in range(NT):
                    last = V.scalar_tensor_tensor(out=xc[:, t, :], in0=X[:, t, :], scalar=moments[:, t, 0:1],
                                                  in1=lnr[:, at, :], op0=ALU.subtract, op1=ALU.mult)
                link(last)
                v.wait_ge(S["ln_rs"], n + 1)
                for c in range(2):
                    cols = slice(c * W, (c + 1) * W)
                    for t in range(NT):
                        last = V.scalar_tensor_tensor(out=X[:, t, cols], in0=xc[:, t, cols], scalar=rs[:, t:t + 1],
                                                      in1=lnr[:, at + 1, cols], op0=ALU.mult, op1=ALU.add)
                    last.then_inc(S["xh"], 1)

            layer_norm(0, 0, ("mo0", "mo1"))

            def feed_forward(i):
                turn(("x4", "x7")[i], XThi, XTlo)
                for c in range(-(-DFF2 // W)):
                    k = 6 * i + c
                    nf = chunks[f"fg{i}_{c}"][4] // P
                    v.wait_ge(S["w_used"], landed(f"fu{i}_{c}"))
                    v.wait_ge(*evac_at(f"fg{i}_{c}"))
                    if k:
                        v.wait_ge(S["h_lo"], k)
                    V.tensor_tensor(fh[:, 0:nf, :], accF(f"fu{i}_{c}"), sg[:, 0:nf, :], ALU.mult)\
                        .then_inc(evac_at(f"fu{i}_{c}")[0], 1)
                    v.wait_ge(*evac_at(f"fu{i}_{c}"))
                    V.engine_nop().then_inc(S["h_x"], 1)
                    v.wait_ge(S["h_hi"], k + 1)
                    V.tensor_tensor(Hlo[:, 4 * c:4 * c + nf, :], fh[:, 0:nf, :],
                                    Hhi[:, 4 * c:4 * c + nf, :].bitcast(F32), ALU.subtract).then_inc(S["h_lo"], 1)
                layer_norm(2 * i + 1, 2, (f"fd{i}_0", f"fd{i}_1"))
                turn(("x5", "x8")[i], XThi, XTlo)
                for c in range(2):
                    cols = slice(c * W, (c + 1) * W)
                    v.wait_ge(S["w_used"], landed(f"pg{i}_{c}"))
                    V.tensor_tensor(pgt[:], accT(f"pg{i}_{c}"),
                                    lnr[:, 4, cols].unsqueeze(1).to_broadcast([P, NT, W]), ALU.add)\
                        .then_inc(evac_at(f"pg{i}_{c}")[0], 1)
                    v.wait_ge(*evac_at(f"pg{i}_{c}"))
                    V.engine_nop().then_inc(S["g_x"], 1)
                    v.wait_ge(S["g_s"], 2 * i + c + 1)
                    v.wait_ge(*evac_at(f"pw{i}_{c}"))
                    link(V.tensor_tensor(pgt[:], pwt[:, c], pgt[:], ALU.mult))
                    last = V.tensor_tensor(X[:, :, cols], X[:, :, cols], pgt[:], ALU.add)
                    if c == 0:
                        link(last)
                last.then_inc(S["x_end"], 1)
            feed_forward(0)

            turn("x6", XThi, XTlo)
            V.tensor_scalar(nsink[:], headv("attn_sinks"), -1.0, None, ALU.mult)
            v.wait_ge(*evac_at("ak"))
            for kv in range(AKV):
                src = akr[64 * (kv % 2):64 * (kv % 2) + 64, kv // 2, :]
                for half in range(2):
                    last = V.tensor_copy(akd[64 * half:64 * half + 64, kv, :], src)
            v.wait_ge(S["w_used"], landed("av"))
            v.wait_ge(S["q_in"], 32)
            V.tensor_tensor(av[:], accT("av"), bv[:].unsqueeze(1).to_broadcast([P, NT, AKV * AD]), ALU.add)\
                .then_inc(evac_at("av")[0], 1)
            wmask = span("causal1", "causal2").unsqueeze(1).to_broadcast([P, 4, 3 * P])
            for pair in ((0, 1), (2, 3)):
                for kv in pair:
                    wS, neg = wS2[:, kv % 2], attn_neg2[:, kv % 2]
                    v.wait_ge(S["a_sc"], kv + 3)
                    link(V.scalar_tensor_tensor(out=wS, in0=banks(kv)[:, :, 0:3 * P], scalar=AD ** -0.5, in1=wmask,
                                                op0=ALU.mult, op1=ALU.add))
                    V.tensor_reduce(neg[:, :, 0:1], wS[:, :, 0:P], AX_X, ALU.max, negate=True)
                    link(V.tensor_reduce(neg[:, :, 1:2], wS[:, :, P:3 * P], AX_X, ALU.max, negate=True))
                    sink = nsink[:, 4 * kv:4 * kv + 4].unsqueeze(2).to_broadcast([P, 4, 2])
                    link(V.tensor_tensor(neg, neg, sink, ALU.min))
                    V.tensor_tensor(esink2[:, kv % 2], neg, sink, ALU.subtract).then_inc(S["a_s"], 1)
                for kv in pair:
                    wS, total, inv = wS2[:, kv % 2], attn_sum2[:, kv % 2], attn_inv2[:, kv % 2]
                    v.wait_ge(S["a_e"], kv + 3)
                    link(V.tensor_tensor(total, total, esink2[:, kv % 2], ALU.add))
                    link(V.reciprocal(inv, total))
                    V.tensor_tensor(wS[:, :, 0:P], wS[:, :, 0:P], inv[:, :, 0:1].to_broadcast([P, 4, P]), ALU.mult)
                    V.tensor_tensor(wS[:, :, P:3 * P], wS[:, :, P:3 * P],
                                    inv[:, :, 1:2].to_broadcast([P, 4, 2 * P]), ALU.mult).then_inc(S["a_p"], 1)
                for kv in pair:
                    v.wait_ge(S["a_hi"], kv + 3)
                    V.tensor_tensor(ATlo[:, 2 * kv:2 * kv + 2, :].rearrange("p a b -> p (a b)"), banks(kv)[:, 0, :],
                                    AThi[:, 2 * kv:2 * kv + 2, :].rearrange("p a b -> p (a b)").bitcast(F32),
                                    ALU.subtract).then_inc(S["a_lo"], 1)
            layer_norm(2, 0, ("ao0", "ao1"))
            turn("p1", PThi, PTlo)
            feed_forward(1)
            v.wait_ge(S["x_end"], 2)
            V.engine_nop().then_inc(S["fin"], 1)

        @block.tensor
        def _(pe):
            T = nc.tensor

            def turn(name, src, norm=None):
                g0, n, nf = turns[name]
                for g in range(n):
                    if norm is not None and g % 2 == 0:
                        pe.wait_ge(S["xh"], 2 * norm + g // 2 + 1)
                    if g0 + g >= 4:
                        pe.wait_ge(S["t_lo"], g0 + g - 3)
                    for f in range(min(2, nf - 2 * g)):
                        for t in range(NT):
                            k = 2 * g + f
                            last = T.transpose(pm[:, (g0 + g) % 4, f * TOK + t * P:f * TOK + (t + 1) * P],
                                               src[:, t, k * P:(k + 1) * P], ident)
                    last.then_inc(S["t_pe"], 1)

            def turned(name):
                pe.wait_ge(S["t_lo"], turns[name][0] + turns[name][1])

            def product(name, hi, lo, start=0, stop=None):
                n, first, end, kt, width, mode = chunks[name]
                if n >= 2 and start == 0:
                    pe.wait_ge(evac[n % 2], n // 2)
                k = UK * start
                for u in range(first + start, end if stop is None else first + stop):
                    pe.wait_ge(S["w_lo"], u + 1)
                    nk = units[u][2]
                    s = u % SPLIT
                    for i in range(nk):
                        wh, wl = whi[:, s, i, 0:width], wlo[:, s, i, 0:width]
                        done = k == kt - 1
                        if mode == "T":
                            for t in range(NT):
                                tok = slice(t * P, (t + 1) * P)
                                o = acc[:, n % 2, t, 0:width]
                                T.matmul(o, hi[:, k, tok], wh, start=k == 0, stop=False)
                                T.matmul(o, hi[:, k, tok], wl, start=False, stop=False)
                                last = T.matmul(o, lo[:, k, tok], wh, start=False, stop=done)
                        else:
                            for f in range(width // P):
                                o = acc[:, n % 2, f // 2, (f % 2) * TOK:(f % 2 + 1) * TOK]
                                fs = slice(f * P, (f + 1) * P)
                                T.matmul(o, wh[:, fs], hi[:, k, :], start=k == 0 and f % 2 == 0, stop=False,
                                         skip_group_check=True)
                                T.matmul(o, wh[:, fs], lo[:, k, :], start=False, stop=False, skip_group_check=True)
                                last = T.matmul(o, wl[:, fs], hi[:, k, :], start=False, stop=done,
                                                skip_group_check=True)
                        k += 1
                    last.then_inc(S["w_used"], 1)

            def mm(o, lhs, rhs, start=True, stop=True, **k):
                return T.matmul(o, lhs, rhs, start=start, stop=stop, **k)

            def flat(i, n=P):
                return pm[:, i // BANK, i % BANK:i % BANK + n]

            pe.wait_ge(S["x_in"], 32)
            pe.wait_ge(S["c_in"], 64)
            T.transpose(pm[:, 0, 0:n_a], rowsA[0:n_a, :], ident[0:n_a, 0:n_a])
            T.transpose(pm[:, 0, P:P + n_b], rowsB[0:n_b, :], ident[0:n_b, 0:n_b]).then_inc(S["cols"], 1)
            pe.wait_ge(S["cols"], 2)
            pe.wait_ge(S["xn"], 1)
            turn("x1", XN1)
            turned("x1")
            pe.wait_ge(S["k_in"], 16)
            for name in ("dq", "dk", "dv", "abc", "ff"):
                product(name, XThi, XTlo)

            def from_x(name, start=0, stop=None):
                product(name, XThi, XTlo, start, stop)

            pe.wait_ge(S["dn_sq"], 1)
            for i in range(4):
                last = mm(pm[:, i, :], ones, d_sq[:, i * BANK:(i + 1) * BANK])
            last.then_inc(S["dn_l2"], 1)
            from_x("z")
            pe.wait_ge(S["dn_rn"], 1)
            pe.wait_ge(S["dn_g"], 1)
            for t in range(NT):
                mm(pm[:, 0, 4 * t:4 * t + 4], con("tri64"), dng[:, t, :])
                last = mm(pm[:, 0, 8 + 4 * t:12 + 4 * t], con("blk64"), dng[:, t, :])
            last.then_inc(S["dn_gc"], 1)
            from_x("fq", 0, 2)
            pe.wait_ge(S["dn_gcs"], 1)
            for h in range(4):
                for t in range(NT):
                    i = (h * NT + t) * P
                    mm(flat(i), dng[:, t, h:h + 1].to_broadcast([P, P]), con("tri64"))
                    last = mm(flat(2 * BANK + i), beta[:, t, h:h + 1].to_broadcast([P, P]), ident)
            last.then_inc(S["dn_rows"], 1)
            from_x("fq", 2, 4)
            from_x("fk", 0, 1)
            pe.wait_ge(S["dn_qkn"], 1)
            pe.wait_ge(S["dn_e0"], 1)
            pe.wait_ge(S["dn_egr"], 1)
            for h in range(4):
                for t in range(NT):
                    i = (h * NT + t) * P
                    mm(flat(i), kT[:, i:i + P], kT[:, i:i + P])
                    last = mm(flat(2 * BANK + i), kT[:, i:i + P], qT[:, i:i + P])
            last.then_inc(S["dn_kk"], 1)
            from_x("fk", 1, 3)
            pe.wait_ge(S["dn_lt"], 1)
            for i in range(0, 1024, P):
                T.transpose(flat(i), kT[:, i:i + P], ident)
                last = T.transpose(flat(2 * BANK + i), d_v[:, i:i + P], ident)
            last.then_inc(S["dn_kv"], 1)
            from_x("fk", 3, 4)
            from_x("fv", 0, 1)
            pe.wait_ge(S["dn_vb"], 1)
            for s in range(6):
                for hf in range(2):
                    pe.wait_ge(S["dn_ml"], 2 * s + hf + 1)
                    for j in range(4):
                        i = hf * W + j * P
                        last = mm(pm[:, 2 * hf, j * P:(j + 1) * P], d_ml[:, i:i + P], d_x[:, i:i + P])
                    last.then_inc(S["dn_t1"], 1)
                for hf in range(2):
                    pe.wait_ge(S["dn_t1c"], 2 * s + hf + 1)
                    for j in range(4):
                        i = hf * W + j * P
                        if s < 5:
                            mm(pm[:, 2 * hf + 1, j * P:(j + 1) * P], d_y[:, i:i + P], d_t1[:, i:i + P])
                        last = mm(pm[:, 2 * hf, j * P:(j + 1) * P], d_t1[:, i:i + P], d_y[:, i:i + P])
                    last.then_inc(S["dn_pq"], 1)
                from_x(*(("fv", s + 1, s + 2) if s < 3 else ("sv", s - 3, s - 2)))
            pe.wait_ge(S["dn_y"], 3)
            for i in range(0, 1024, P):
                mm(flat(i), d_y[:, i:i + P], d_vb[:, i:i + P])
                last = mm(flat(2 * BANK + i), d_kbe[:, i:i + P], d_y[:, i:i + P])
            last.then_inc(S["dn_uw"], 1)
            from_x("sv", 3, 4)
            from_x("su", 0, 1)
            for n in range(4):
                t, r = n // 2, 64 * (n % 2)
                rows = slice(r, r + 64)

                def tile(h):
                    return (h * NT + t) * P
                o_bank = pm[rows, 1 + t, :]
                if n:
                    pe.wait_ge(S["sc_s"], n)
                    for h in range(4):
                        last = mm(pm[rows, 0, h * P:(h + 1) * P], d_w[:, tile(h) + r:tile(h) + r + 64],
                                  d_s[:, h * P:(h + 1) * P])
                    last.then_inc(S["sc_ws"], 1)
                    from_x(*(("su", 2, 3), ("gate0_0", 0, 1), ("gate0_0", 2, 3))[n - 1])
                    for h in range(4):
                        mm(o_bank[:, h * P:(h + 1) * P], qT[:, tile(h) + r:tile(h) + r + 64],
                           d_s[:, h * P:(h + 1) * P], start=h == 0, stop=False, skip_group_check=True)
                pe.wait_ge(S["sc_vn"], n + 1)
                for h in range(4):
                    i = tile(h)
                    last = mm(o_bank[:, h * P:(h + 1) * P], d_at[rows, i + r:i + r + 64], d_vn[rows, i:i + P],
                              start=n == 0 and h == 0, stop=True, skip_group_check=True)
                    if n < 3:
                        last = mm(pm[:, 3, h * P:(h + 1) * P], d_kdec[rows, i:i + P], d_vn[rows, i:i + P])
                last.then_inc(S["sc_su"], 1)
                from_x(*(("su", 1, 2), ("su", 3, 4), ("gate0_0", 1, 2), ("gate0_0", 3, 4))[n])
            from_x("gate0_1", 0, 3)
            pe.wait_ge(S["dn_o"], 1)
            turn("oa", d_o.rearrange("p (t d) -> p t d", t=NT))
            from_x("gate0_1", 3, 4)
            turned("oa")

            def branch(i):
                for c in range(2):
                    product(f"br{i}_{c}", BRhi[:, branch_tiles(i)], BRlo[:, branch_tiles(i)])
            branch(0)

            pe.wait_ge(S["m_cn2"], 1)
            turn("cqkv", cn)
            turned("cqkv")
            for j in range(2):
                product(f"uq{j}", MQhi[:, 0:2], MQlo[:, 0:2])
            for j in range(2):
                product(f"ukv{j}", MQhi[:, 2:3], MQlo[:, 2:3])
            from_x("gate1_0")
            from_x("gate1_1", 0, 2)
            pe.wait_ge(S["m_rope"], 2)
            for i in range(2):
                for h in range(4):
                    for t in range(NT):
                        last = T.transpose(flat((i * 4 + h) * TOK + t * P), mq[:, i, t, h, 0:NOPE], ident)
            last.then_inc(S["m_tn"], 1)
            from_x("gate1_1", 2, 3)
            pe.wait_ge(S["m_tnc"], 1)
            for i in range(2):
                for h in range(4):
                    for t in range(NT):
                        last = T.transpose(flat((i * 4 + h) * TOK + t * P)[0:ROPE], mq[:, i, t, h, NOPE:QK], ident)
            last.then_inc(S["m_tr"], 1)
            from_x("gate1_1", 3, 4)
            pe.wait_ge(S["m_trc"], 1)
            for h in range(4):
                for t in range(NT):
                    o = pm[:, h, P * t:P * t + P * (t + 1)]
                    n = P * (t + 1)
                    mm(o, mT[:, h, t * P:(t + 1) * P], mT[:, 4 + h, 0:n], stop=False)
                    last = mm(o, mR[:, h, t * P:(t + 1) * P], mR[:, 4 + h, 0:n], start=False)
            last.then_inc(S["a_sc"], 1)

            def attention(n, s, pt, vals):
                pe.wait_ge(S["a_p"], n + 1)
                for h in range(4):
                    for j in range(3):
                        last = T.transpose(pm[:, h, j * P:(j + 1) * P], s[:, h, j * P:(j + 1) * P], ident)
                last.then_inc(S["a_pt"], 1)
                pe.wait_ge(S["a_ptc"], n + 1)
                for h in range(4):
                    o = pm[:, h // 2, (h % 2) * TOK:(h % 2 + 1) * TOK]
                    mm(o, vals(0, h), pt[:, h, 0:2 * P], stop=False)
                    last = mm(o[:, P:TOK], vals(1, h), pt[:, h, 2 * P:3 * P], start=False)
                last.then_inc(S["a_o"], 1)

            mS = mq[:, 0].rearrange("p t h d -> p (t h d)").rearrange("p (h s) -> p h s", h=4)
            mP = mq[:, 1].rearrange("p t h d -> p (t h d)").rearrange("p (h s) -> p h s", h=4)
            attention(0, mS, mP, lambda t, h: mv[:, t, h * P:(h + 1) * P])

            pe.wait_ge(S["a_lo"], 1)
            mm(pm[:, 0, 0:4], con("tri"), nlf[:, 0, :])
            mm(pm[:, 0, 4:8], ones, nlf[:, 0, :], stop=False)
            mm(pm[:, 0, 4:8], con("tri"), nlf[:, 1, :], start=False).then_inc(S["f_cum"], 1)
            for h in range(4):
                row = pm[:, 1 + h // 2, (h % 2) * TOK:(h % 2 + 1) * TOK]
                mm(row, nlf[:, 0, h:h + 1].to_broadcast([P, P]), span("tri", "ones"), stop=False)
                last = mm(row[:, P:TOK], nlf[:, 1, h:h + 1].to_broadcast([P, P]), con("tri"), start=False)
            last.then_inc(S["f_cum"], 1)
            branch(1)
            pe.wait_ge(S["f_xn"], 1)
            pe.wait_ge(S["f_d"], 1)
            for k in range(8):
                for t in range(NT):
                    last = T.transpose(flat(k * TOK + t * P), fx[:, t, k * P:(k + 1) * P], ident)
            last.then_inc(S["f_t"], 1)
            from_x("gate3_0", 0, 1)
            pe.wait_ge(S["f_tc"], 1)
            for h in range(4):
                for t in range(NT):
                    n = P * (t + 1)
                    last = mm(pm[:, h, P * t:P * t + n], fT[:, h, t * P:(t + 1) * P], fT[:, 4 + h, 0:n])
            last.then_inc(S["a_sc"], 1)
            from_x("gate3_0", 1, 4)
            attention(1, fS, fPT, lambda t, h: fx[:, t, 2 * W + h * P:2 * W + (h + 1) * P])

            from_x("gate3_1")
            pe.wait_ge(S["s_w"], 48)
            for g in range(4):
                last = T.transpose(pm[:, 3, g * P:(g + 1) * P], sw[:, g, :], ident)
            last.then_inc(S["s_wt"], 1)
            pe.wait_ge(S["s_v"], 1)
            for g in range(4):
                for n in range(NT):
                    last = mm(pm[:, g // 2, (g % 2) * TOK + n * P:(g % 2) * TOK + (n + 1) * P],
                              sgv[:, n, g * P:(g + 1) * P], swT[:, g, :])
            last.then_inc(S["s_mx"], 1)
            branch(3)
            from_x("gate2_0")
            from_x("gate2_1")
            pe.wait_ge(S["s_lo"], 1)
            branch(2)
            pe.wait_ge(S["g_done"], 1)
            turn("merged", merged)
            turned("merged")
            for c in range(2):
                product(f"wo{c}", XThi, XTlo)
            pe.wait_ge(S["xn"], 2)
            turn("x2", XN)
            turned("x2")
            for c in range(DFF // W):
                product(f"f1_{c}", XThi, XTlo)
            pe.wait_ge(S["f1_lo"], DFF // W)
            for c in range(2):
                product(f"f2_{c}", FFhi, FFlo)

            for c in range(2):
                pe.wait_ge(*evac_at(f"f2_{c}"))
            turn("x3", X)
            pe.wait_ge(S["p_in"], 16)
            turn("p0", pin)
            turned("p0")
            for name in ("xbc0", "xbc1", "xbc2", "dt", "mz0", "mz1"):
                product(name, XThi, XTlo)
            pe.wait_ge(S["silu2"], 3)
            for c in range(2):
                for g in range(2):
                    k = 2 * c + g
                    last = mm(pm[:, 0, k * P:(k + 1) * P], xbcT[:, 8 + g, c * P:(c + 1) * P],
                              xbcT[:, 10 + g, c * P:(c + 1) * P])
            last.then_inc(S["s_cb"], 1)
            from_x("sc0", 0, 1)
            pe.wait_ge(S["s_xd"], 1)
            for t in range(NT):
                for f in range(8):
                    last = T.transpose(flat(t * D + f * P), xbcT[:, f, t * P:(t + 1) * P], ident)
            last.then_inc(S["s_xs"], 1)
            from_x("sc0", 1, 2)
            pe.wait_ge(S["s_xsc"], 1)
            for g in range(2):
                last = T.transpose(pm[:, 0, g * P:(g + 1) * P], xbcT[:, 8 + g, 0:P], ident)
            last.then_inc(S["s_bt"], 1)
            from_x("sc0", 2, 3)
            pe.wait_ge(S["dt_g"], 1)
            for c in range(2):
                mm(pm[:, 1, c * SSD_H:(c + 1) * SSD_H], con("tri"), da[:, c, :])
            mm(pm[:, 1, 2 * SSD_H:3 * SSD_H], ones, da[:, 0, :]).then_inc(S["s_ac"], 1)
            from_x("sc0", 3, 4)
            from_x("sh0", 0, 1)
            pe.wait_ge(S["s_btc"], 1)
            pe.wait_ge(S["s_xe"], 1)
            for g in range(2):
                last = mm(pm[:, 2 + g, :], bmt[:, g * P:(g + 1) * P], xe[:, g * W:(g + 1) * W])
            last.then_inc(S["s_st"], 1)
            from_x("sh0", 1, 2)
            pe.wait_ge(S["s_stc"], 1)
            for g in range(2):
                last = mm(pm[:, 2 + g, :], xbcT[:, 10 + g, P:2 * P], hst[:, g * W:(g + 1) * W])
            last.then_inc(S["s_yo"], 1)
            from_x("sh0", 2, 3)
            pe.wait_ge(S["s_yod"], 1)

            def rows(b):
                c, g = b // 2, b % 2
                if b:
                    pe.wait_ge(S["b_e0"], b)
                for r in range(8):
                    h = 8 * g + r
                    last = mm(flat(r * P), da[:, c, h:h + 1].to_broadcast([P, P]), con("tri"))
                last.then_inc(S["b_row"], 1)
            rows(0)
            for b in range(4):
                c, g = b // 2, b % 2
                if b < 3:
                    rows(b + 1)
                from_x(*(("sh0", 3, 4), ("sb0", 0, 1), ("sb0", 1, 2), ("sb0", 2, 3))[b])
                pe.wait_ge(S["b_m"], b + 1)
                if b:
                    pe.wait_ge(S["b_yd"], b)
                for r in range(8):
                    at = (8 * g + r) * SSD_D
                    last = mm(pm[:, 2, r * SSD_D:(r + 1) * SSD_D], em[:, r, :], xdt[:, c, at:at + SSD_D])
                last.then_inc(S["b_y"], 1)
            from_x("sb0", 3, 4)
            from_x("sc1")
            from_x("sh1")
            pe.wait_ge(S["y_n"], 1)
            turn("y", yd)
            from_x("sb1")
            turned("y")
            pe.wait_ge(S["c_lo"], 2)
            for c in range(2):
                product(f"mo{c}", BYhi, BYlo)

            def feed_forward(i):
                turn(("x4", "x7")[i], X, norm=2 * i)
                turned(("x4", "x7")[i])
                n = -(-DFF2 // W)
                for c in range(n):
                    product(f"fg{i}_{c}", XThi, XTlo)
                    product(f"fu{i}_{c}", XThi, XTlo)
                pe.wait_ge(S["h_lo"], n * (i + 1))
                for c in range(2):
                    product(f"fd{i}_{c}", Hhi, Hlo)
                for c in range(2):
                    product(f"pw{i}_{c}", PThi, PTlo)
                turn(("x5", "x8")[i], X, norm=2 * i + 1)
                turned(("x5", "x8")[i])
                for c in range(2):
                    product(f"pg{i}_{c}", XThi, XTlo)
            feed_forward(0)

            pe.wait_ge(S["x_end"], 1)
            turn("x6", X)
            turned("x6")
            for name in ("aq0", "aq1", "ak", "av"):
                product(name, XThi, XTlo)
            pe.wait_ge(*evac_at("aq1"))
            pe.wait_ge(*evac_at("ak"))
            pe.wait_ge(*evac_at("av"))
            for pair in ((0, 1), (2, 3)):
                for kv in pair:
                    if kv >= 2:
                        pe.wait_ge(S["a_lo"], kv + 1)
                    for j in range(4):
                        h = 4 * kv + j
                        r = slice(64 * (h % 2), 64 * (h % 2) + 64)
                        mm(banks(kv)[:, j, 0:P], aqT[r, h // 2, 0:P], akd[r, kv, 0:P])
                        last = mm(banks(kv)[:, j, P:3 * P], aqT[r, h // 2, P:TOK], akd[r, kv, :])
                    last.then_inc(S["a_sc"], 1)
                for kv in pair:
                    pe.wait_ge(S["a_p"], kv + 3)
                    for h in range(4):
                        for j in range(3):
                            last = T.transpose(banks(kv)[:, h, j * P:(j + 1) * P],
                                               wS2[:, kv % 2, h, j * P:(j + 1) * P], ident)
                    last.then_inc(S["a_pt"], 1)
                for kv in pair:
                    pe.wait_ge(S["a_ptc"], kv + 3)
                    for j in range(4):
                        r = slice(64 * (j % 2), 64 * (j % 2) + 64)
                        o = banks(kv)[r, 0, (j // 2) * TOK:(j // 2 + 1) * TOK]
                        pt = wPT2[:, kv % 2, j]
                        mm(o, av[:, 0, kv * AD:(kv + 1) * AD], pt[:, 0:2 * P], stop=False)
                        last = mm(o[:, P:TOK], av[:, 1, kv * AD:(kv + 1) * AD], pt[:, 2 * P:3 * P], start=False)
                    last.then_inc(S["a_o"], 1)
            pe.wait_ge(S["a_lo"], 6)
            for c in range(2):
                product(f"ao{c}", AThi, ATlo)
            pe.wait_ge(S["p_in"], 32)
            turn("p1", pin1)
            feed_forward(1)


def kernel(**inputs):
    import concourse.bacc as bacc
    from concourse.bass_utils import run_bass_kernel_spmd

    def flat(name, *shape):
        return np.ascontiguousarray(inputs[name]).reshape(shape)

    arrays = {"x": flat("x", TOK, D), "consts": CONST_ARRAY, "w_in": flat("w_in", D, -1)}
    arrays["positions"] = np.ascontiguousarray(flat("positions", NT, P).T)
    for name in ("mla_w_uq", "mla_w_ukv", "w_out", "w_ff1", "w_ff2"):
        arrays[name] = np.ascontiguousarray(inputs[name])[0]
    for i in range(4):
        arrays[f"w_branch{i}"] = np.ascontiguousarray(inputs["w_branch"])[0, i]
    for i in range(2):
        for name, old in (("w_gate", "w_ffn_gate_2"), ("w_up", "w_ffn_up_2"), ("w_down", "w_ffn_down_2"),
                          ("w_ple", "w_ple_2"), ("w_pgate", "w_ple_gate_2")):
            arrays[f"{name}{i}"] = np.ascontiguousarray(inputs[old])[i]
        arrays[f"p{i}"] = np.ascontiguousarray(inputs["p_2"])[i, 0]
    for name, old in (("w_in_mix", "w_in_mix_2"), ("w_out_mix", "w_out_mix_2"), ("w_qkv", "w_qkv_2"),
                      ("w_o", "w_o_2")):
        arrays[name] = np.ascontiguousarray(inputs[old])[0]
    qk_bias = np.ascontiguousarray(flat("b_qkv_2", -1)[0:10 * P]).reshape(10, P)
    arrays["rows_a"] = np.concatenate([flat(name, -1, P) for name, _ in ROWS_A])
    arrays["rows_b"] = np.concatenate([qk_bias if name == "b_qk" else flat(name + "_2", -1, P)
                                       for name, _ in ROWS_B])
    arrays["heads"] = np.concatenate([flat(name if name[0] in "df" else name + "_2", -1) for name, _ in HEADS])
    arrays["b_v"] = np.ascontiguousarray(flat("b_qkv_2", -1)[10 * P:])
    for name in ("dn_out_norm_g", "mla_qk_q_g", "mla_qk_k_g", "sg_v_norm_g", "sg_b_s"):
        arrays[name] = flat(name, -1)
    arrays["sg_w_s"] = np.ascontiguousarray(inputs["sg_w_s"])[0]
    arrays["b_o"] = flat("b_o_2", -1)
    for i in range(2):
        for name in ("ln_mix_g", "ln_mix_b", "ln_ffn_g", "ln_ffn_b", "b_ple_gate"):
            arrays[f"{name}{i}"] = np.ascontiguousarray(inputs[name + "_2"])[i]

    nc = bacc.Bacc("TRN2", target_bir_lowering=False, num_devices=1)
    a = {n: nc.dram_tensor(f"in_{n}", v.shape, mybir.dt.from_np(v.dtype), kind="ExternalInput").ap()
         for n, v in arrays.items()}
    out = nc.dram_tensor("out_x", (TOK, D), F32, kind="ExternalOutput").ap()
    build(nc, a, out)
    r = run_bass_kernel_spmd(nc, [{f"in_{n}": v for n, v in arrays.items()}], core_ids=[0])
    return r.results[0]["out_x"].reshape(1, TOK, D)
```
